# Optimizing a Trainium2 kernel written in Bass

```python
import jax, jax.numpy as jnp
from jax import lax
import numpy as np

D_MODEL = 1024
BATCH = 1
SEQ = 1024
DEPTH = 1
DEC_BATCH = 8
DEC_SEQ = 1
PAST_LEN = 8192
PAGE_SIZE = 128

D_MIX = D_MODEL
C_A = D_MIX // 2
C_B = D_MIX - C_A
HEAD_A = 64
H_A = C_A // HEAD_A
LORA_DECAY = 32
LORA_AAA = 32
LORA_GATE = 96
N_SHIFT = 3 * C_A + LORA_DECAY + LORA_AAA + LORA_GATE
N_IN = N_SHIFT + 2 * C_B
SPLIT_A = (C_A, 2 * C_A, 3 * C_A, 3 * C_A + LORA_DECAY, 3 * C_A + LORA_DECAY + LORA_AAA)
CONV_W = 4
LRU_BLOCKS = 8
LRU_BW = C_B // LRU_BLOCKS
LRU_C = 8.0
N_GROUPS = 4
EXP_PER_GROUP = 4
N_EXPERTS = N_GROUPS * EXP_PER_GROUP
TOP_K = 2
D_EXPERT = 256
ALPHA = (2 * DEPTH) ** 0.25
BETA = (8 * DEPTH) ** -0.25
LN_EPS = 1e-5
GN_EPS = 64e-5

kernel_name = "hymba_rwkv7_rglru_hmoe_deepnorm_step"

def _layer_norm(x, eps=LN_EPS):
    xf = x.astype(jnp.float32)
    mu = jnp.mean(xf, -1, keepdims=True)
    var = jnp.mean(jnp.square(xf - mu), -1, keepdims=True)
    return (xf - mu) * lax.rsqrt(var + eps)

def _token_shift(p, p_prev, mu):
    prev = jnp.concatenate([p_prev[:, None, :], p[:, :-1]], axis=1)
    return p + (prev - p) * mu

def _wkv7_scan(r, decay, k, v, a_vec, b_vec, s0):
    def step(s, inp):
        r_t, w_t, k_t, v_t, a_t, b_t = inp
        sa = jnp.einsum('bhij,bhj->bhi', s, a_t)
        s = s * w_t[:, :, None, :] + sa[..., None] * b_t[:, :, None, :] + v_t[..., None] * k_t[:, :, None, :]
        return s, jnp.einsum('bhij,bhj->bhi', s, r_t)
    xs = tuple(jnp.moveaxis(t, 1, 0) for t in (r, decay, k, v, a_vec, b_vec))
    s_T, ys = lax.scan(step, s0, xs)
    return jnp.moveaxis(ys, 0, 1), s_T

def _rglru_scan(a, u, h0):
    def step(h, inp):
        a_t, u_t = inp
        h = a_t * h + u_t
        return h, h
    h_T, hs = lax.scan(step, h0, (jnp.moveaxis(a, 1, 0), jnp.moveaxis(u, 1, 0)))
    return jnp.moveaxis(hs, 0, 1), h_T

def _causal_conv(x, buf, w, b):
    T = x.shape[1]
    xp = jnp.concatenate([buf.astype(x.dtype), x], axis=1)
    y = b + xp[:, 0:T] * w[0]
    for j in range(1, CONV_W):
        y = y + xp[:, j:j + T] * w[j]
    return y, xp[:, T:]

def _time_mix(h, h_prev, s_wkv, conv_buf, lru_h, p):
    B, T, _ = h.shape
    f32 = jnp.float32
    P = h @ p['w_in']
    p_prev = h_prev.astype(h.dtype) @ p['w_in'][:, :N_SHIFT]
    xs = _token_shift(P[..., :N_SHIFT], p_prev, p['mu_shift'])
    r, k, v, wd, ad, gd = jnp.split(xs, SPLIT_A, axis=-1)
    w_log = -jax.nn.softplus(-(p['w0'] + jnp.tanh(wd) @ p['w_decay_up'])) - 0.5
    decay = jnp.exp(-jnp.exp(w_log.astype(f32)))
    a = jax.nn.sigmoid(p['a0'] + ad @ p['w_a_up'])
    g = jax.nn.sigmoid(gd) @ p['w_g_up']

    def heads(t):
        return t.reshape(B, T, H_A, HEAD_A).astype(f32)
    kk = heads(k * p['k_k'])
    kk = kk / jnp.maximum(jnp.sqrt(jnp.sum(kk * kk, -1, keepdims=True)), 1e-12)
    k = k * (1 + (a - 1) * p['k_a'])
    r_h, k_h, v_h, a_h = heads(r), heads(k), heads(v), heads(a)
    y_a, s_new = _wkv7_scan(r_h, heads(decay), k_h, v_h, -kk, kk * a_h, s_wkv.astype(f32))
    mu = jnp.mean(y_a, -1, keepdims=True)
    var = jnp.mean(jnp.square(y_a - mu), -1, keepdims=True)
    y_a = ((y_a - mu) * lax.rsqrt(var + GN_EPS)).reshape(B, T, C_A) * p['lnx_gain'] + p['lnx_bias']
    bonus = jnp.sum(r_h * k_h * p['r_k'], -1, keepdims=True) * v_h
    y_a = (y_a + bonus.reshape(B, T, C_A)) * g
    gate_b = P[..., N_SHIFT:N_SHIFT + C_B]
    rec_b = P[..., N_SHIFT + C_B:]
    xc, conv_new = _causal_conv(rec_b, conv_buf, p['conv_w'], p['conv_b'])
    xcb = xc.reshape(B, T, LRU_BLOCKS, LRU_BW)
    r_t = jax.nn.sigmoid(jnp.einsum('btnc,ncd->btnd', xcb, p['w_rgate']).reshape(B, T, C_B) + p['b_rgate'])
    i_t = jax.nn.sigmoid(jnp.einsum('btnc,ncd->btnd', xcb, p['w_igate']).reshape(B, T, C_B) + p['b_igate'])
    log_a = -LRU_C * r_t.astype(f32) * jax.nn.softplus(-p['lru_lambda'].astype(f32))
    mult = jnp.sqrt(-jnp.expm1(2.0 * log_a))
    u = mult * (i_t * xc).astype(f32)
    hs, lru_new = _rglru_scan(jnp.exp(log_a), u, lru_h.astype(f32))
    y_b = hs * jax.nn.gelu(gate_b.astype(f32))
    y = jnp.concatenate([y_a, y_b], axis=-1).astype(h.dtype) @ p['w_out']
    return y, s_new, h[:, -1], conv_new, lru_new

def _hier_moe(h, p):
    B, T, D = h.shape
    f32 = jnp.float32
    t = h.reshape(B * T, D)
    gl = (t @ p['w_router_group'] + p['b_router_group']).astype(f32)
    gp = jax.nn.softmax(gl, -1)
    gi = jnp.argmax(gl, -1)
    p_grp = jnp.take_along_axis(gp, gi[:, None], -1)
    el = (t @ p['w_router_expert'] + p['b_router_expert']).astype(f32).reshape(-1, N_GROUPS, EXP_PER_GROUP)
    el = jnp.take_along_axis(el, gi[:, None, None], 1)[:, 0]
    top_v, top_i = lax.top_k(jax.nn.softmax(el, -1), TOP_K)
    top_v = top_v / jnp.sum(top_v, -1, keepdims=True) * p_grp
    eid = gi[:, None] * EXP_PER_GROUP + top_i
    comb = jnp.sum(jax.nn.one_hot(eid, N_EXPERTS, dtype=f32) * top_v[..., None], 1)
    hid = jax.nn.silu(jnp.einsum('nd,edf->nef', t, p['w_exp_gate'])) * jnp.einsum('nd,edf->nef', t, p['w_exp_up'])
    y = jnp.einsum('nef,efd->nd', hid * comb[..., None].astype(hid.dtype), p['w_exp_down'])
    return y.reshape(B, T, D)

def _post_norm(z, gain, bias, dtype):
    return (_layer_norm(z) * gain + bias).astype(dtype)

def _layer(x, c, s_wkv, s_shift, s_conv, s_lru, p):
    mod = jax.nn.silu(c) @ p['w_ada'] + p['b_ada']
    sh1, sc1, g1, sh2, sc2, g2 = jnp.split(mod[:, None, :], 6, axis=-1)
    h = (_layer_norm(x) * (1 + sc1) + sh1).astype(x.dtype)
    y, s_wkv, s_shift, s_conv, s_lru = _time_mix(h, s_shift, s_wkv, s_conv, s_lru, p)
    x = _post_norm(ALPHA * x + (1 + g1) * y, p['ln1_gain'], p['ln1_bias'], x.dtype)
    h = (_layer_norm(x) * (1 + sc2) + sh2).astype(x.dtype)
    x = _post_norm(ALPHA * x + (1 + g2) * _hier_moe(h, p), p['ln2_gain'], p['ln2_bias'], x.dtype)
    return x, s_wkv, s_shift, s_conv, s_lru

def _trunk(x, c, st_wkv, st_shift, st_conv, st_lru, layers):
    wkv, shf, cnv, lru = [], [], [], []
    for l in range(DEPTH):
        x, a, b, d, e = _layer(x, c, st_wkv[l], st_shift[l], st_conv[l], st_lru[l], layers[l])
        wkv.append(a); shf.append(b); cnv.append(d); lru.append(e)
    return x, jnp.stack(wkv), jnp.stack(shf), jnp.stack(cnv), jnp.stack(lru)

def setup_inputs(seed: int = 0) -> dict:
    key = jax.random.key(seed)
    ks = iter(jax.random.split(key, 48))
    f32 = jnp.float32

    def nrm(shape, s):
        return jax.random.normal(next(ks), shape, f32) * s

    Dm = D_MODEL
    u = jax.random.uniform(next(ks), (DEPTH, C_B), f32, 0.9, 0.999)
    base = u ** (1.0 / LRU_C)
    lam = jnp.log(base) - jnp.log1p(-base)
    return {
        'x_prompt': nrm((BATCH, SEQ, Dm), 1.0),
        'x_sample': nrm((DEC_BATCH, DEC_SEQ, Dm), 1.0),
        'c_prompt': nrm((BATCH, Dm), 1.0),
        'c_sample': nrm((DEC_BATCH, Dm), 1.0),
        'state_wkv': nrm((DEPTH, DEC_BATCH, H_A, HEAD_A, HEAD_A), 0.5),
        'state_shift': nrm((DEPTH, DEC_BATCH, Dm), 1.0),
        'state_conv': nrm((DEPTH, DEC_BATCH, CONV_W - 1, C_B), 1.0),
        'state_lru': nrm((DEPTH, DEC_BATCH, C_B), 1.0),
        'w_ada': nrm((DEPTH, Dm, 6 * Dm), 0.1 * Dm ** -0.5),
        'b_ada': nrm((DEPTH, 6 * Dm), 0.01),
        'w_in': nrm((DEPTH, Dm, N_IN), Dm ** -0.5),
        'mu_shift': jax.random.uniform(next(ks), (DEPTH, N_SHIFT), f32),
        'w0': jax.random.uniform(next(ks), (DEPTH, C_A), f32, -5.0, 0.0),
        'w_decay_up': nrm((DEPTH, LORA_DECAY, C_A), 0.1),
        'a0': nrm((DEPTH, C_A), 0.1),
        'w_a_up': nrm((DEPTH, LORA_AAA, C_A), 0.5 * LORA_AAA ** -0.5),
        'w_g_up': nrm((DEPTH, LORA_GATE, C_A), LORA_GATE ** -0.5),
        'k_k': 1.0 + nrm((DEPTH, C_A), 0.1),
        'k_a': 1.0 + nrm((DEPTH, C_A), 0.1),
        'r_k': nrm((DEPTH, H_A, HEAD_A), 0.1),
        'lnx_gain': 1.0 + nrm((DEPTH, C_A), 0.05),
        'lnx_bias': nrm((DEPTH, C_A), 0.01),
        'conv_w': nrm((DEPTH, CONV_W, C_B), CONV_W ** -0.5),
        'conv_b': nrm((DEPTH, C_B), 0.01),
        'w_rgate': nrm((DEPTH, LRU_BLOCKS, LRU_BW, LRU_BW), LRU_BW ** -0.5),
        'b_rgate': nrm((DEPTH, C_B), 0.01),
        'w_igate': nrm((DEPTH, LRU_BLOCKS, LRU_BW, LRU_BW), LRU_BW ** -0.5),
        'b_igate': nrm((DEPTH, C_B), 0.01),
        'lru_lambda': lam,
        'w_out': nrm((DEPTH, D_MIX, Dm), BETA * D_MIX ** -0.5),
        'ln1_gain': 1.0 + nrm((DEPTH, Dm), 0.05),
        'ln1_bias': nrm((DEPTH, Dm), 0.01),
        'w_router_group': nrm((DEPTH, Dm, N_GROUPS), Dm ** -0.5),
        'b_router_group': nrm((DEPTH, N_GROUPS), 0.01),
        'w_router_expert': nrm((DEPTH, Dm, N_EXPERTS), Dm ** -0.5),
        'b_router_expert': nrm((DEPTH, N_EXPERTS), 0.01),
        'w_exp_gate': nrm((DEPTH, N_EXPERTS, Dm, D_EXPERT), Dm ** -0.5),
        'w_exp_up': nrm((DEPTH, N_EXPERTS, Dm, D_EXPERT), Dm ** -0.5),
        'w_exp_down': nrm((DEPTH, N_EXPERTS, D_EXPERT, Dm), BETA * D_EXPERT ** -0.5),
        'ln2_gain': 1.0 + nrm((DEPTH, Dm), 0.05),
        'ln2_bias': nrm((DEPTH, Dm), 0.01),
    }

def reference(x_prompt, x_sample, c_prompt, c_sample, state_wkv, state_shift, state_conv, state_lru,
              w_ada, b_ada, w_in, mu_shift, w0, w_decay_up, a0, w_a_up, w_g_up, k_k, k_a, r_k,
              lnx_gain, lnx_bias, conv_w, conv_b, w_rgate, b_rgate, w_igate, b_igate, lru_lambda,
              w_out, ln1_gain, ln1_bias, w_router_group, b_router_group, w_router_expert,
              b_router_expert, w_exp_gate, w_exp_up, w_exp_down, ln2_gain, ln2_bias):
    layers = [dict(w_ada=w_ada[l], b_ada=b_ada[l], w_in=w_in[l], mu_shift=mu_shift[l], w0=w0[l],
                   w_decay_up=w_decay_up[l], a0=a0[l], w_a_up=w_a_up[l], w_g_up=w_g_up[l],
                   k_k=k_k[l], k_a=k_a[l], r_k=r_k[l], lnx_gain=lnx_gain[l], lnx_bias=lnx_bias[l],
                   conv_w=conv_w[l], conv_b=conv_b[l], w_rgate=w_rgate[l], b_rgate=b_rgate[l],
                   w_igate=w_igate[l], b_igate=b_igate[l], lru_lambda=lru_lambda[l], w_out=w_out[l],
                   ln1_gain=ln1_gain[l], ln1_bias=ln1_bias[l], w_router_group=w_router_group[l],
                   b_router_group=b_router_group[l], w_router_expert=w_router_expert[l],
                   b_router_expert=b_router_expert[l], w_exp_gate=w_exp_gate[l],
                   w_exp_up=w_exp_up[l], w_exp_down=w_exp_down[l], ln2_gain=ln2_gain[l],
                   ln2_bias=ln2_bias[l]) for l in range(DEPTH)]
    bp = x_prompt.shape[0]
    z_wkv = jnp.zeros((DEPTH, bp, H_A, HEAD_A, HEAD_A), jnp.float32)
    z_shift = jnp.zeros((DEPTH, bp, D_MODEL), x_prompt.dtype)
    z_conv = jnp.zeros((DEPTH, bp, CONV_W - 1, C_B), x_prompt.dtype)
    z_lru = jnp.zeros((DEPTH, bp, C_B), jnp.float32)
    y_prompt, wkv_p, shift_p, conv_p, lru_p = _trunk(x_prompt, c_prompt, z_wkv, z_shift, z_conv, z_lru, layers)
    y_sample, wkv_s, shift_s, conv_s, lru_s = _trunk(x_sample, c_sample, state_wkv, state_shift,
                                                     state_conv, state_lru, layers)
    return (y_prompt, y_sample, wkv_p, shift_p, conv_p, lru_p, wkv_s, shift_s, conv_s, lru_s)


_drawn_inputs = setup_inputs


def setup_inputs(seed=0):
    import zlib

    import numpy as np

    out = dict(_drawn_inputs(seed))
    spreads = {}
    factors = {'lnx_gain': 4.399,
     'lnx_bias': 30.898,
     'b_rgate': 24.857,
     'b_igate': 8.0,
     'ln1_bias': 4.086,
     'b_router_group': 6.608,
     'b_router_expert': 21.952,
     'ln2_bias': 5.162}
    for name, (base, spread) in spreads.items():
        noise = np.random.default_rng([zlib.crc32(name.encode()), seed]).standard_normal(out[name].shape)
        drawn = base * np.exp(spread * noise) if base else spread * noise
        out[name] = __import__('jax').numpy.asarray(drawn.astype(out[name].dtype))
    for name, factor in factors.items():
        out[name] = (out[name] * factor).astype(out[name].dtype)
    return out
```

```python
from contextlib import ExitStack

import numpy as np
import concourse.bass as bass
from concourse import mybir

ALU = mybir.AluOpType
ACT = mybir.ActivationFunctionType
F32 = mybir.dt.float32
AX_X = mybir.AxisListType.X

P = 128
D_MODEL = 1024
KC = D_MODEL // P
SEQ = 1024
DEC = 8
NTOK = SEQ + DEC
NCOL = NTOK + DEC
NJ = 4
HEAD = 64
CHUNK = 64
HALF = 512
GRP = 256
PAD = 3
NEXP = 16
DEXP = 256
ALPHA = 2 ** 0.25
DECAY = float(np.exp(-0.5))
LN_EPS = 1e-5
GN_EPS = 64e-5
COLS = [(0, 348), (348, 348), (696, 344)]
MCOLS = [(0, 344), (344, 344), (688, 344)]
TILES = [(i * P, P) for i in range(SEQ // P)] + [(SEQ, DEC)]
(MU_R, MU_K, MU_V, W0, A0, K_K, K_A, R_K, LNX_G, LNX_B, CW0, CW1, CW2, CW3, C_BIAS, B_RG, B_IG,
 LAM) = range(18)
NPRM = 18
ARENA = 53000


class Signal:

    def __init__(self, ctx, nc, name):
        self.sem = ctx.enter_context(nc.semaphore(name))
        self.n = 0

    def on(self, ins, k=1):
        ins.then_inc(self.sem, k)
        self.n += k


def build(nc, x_all, c_t, shift_t, wkv0, conv0, lru0, state_conv, w_ada, b_ada, w_in, w_lo, prm, mu_lo,
          w_wa_up, w_g_up, w_rg, w_ig, w_out, ln_rows, w_rt, b_rt, w_gu, w_dn,
          y_all, wkvp_o, wkvs_o, shift_o, conv_o, convs_o, lru_o):
    q_scr = nc.dram_tensor("q_scr", (6, 32, P), F32, kind="Internal").ap()
    y_scr = nc.dram_tensor("y_scr", (32, P), F32, kind="Internal").ap()

    with ExitStack() as ctx:
        def sb(name, shape, stack=ctx):
            return stack.enter_context(nc.sbuf_tensor(name, shape, F32))

        def sem(name):
            return ctx.enter_context(nc.semaphore(name))

        ps = ctx.enter_context(nc.psum_tensor("ps", [P, 8, 512], F32))

        arena = ctx.enter_context(nc.sbuf_tensor("arena", [P, ARENA], F32))
        at = [0]

        def take(n):
            at[0] += n
            assert at[0] <= ARENA
            return arena[:, at[0] - n:at[0]]

        def v3(ap, a):
            return ap.rearrange("p (a b) -> p a b", a=a)

        hT = v3(take(KC * NCOL), KC)
        yT_at = at[0]
        yT = v3(take(KC * NTOK), KC)
        modT = v3(take(48 * 9), 48)
        ident = take(P)
        blk_ones = take(P)
        blk_mean = take(P)
        ones = take(P)
        mask_dt = v3(take(2 * P), 2)
        mask_ak = v3(take(2 * P), 2)
        mask_d = take(P)
        mask_e = take(P)
        par = v3(take(NPRM * NJ), NPRM)
        der = v3(take(12 * NJ), 12)
        mu_wa = take(1)[0:64]
        mu_gd = take(1)[0:96]
        bada = take(48)
        eps = take(2)
        S = v3(take(2 * P), 2)
        sfin = v3(take(NJ * P), NJ)
        lru_last = v3(take(NJ * 9), NJ)
        st = v3(take(12), 2)
        mv = take(2)
        sd = take(1)
        rs = take(1)
        psm = take(3 * NJ * DEC).rearrange("p (q j b) -> p q j b", q=3, j=NJ)
        pgs = v3(take(NJ * DEC), NJ)
        pxs = v3(take(NJ * DEC), NJ)
        base = at[0]

        ld_const = sem("ld_const")
        ld_cs = sem("ld_cs")
        ld_prev = sem("ld_prev")
        ld_samp = sem("ld_samp")
        ld_ada = [sem(f"ld_ada{i}") for i in range(2)]
        ld_x = [sem(f"ld_x{i}") for i in range(3)]
        ld_win = [sem(f"ld_win{i}") for i in range(3)]
        ld_lo = sem("ld_lo")
        consts_ready = sem("consts_ready")
        silu_ready = sem("silu_ready")
        cond_tanh = sem("cond_tanh")
        mod_mm = sem("mod_mm")
        mod_out = sem("mod_out")
        var_ready = sem("var_ready")
        sd_ready = sem("sd_ready")
        xn_ready = sem("xn_ready")
        xn_turned = sem("xn_turned")
        ht_dve = sem("ht_dve")
        ht_act = sem("ht_act")
        params_ready = sem("params_ready")
        lam_exp = sem("lam_exp")
        lam_ln = sem("lam_ln")
        win_mm = sem("win_mm")
        win_out = sem("win_out")
        pads_zero = sem("pads_zero")
        lora_shifted = sem("lora_shifted")
        lora_tanh = sem("lora_tanh")
        lora_ready = sem("lora_ready")
        outs = sem("outs")

        def names(*ns):
            return {n: sem(n) for n in ns}

        h = names("up_mm", "gate_mm", "norm_mm", "bonus_mm", "mean_mm", "var_mm",
                  "tw_ready", "ta_ready", "g_ready", "sq_ready", "nrm_ready", "exp_ready", "gates_tanh",
                  "lru_exp", "lru_mult", "gelu_ready", "conv_ready", "cum_ready", "q_ready",
                  "rkp_ready", "prep_done", "shifted", "bonus_out", "centred", "ysq_ready", "gsd_ready", "half_done")
        g_ = names("gram_b", "gram_k", "gram_l", "turned", "akv_mm", "d2_mm", "p2_mm", "p3_mm", "p4_mm",
                   "f_mm", "z1_mm", "z2_mm", "rt_mm",
                   "dt_out", "ak_out", "de_out", "tok_out", "akv_out", "d2_out", "d4_out", "d8_out",
                   "p1_out", "p2_out", "p3_out", "nt_out", "f_out", "z0_out", "f2_out", "z1_out",
                   "z2_out", "rh_out", "tt_out", "y_out")
        state_mm = sem("state_mm")
        state_out = sem("state_out")
        s_zero = sem("s_zero")
        SAMP = {}
        for who, steps in (("pe", ("s_up", "s_gates", "s_norm", "s_bonmm", "s_turn", "s_yturn", "s_mean", "s_var")),
                           ("act", ("s_wa", "s_lexp", "s_w", "s_nrm", "s_mult", "s_gelu", "s_sqr", "s_gsd")),
                           ("dve", ("s_conv", "s_sq", "s_lam", "s_bon", "s_vec", "s_q", "s_vrow", "s_y", "s_yc",
                                    "s_cent", "s_done"))):
            steps_done = sem(f"sample_steps_{who}")
            SAMP.update({n: (steps_done, i + 1) for i, n in enumerate(steps)})
        samp = names("s_stored", "s_rows", "s_ystored", "s_yrow")
        ld_late = sem("ld_late")
        ld_wout = sem("ld_wout")
        ld_x2 = [sem(f"ld_x2{i}") for i in range(2)]
        row_diag = sem("row_diag")
        row_mm = sem("row_mm")
        row_out = sem("row_out")
        wo_mm = sem("wo_mm")
        wo_out = sem("wo_out")
        v1_ready = sem("v1_ready")
        v1_sd = sem("v1_sd")
        v2_ready = sem("v2_ready")
        v2_sd = sem("v2_sd")
        n1_ready = sem("n1_ready")
        x1_ready = sem("x1_ready")
        n2_ready = sem("n2_ready")
        n2_turned = sem("n2_turned")
        h2_out = sem("h2_out")
        router_mm = sem("router_mm")
        lg_ready = sem("lg_ready")
        ex_ready = sem("ex_ready")
        lg2_ready = sem("lg2_ready")
        ex2_ready = sem("ex2_ready")
        comb_ready = sem("comb_ready")
        ld_exp = [sem(f"ld_exp{i}") for i in range(2)]
        gu_mm = sem("gu_mm")
        silu_out = sem("silu_out")
        hid_out = sem("hid_out")
        dn_mm = sem("dn_mm")
        dn_out = sem("dn_out")
        v3_ready = sem("v3_ready")
        v3_sd = sem("v3_sd")
        n3_ready = sem("n3_ready")
        y_ready = sem("y_ready")
        y_stored = [sem(f"y_stored{i}") for i in range(2)]
        chain_v = Signal(ctx, nc, "chain_v")
        chain_a = Signal(ctx, nc, "chain_a")
        chain_p = Signal(ctx, nc, "chain_p")

        pk, pr, pv, prec, pgate = (take(PAD + NCOL) for _ in range(5))
        pwa = take(PAD + NCOL)[0:64]
        pgd = take(PAD + NCOL)[0:96]
        win = v3(take(3 * KC * P), 3)
        wa_up = take(512)[0:64]
        g_up = take(512)[0:96]
        rg = v3(take(NJ * P), NJ)
        ig = v3(take(NJ * P), NJ)
        reset = take(HALF)
        work = take(16 * HALF)
        (tmp, lam, cum, eP, eN, aa, kk, k2, bb, AR0, AR1, Bh, Kh, rkp, gg, Y) = (
            work[:, i * HALF:(i + 1) * HALF] for i in range(16))
        AR = work[:, 9 * HALF:11 * HALF].rearrange("p (w t) -> p w t", w=2)
        GB = 6144
        grpb = take(2 * GB)
        xc, tr, ti, t2, hs = (grpb[:, i * HALF:(i + 1) * HALF] for i in range(5))
        wlo = grpb[:, 4096:4096 + KC * 160].rearrange("p (k m) -> p k m", k=KC)

        class Grp:
            def __init__(self, g):
                o = g * GB
                self.c0 = g * GRP
                self.b = 4 * g

                def take(n):
                    nonlocal o
                    o += n
                    return grpb[:, o - n:o]
                self.dtg = take(1024).rearrange("p (h a w t) -> p h a w t", h=2, a=2, w=2)
                self.ak = take(1024).rearrange("p (h a w t) -> p h a w t", h=2, a=2, w=2)
                self.ab_flat = take(1024)
                self.a = self.ab_flat[:, 0:512].rearrange("p (h a t) -> p h a t", h=2, a=2)
                self.bt = self.ab_flat[:, 512:1024].rearrange("p (h a t) -> p h a t", h=2, a=2)
                d = take(512)
                self.d = d.rearrange("p (h a t) -> p h a t", h=2, a=2)
                self.tt = d.rearrange("p (c a t) -> p c a t", c=2, a=2)
                self.e = take(512).rearrange("p (h a t) -> p h a t", h=2, a=2)
                self.p_flat = take(512)
                self.p = self.p_flat.rearrange("p (h a t) -> p h a t", h=2, a=2)
                self.z_flat = take(512)
                self.z = self.z_flat.rearrange("p (w a h t) -> p w a h t", w=2, a=2, h=2)
                self.zt = self.z_flat.rearrange("p (w a t) -> p w a t", w=2, a=2)
                self.vb = take(512)
                self.vtok = self.vb[:, 0:256].rearrange("p (a t) -> p a t", a=2)
                self.btok = self.vb[:, 256:512].rearrange("p (a t) -> p a t", a=2)
                self.kflat = take(256)
                self.ktok = self.kflat.rearrange("p (a t) -> p a t", a=2)
                self.rh = take(256)

            def bank(self, i):
                return ps[:, self.b + i, :]
        grp = [Grp(0), Grp(1)]

        ada = [grpb[:, 2048 * i:2048 * (i + 1)].rearrange("p (k m) -> p k m", k=KC) for i in range(2)]
        xr = [work[:, D_MODEL * i:D_MODEL * (i + 1)] for i in range(3)]
        xn = [work[:, D_MODEL * (3 + i):D_MODEL * (4 + i)] for i in range(2)]
        cs = work[:, 5 * D_MODEL:5 * D_MODEL + 72].rearrange("p (k b) -> p k b", k=KC)
        csg = work[:, 5 * D_MODEL + 72:5 * D_MODEL + 144].rearrange("p (k b) -> p k b", k=KC)

        SN = NJ * DEC
        sq_ = [grpb[:, 4096 + SN * i:4096 + SN * (i + 1)].rearrange("p (j b) -> p j b", j=NJ) for i in range(24)]
        (s_lam, s_a, s_kk, s_t, s_t1, s_g, s_bon, s_y, s_xc, s_tr, s_ti, s_t2, s_hs, s_gl, s_mu) = sq_[:15]
        s_vecs = grpb[:, 5120:5120 + 6 * SN].rearrange("p (q j b) -> p q j b", q=6, j=NJ)
        s_vflat = grpb[:, 5120:5120 + 6 * SN]
        s_qt = grpb[0:32, 5400:5400 + 6 * P]
        s_row = grpb[:, 6200:6200 + 5 * HEAD].rearrange("p (q k) -> p q k", q=5)
        s_vr = grpb[:, 6600:6632]
        s_sa = grpb[:, 6640:6672]
        s_yr = grpb[:, 6680:6712]
        s_yrow = grpb[0:32, 6720:6848]
        s_conv = grpb[:, 6900:6900 + 96].rearrange("p (j r b) -> p j r b", j=NJ, r=3)
        s_lru0 = grpb[:, 7000:7032].rearrange("p (j b) -> p j b", j=NJ)
        s_S = work[:, 0:2048].rearrange("p (v k) -> p v k", v=32)
        s_T = work[:, 2048:4096].rearrange("p (v k) -> p v k", v=32)
        s_Sf = work[:, 0:2048]

        at[0] = base
        x1 = v3(take(9 * D_MODEL), 9)
        g2b = take(D_MODEL)
        g2s = take(D_MODEL)
        lnr = v3(take(4 * D_MODEL), 4)
        lgt = v3(take(9 * 20), 9)
        rt_a = [v3(take(9 * 4), 9) for _ in range(8)]
        rt_s = [take(9) for _ in range(8)]
        comb = v3(take(9 * NEXP), 9)
        wrt = v3(take(KC * 20), KC)
        brt = take(20)
        late = at[0]
        wout = v3(take(KC * D_MODEL), KC)
        g1b = take(D_MODEL)
        g1s = take(D_MODEL)
        xr2 = v3(take(2 * D_MODEL), 2)
        zz = take(D_MODEL)
        n2 = v3(take(2 * D_MODEL), 2)
        diag = v3(take(8 * P), 8)
        h2T = hT[:, :, 0:NTOK]
        at[0] = late
        acc = v3(take(9 * D_MODEL), 9)
        exw = [take(3 * 2048), arena[:, yT_at:yT_at + 3 * 2048]]
        sil = v3(take(2 * 344), 2)
        hid = v3(arena[:, yT_at + 3 * 2048:yT_at + 3 * 2048 + 2 * NTOK], 2)
        fz = v3(exw[0][:, 0:2 * D_MODEL], 2)

        block = ctx.enter_context(nc.Block())
        V, A, T, G = nc.vector, nc.scalar, nc.tensor, nc.gpsimd
        HV = {**h, **g_, **samp}

        def pcol(q, j):
            return par[:, q, j:j + 1]

        D_W0, D_A0, D_OKA, D_RG, D_IG, D_ML, D_NML, D_TMP = range(8)

        def dcol(q, j):
            return der[:, q, j:j + 1]

        @block.sync
        def _(sp):
            sp.dma_start(cs, c_t).then_inc(ld_cs, 16)
            for dst, src in ((par, prm), (mu_wa, mu_lo[0:64]), (mu_gd, mu_lo[64:160]), (bada, b_ada),
                             (wa_up, w_wa_up), (g_up, w_g_up)):
                sp.dma_start(dst, src).then_inc(ld_const, 16)
            sp.wait_ge(consts_ready, 1)
            for n in range(2):
                for dst, src in ((rg, w_rg), (ig, w_ig)):
                    r0 = slice(64 * n, 64 * n + 64)
                    sp.dma_start(dst[r0, :, r0], src[:, r0, :].rearrange("j c d -> c j d")).then_inc(ld_const, 16)
            sp.dma_start(hT[:, :, NTOK:NCOL], shift_t).then_inc(ld_prev, 16)
            for i in range(3):
                sp.dma_start(xr[i], x_all[P * i:P * i + P, :]).then_inc(ld_x[i], 16)
            for n in range(24):
                if n >= 2:
                    sp.wait_ge(mod_mm, n - 1)
                sp.dma_start(ada[n % 2].rearrange("p k m -> p (k m)"), w_ada[n]).then_inc(ld_ada[n % 2], 16)
            for i, (r0, rt) in enumerate(TILES[3:]):
                sp.wait_ge(xn_ready, i + 1)
                sp.dma_start(xr[i % 3][0:rt], x_all[r0:r0 + rt, :]).then_inc(ld_x[i % 3], 16)
            sp.wait_ge(mod_mm, 24)
            sp.dma_start(wlo.rearrange("p k m -> p (k m)"), w_lo).then_inc(ld_lo, 16)
            for n in range(5 * NJ):
                if n >= 3:
                    sp.wait_ge(win_mm, 3 * (n - 3 + 2) + 3)
                sp.dma_start(win[:, n % 3, :], w_in[n]).then_inc(ld_win[n % 3], 16)

        @block.gpsimd
        def _(pool):
            def link(ins):
                chain_p.on(ins)
                pool.wait_ge(chain_p.sem, chain_p.n)

            def select(t, pattern, op, base, cm):
                link(G.affine_select(out=t, in_=t, compare_op=op, fill=0.0, base=base, pattern=pattern,
                                     channel_multiplier=cm))

            def same_block(t, size):
                v = t.rearrange("p (n c) -> p n c", c=size)
                select(v, [[-size, P // size], [0, size]], ALU.is_ge, 0, 1)
                select(v, [[size, P // size], [0, size]], ALU.is_ge, size - 1, -1)

            def later_block(t, size):
                v = t.rearrange("p (n c) -> p n c", c=size)
                select(v, [[-size, P // size], [0, size]], ALU.is_ge, -size, 1)

            for t in (rg, ig):
                link(G.memset(t, 0.0))
            link(G.memset(ones, 1.0))
            for t in (ident, blk_ones, mask_dt[:, 0], mask_dt[:, 1], mask_ak[:, 0], mask_d, mask_e):
                link(G.memset(t, 1.0))
            link(G.memset(eps[:, 0:1], LN_EPS))
            link(G.memset(eps[:, 1:2], GN_EPS))
            link(G.memset(reset, 1.0))
            link(G.memset(reset.rearrange("p (c t) -> p c t", t=CHUNK)[:, :, 0:1], 0.0))
            for t in (pk, pr, pv, prec, pwa, pgd):
                link(G.memset(t[:, 0:PAD], 0.0))
            select(ident, [[-1, P]], ALU.is_equal, 0, 1)
            same_block(blk_ones, HEAD)
            same_block(mask_dt[:, 0], 16)
            select(mask_dt[:, 0], [[1, P]], ALU.is_gt, 0, -1)
            same_block(mask_dt[:, 1], CHUNK)
            select(mask_dt[:, 1], [[1, P]], ALU.is_ge, 0, -1)
            same_block(mask_ak[:, 0], CHUNK)
            select(mask_ak[:, 0], [[1, P]], ALU.is_gt, 0, -1)
            link(G.tensor_copy(mask_ak[:, 1], mask_dt[:, 1]))
            same_block(mask_d, 16)
            select(mask_d, [[-1, P]], ALU.is_gt, 0, 1)
            same_block(mask_e, CHUNK)
            later_block(mask_e, 16)
            G.tensor_scalar(blk_mean, blk_ones, 1.0 / HEAD, None, ALU.mult).then_inc(consts_ready, 1)
            pool.wait_ge(ht_dve, 9)
            pool.wait_ge(ht_act, 8)
            pool.dma_start(shift_o, hT[:, :, SEQ - 1:NTOK]).then_inc(outs, 16)
            pool.dma_start(convs_o, state_conv[:, 1:3, :]).then_inc(outs, 16)
            for j in range(NJ):
                pool.wait_ge(win_out, 6 + 15 * j + 12)
                pool.dma_start(conv_o[j], prec[:, PAD + SEQ - 3:PAD + NTOK]).then_inc(outs, 16)
            pool.wait_ge(HV["half_done"], 2 * NJ)
            pool.wait_ge(HV["y_out"], 16)
            pool.dma_start(s_Sf, wkv0).then_inc(ld_samp, 16)
            pool.dma_start(s_conv, conv0).then_inc(ld_samp, 16)
            pool.dma_start(s_lru0, lru0).then_inc(ld_samp, 16)
            pool.wait_ge(*SAMP["s_vrow"])
            pool.dma_start(q_scr.rearrange("q r c -> r q c"), s_qt.rearrange("r (q c) -> r q c", q=6)).then_inc(HV["s_stored"], 16)
            pool.wait_ge(HV["s_stored"], 16)
            flat = q_scr.rearrange("q r c -> q (r c)")
            for n, q in enumerate((0, 1, 2, 4, 5)):
                src = flat[q].rearrange("(r k) -> r k", k=HEAD).unsqueeze(1).to_broadcast([64, 2, HEAD])
                pool.dma_start(s_row[:, n, :], src).then_inc(HV["s_rows"], 16)
            pool.dma_start(s_vr, flat[3].rearrange("(r k) -> r k", k=32)).then_inc(HV["s_rows"], 16)
            pool.wait_ge(*SAMP["s_y"])
            pool.dma_start(wkvs_o, s_Sf).then_inc(outs, 16)
            pool.dma_start(y_scr.rearrange("r c -> (r c)").rearrange("(p v) -> p v", v=32), s_yr).then_inc(HV["s_ystored"], 16)
            pool.wait_ge(HV["s_ystored"], 16)
            pool.dma_start(s_yrow, y_scr).then_inc(HV["s_yrow"], 16)
            pool.dma_start(wkvp_o.rearrange("j p v -> p j v"), sfin).then_inc(outs, 16)
            pool.wait_ge(*SAMP["s_done"])
            pool.dma_start(lru_o, lru_last).then_inc(outs, 16)
            pool.wait_ge(outs, 16 * 9)
            for k in range(KC):
                pool.dma_start(wout[:, k, :], w_out[k]).then_inc(ld_wout, 16)
            for n in range(4):
                pool.dma_start(lnr[:, n, :], ln_rows[n:n + 1, :].partition_broadcast(P)).then_inc(ld_late, 16)
            pool.dma_start(wrt, w_rt).then_inc(ld_late, 16)
            pool.dma_start(brt, b_rt.partition_broadcast(P)).then_inc(ld_late, 16)
            for i, (r0, rt) in enumerate(TILES):
                if i >= 2:
                    pool.wait_ge(v1_ready, i - 1)
                pool.dma_start(xr2[0:rt, i % 2, :], x_all[r0:r0 + rt, :]).then_inc(ld_x2[i % 2], 16)
            for e in range(NEXP):
                if e == 0:
                    pool.wait_ge(h2_out, 9)
                    pool.wait_ge(wo_mm, 18)
                if e >= 2:
                    pool.wait_ge(dn_mm, 18 * (e - 1))
                slot = exw[e % 2]
                pool.dma_start(slot[:, 0:4096], w_gu[e]).then_inc(ld_exp[e % 2], 16)
                pool.dma_start(slot[:, 4096:6144], w_dn[e]).then_inc(ld_exp[e % 2], 16)
            for i, (r0, rt) in enumerate(TILES):
                pool.wait_ge(y_ready, i + 1)
                pool.dma_start(y_all[r0:r0 + rt, :], fz[0:rt, i % 2, :]).then_inc(y_stored[i % 2], 16)
            pool.wait_ge(outs, 16 * 9)
            pool.wait_ge(y_stored[0], 16 * 5)
            pool.wait_ge(y_stored[1], 16 * 4)

        @block.tensor
        def _(pe):
            bank = [ps[:, i, :] for i in range(8)]
            pe.wait_ge(silu_ready, 1)
            for n in range(24):
                pe.wait_ge(ld_ada[n % 2], 16 * (n // 2 + 1))
                if n >= 2:
                    pe.wait_ge(mod_out, n - 1)
                for m in range(2):
                    for k in range(KC):
                        mm = T.matmul(ps[:, n % 2, 16 * m:16 * m + 9], ada[n % 2][:, k, P * m:P * m + P],
                                      csg[:, k, :], start=(k == 0), stop=(k == KC - 1))
                mm.then_inc(mod_mm, 1)
            pe.wait_ge(consts_ready, 1)
            for i, (r0, rt) in enumerate(TILES):
                pe.wait_ge(xn_ready, i + 1)
                if i >= 2:
                    pe.wait_ge(ht_dve, i - 1)
                    pe.wait_ge(ht_act, i - 1)
                for k in range(KC):
                    tr_ = T.transpose(ps[:, 2 + 2 * (i % 2) + k // 4, P * (k % 4):P * (k % 4) + rt],
                                      xn[i % 2][0:rt, P * k:P * k + P], ident[0:rt, 0:rt])
                tr_.then_inc(xn_turned, 1)
            pe.wait_ge(ht_dve, 9)
            pe.wait_ge(ht_act, 8)
            pe.wait_ge(ld_prev, 16)

            def project(n, lhs, rows):
                for c, (c0, w) in enumerate(COLS):
                    if n:
                        pe.wait_ge(win_out, 3 * (n - 1) + c + 1)
                    for k in range(KC):
                        mm = T.matmul(ps[0:rows, c, 0:w], lhs(k), hT[:, k, c0:c0 + w],
                                      start=(k == 0), stop=(k == KC - 1))
                    mm.then_inc(win_mm, 1)

            pe.wait_ge(ld_lo, 16)
            project(0, lambda k: wlo[:, k, 0:64], 64)
            project(1, lambda k: wlo[:, k, 64:160], 96)
            pe.wait_ge(ld_const, 16 * 10)
            for j in range(NJ):
                if j:
                    pe.wait_ge(HV["half_done"], 2 * j)
                for q in range(5):
                    n = 5 * j + q
                    pe.wait_ge(ld_win[n % 3], 16 * (n // 3 + 1))
                    project(n + 2, lambda k: win[:, n % 3, P * k:P * k + P], P)
                for hf in range(2):
                    it = 2 * j + hf
                    t0 = PAD + hf * HALF
                    js = slice(P * j, P * j + P)
                    if it == 0:
                        pe.wait_ge(lora_ready, 1)
                    if it:
                        pe.wait_ge(HV["half_done"], it)
                    pe.wait_ge(win_out, 3 * (5 * j + 7))
                    T.matmul(bank[3], wa_up[0:32, js], pwa[0:32, t0:t0 + HALF], start=True, stop=True)
                    T.matmul(bank[4], wa_up[32:64, js], pwa[32:64, t0:t0 + HALF], start=True, stop=True)
                    T.matmul(bank[5], g_up[:, js], pgd[:, t0:t0 + HALF], start=True, stop=True).then_inc(HV["up_mm"], 1)
                    pe.wait_ge(HV["sq_ready"], it + 1)
                    T.matmul(bank[6], blk_ones, tmp, start=True, stop=True).then_inc(HV["norm_mm"], 1)
                    pe.wait_ge(HV["conv_ready"], it + 1)
                    T.matmul(bank[0], rg[:, j, :], xc, start=True, stop=True)
                    T.matmul(bank[1], ig[:, j, :], xc, start=True, stop=True).then_inc(HV["gate_mm"], 1)
                    pe.wait_ge(HV["rkp_ready"], it + 1)
                    T.matmul(bank[7], blk_ones, rkp, start=True, stop=True).then_inc(HV["bonus_mm"], 1)
                    pe.wait_ge(HV["prep_done"], it + 1)
                    pe.wait_ge(HV["bonus_out"], it + 1)

                    def heads():
                        for hh in range(2):
                            for a in range(2):
                                yield hh, a, slice(HEAD * hh, HEAD * hh + HEAD)

                    def stage(g, name, waits, products):
                        gi = 2 * it + g
                        for w in waits:
                            pe.wait_ge(HV[w], gi + 1)
                        for out, lhs, rhs in products:
                            mm = T.matmul(out, lhs, rhs, start=True, stop=True)
                        mm.then_inc(HV[name], 1)

                    def unit(g, b):
                        return grp[g].bank(b).rearrange("p (h a t) -> p h a t", h=2, a=2)

                    def zunit(g, b):
                        return grp[g].bank(b).rearrange("p (w a h t) -> p w a h t", w=2, a=2, h=2)

                    def toks(g, a):
                        return slice(grp[g].c0 + P * a, grp[g].c0 + P * a + P)

                    for g in range(2):
                        q = grp[g]
                        stage(g, "gram_b", (), [(q.bank(hh)[:, 256 * a:256 * a + 256], bb[r, toks(g, a)],
                                                 AR[r, :, toks(g, a)]) for hh, a, r in heads()])
                    for g in range(2):
                        q = grp[g]
                        stage(g, "gram_k", (), [(q.bank(2 + hh)[:, 256 * a:256 * a + 256], k2[r, toks(g, a)],
                                                 AR[r, :, toks(g, a)]) for hh, a, r in heads()])
                    for g in range(2):
                        q = grp[g]
                        stage(g, "gram_l", ("dt_out",), [(q.bank(hh)[:, P * a:P * a + P], AR0[r, toks(g, a)],
                                                          bb[r, toks(g, a)]) for hh, a, r in heads()])
                    for g in range(2):
                        q = grp[g]
                        pe.wait_ge(HV["ak_out"], 2 * it + g + 1)
                        for a in range(2):
                            for b_, o, src in ((2, 0, AR0[:, toks(g, a)]), (2, 256, Kh[:, toks(g, a)]),
                                               (3, 0, pv[:, t0 + q.c0 + P * a:t0 + q.c0 + P * a + P]),
                                               (3, 256, Bh[:, toks(g, a)])):
                                mm = T.transpose(q.bank(b_)[:, o + P * a:o + P * a + P], src, ident)
                        mm.then_inc(HV["turned"], 1)
                    for g in range(2):
                        q = grp[g]
                        stage(g, "akv_mm", ("tok_out",),
                              [(q.bank(3)[:, P * a + HEAD * hh:P * a + HEAD * hh + HEAD], q.ak[:, hh, a, 0, :],
                                q.vtok[:, a, HEAD * hh:HEAD * hh + HEAD]) for hh, a, r in heads()])
                    for g in range(2):
                        q = grp[g]
                        stage(g, "d2_mm", ("de_out",),
                              [(unit(g, 0)[:, hh, a], q.dtg[:, hh, a, 0, :], q.d[:, hh, a]) for hh, a, r in heads()] +
                              [(unit(g, 1)[:, hh, a], q.d[:, hh, a], q.dtg[:, hh, a, 0, :]) for hh, a, r in heads()])
                    for g in range(2):
                        q = grp[g]
                        stage(g, "p2_mm", ("d2_out", "p1_out"),
                              [(unit(g, 2)[:, hh, a], q.a[:, hh, a], q.p[:, hh, a]) for hh, a, r in heads()] +
                              [(unit(g, 0)[:, hh, a], q.bt[:, hh, a], q.a[:, hh, a]) for hh, a, r in heads()] +
                              [(unit(g, 1)[:, hh, a], q.a[:, hh, a], q.bt[:, hh, a]) for hh, a, r in heads()])
                    for g in range(2):
                        q = grp[g]
                        stage(g, "p3_mm", ("d4_out", "p2_out"),
                              [(unit(g, 2)[:, hh, a], q.a[:, hh, a], q.p[:, hh, a]) for hh, a, r in heads()] +
                              [(unit(g, 0)[:, hh, a], q.bt[:, hh, a], q.a[:, hh, a]) for hh, a, r in heads()])
                    for g in range(2):
                        q = grp[g]
                        stage(g, "p4_mm", ("d8_out", "p3_out"),
                              [(unit(g, 2)[:, hh, a], q.a[:, hh, a], q.p[:, hh, a]) for hh, a, r in heads()])
                    for g in range(2):
                        q = grp[g]
                        stage(g, "f_mm", ("nt_out", "akv_out"),
                              [(unit(g, 0)[:, hh, a], q.p[:, hh, a], q.e[:, hh, a]) for hh, a, r in heads()] +
                              [(unit(g, 1)[:, hh, a], q.e[:, hh, a], q.p[:, hh, a]) for hh, a, r in heads()] +
                              [(zunit(g, 2)[:, :, a, hh], q.p[:, hh, a], q.z[:, :, a, hh]) for hh, a, r in heads()])
                    for g in range(2):
                        q = grp[g]
                        stage(g, "z1_mm", ("f_out", "z0_out"),
                              [(unit(g, 0)[:, hh, a], q.a[:, hh, a], q.bt[:, hh, a]) for hh, a, r in heads()] +
                              [(zunit(g, 2)[:, :, a, hh], q.bt[:, hh, a], q.z[:, :, a, hh]) for hh, a, r in heads()])
                    for g in range(2):
                        q = grp[g]
                        stage(g, "z2_mm", ("f2_out", "z1_out"),
                              [(zunit(g, 1)[:, :, a, hh], q.a[:, hh, a], q.z[:, :, a, hh]) for hh, a, r in heads()])
                    for g in range(2):
                        q = grp[g]
                        stage(g, "rt_mm", ("z2_out",),
                              [(q.bank(0)[r, P * a:P * a + P], q.z[:, 0, a, hh, :], q.dtg[:, hh, a, 1, :])
                               for hh, a, r in heads()] +
                              [(q.bank(2 + c)[:, P * a:P * a + P], q.zt[HEAD * c:HEAD * c + HEAD, 0, a, :],
                                q.btok[HEAD * c:HEAD * c + HEAD, a, :]) for a in range(2) for c in range(2)])
                    for g in range(2):
                        q = grp[g]
                        gi = 2 * it + g
                        for hh, a, r in heads():
                            T.matmul(q.bank(1)[r, P * a:P * a + P], q.z[:, 1, a, hh, :], q.dtg[:, hh, a, 1, :],
                                     start=(a == 0), stop=False, skip_group_check=True)
                            T.matmul(q.bank(1)[r, P * a:P * a + P], q.vtok[:, a, r], q.ak[:, hh, a, 1, :],
                                     start=False, stop=False, skip_group_check=True)
                        pe.wait_ge(HV["tt_out"], gi + 1)
                        pe.wait_ge(HV["rh_out"], gi + 1)
                        for n in range(4):
                            a, c = n // 2, n % 2
                            r = slice(HEAD * c, HEAD * c + HEAD)
                            out = q.bank(2 + c)[:, 256:384]
                            if 4 * gi + n >= 2:
                                pe.wait_ge(state_out, 4 * gi + n - 1)
                            T.matmul(out, q.btok[r, a, :], q.zt[r, 1, a, :], start=True, stop=False)
                            T.matmul(out, q.ktok[r, a, :], q.vtok[r, a, :], start=False, stop=False)
                            cur = 4 * gi + n
                            if 4 * (gi % 4) + n == 0:
                                pe.wait_ge(s_zero, j + 1)
                            if cur:
                                pe.wait_ge(state_out, cur)
                            t_ = slice(P * a + HEAD * c, P * a + HEAD * c + HEAD)
                            T.matmul(q.bank(1)[:, t_], S[:, n % 2, :], q.rh[:, t_], start=False,
                                     stop=(n == 3), skip_group_check=True)
                            T.matmul(out, q.tt[:, c, a, :], S[:, n % 2, :], start=False, stop=True).then_inc(state_mm, 1)
                    pe.wait_ge(HV["y_out"], 2 * it + 2)
                    T.matmul(bank[0], blk_mean, Y, start=True, stop=True).then_inc(HV["mean_mm"], 1)
                    pe.wait_ge(HV["ysq_ready"], it + 1)
                    T.matmul(bank[1], blk_mean, tmp, start=True, stop=True).then_inc(HV["var_mm"], 1)

            pe.wait_ge(HV["half_done"], 2 * NJ)
            for b_, lhs, rhs in ((0, wa_up[0:32], pwa[0:32]), (1, wa_up[32:64], pwa[32:64]), (2, g_up, pgd)):
                for j in range(NJ):
                    mm = T.matmul(bank[b_][:, DEC * j:DEC * j + DEC], lhs[:, P * j:P * j + P],
                                  rhs[:, PAD + SEQ:PAD + NTOK], start=True, stop=True)
            mm.then_inc(SAMP["s_up"][0], 1)
            pe.wait_ge(*SAMP["s_conv"])
            for b_, w_ in ((3, rg), (4, ig)):
                for j in range(NJ):
                    mm = T.matmul(bank[b_][:, DEC * j:DEC * j + DEC], w_[:, j, :], s_xc[:, j, :],
                                  start=True, stop=True)
            mm.then_inc(SAMP["s_gates"][0], 1)
            pe.wait_ge(*SAMP["s_sq"])
            T.matmul(bank[5][:, 0:SN], blk_ones, s_t.rearrange("p j b -> p (j b)"), start=True,
                     stop=True).then_inc(SAMP["s_norm"][0], 1)
            pe.wait_ge(*SAMP["s_bon"])
            T.matmul(bank[6][:, 0:SN], blk_ones, s_t1.rearrange("p j b -> p (j b)"), start=True,
                     stop=True).then_inc(SAMP["s_bonmm"][0], 1)
            pe.wait_ge(*SAMP["s_vec"])
            for q in range(6):
                mm = T.transpose(bank[q // 4][0:SN, P * (q % 4):P * (q % 4) + P], s_vflat[:, SN * q:SN * q + SN], ident)
            mm.then_inc(SAMP["s_turn"][0], 1)
            pe.wait_ge(HV["s_yrow"], 16)
            T.transpose(bank[2][:, 0:SN], s_yrow, ident[0:SN, 0:SN]).then_inc(SAMP["s_yturn"][0], 1)
            pe.wait_ge(*SAMP["s_yc"])
            T.matmul(bank[3][:, 0:SN], blk_mean, s_y.rearrange("p j b -> p (j b)"), start=True,
                     stop=True).then_inc(SAMP["s_mean"][0], 1)
            pe.wait_ge(*SAMP["s_sqr"])
            T.matmul(bank[4][:, 0:SN], blk_mean, s_t.rearrange("p j b -> p (j b)"), start=True,
                     stop=True).then_inc(SAMP["s_var"][0], 1)

            for k in range(2 * KC):
                pe.wait_ge(row_diag, k + 1)
                if k >= 2:
                    pe.wait_ge(row_out, k - 1)
                T.matmul(bank[5 + k % 2][:, 0:P], ones, diag[:, k % 8, :], start=True, stop=True)
                T.transpose(bank[5 + k % 2][0:DEC, P:2 * P], modT[:, (16 if k < 8 else 40) + k % 8, 1:9],
                            ident).then_inc(row_mm, 1)
            pe.wait_ge(ld_wout, 16 * KC)
            pe.wait_ge(*SAMP["s_done"])

            def turn_n2(i):
                r0, rt = TILES[i]
                pe.wait_ge(n2_ready, i + 1)
                if i:
                    pe.wait_ge(h2_out, i)
                for k in range(KC):
                    mm = T.transpose(ps[:, 4 + k // 4, P * (k % 4):P * (k % 4) + rt],
                                     n2[0:rt, i % 2, P * k:P * k + P], ident[0:rt, 0:rt])
                mm.then_inc(n2_turned, 1)

            for i, (r0, rt) in enumerate(TILES):
                for n in range(2):
                    if i >= 2:
                        pe.wait_ge(wo_out, i - 1)
                    for k in range(KC):
                        mm = T.matmul(ps[0:rt, 2 * (i % 2) + n, :], yT[:, k, r0:r0 + rt],
                                      wout[:, k, 512 * n:512 * n + 512], start=(k == 0), stop=(k == KC - 1))
                    mm.then_inc(wo_mm, 1)
                if i:
                    turn_n2(i - 1)
            turn_n2(8)
            pe.wait_ge(ld_late, 16 * 6)
            for i, (r0, rt) in enumerate(TILES):
                pe.wait_ge(h2_out, i + 1)
                for k in range(KC):
                    mm = T.matmul(ps[0:rt, 6, 20 * i:20 * i + 20], h2T[:, k, r0:r0 + rt], wrt[:, k, :],
                                  start=(k == 0), stop=(k == KC - 1))
            mm.then_inc(router_mm, 1)
            pe.wait_ge(lg_ready, 1)
            for e in range(NEXP):
                w = exw[e % 2]
                wg = w[:, 0:2048].rearrange("p (k f) -> p k f", k=KC)
                wu = w[:, 2048:4096].rearrange("p (k f) -> p k f", k=KC)
                wd = w[:, 4096:6144].rearrange("p (c d) -> p c d", c=2)
                pe.wait_ge(ld_exp[e % 2], 32 * (e // 2 + 1))
                for f in range(2):
                    for c, (c0, wi) in enumerate(MCOLS):
                        n = 6 * e + 3 * f + c
                        if n >= 2:
                            pe.wait_ge(hid_out, n - 1)
                        for b_, ww in ((0, wg), (1, wu)):
                            for k in range(KC):
                                mm = T.matmul(ps[:, 2 * (n % 2) + b_, 0:wi], ww[:, k, P * f:P * f + P],
                                              h2T[:, k, c0:c0 + wi], start=(k == 0), stop=(k == KC - 1))
                        mm.then_inc(gu_mm, 1)
                pe.wait_ge(hid_out, 6 * (e + 1))
                for i, (r0, rt) in enumerate(TILES):
                    for n in range(2):
                        m = 18 * e + 2 * i + n
                        if m >= 4:
                            pe.wait_ge(dn_out, m - 3)
                        for c in range(2):
                            mm = T.matmul(ps[0:rt, 4 + m % 4, :], hid[:, c, r0:r0 + rt],
                                          wd[:, c, 512 * n:512 * n + 512], start=(c == 0), stop=(c == 1))
                        mm.then_inc(dn_mm, 1)

        @block.scalar
        def _(act):
            def link(ins):
                chain_a.on(ins)
                act.wait_ge(chain_a.sem, chain_a.n)

            act.wait_ge(ld_cs, 16)
            A.activation(csg, cs, ACT.Tanh, scale=0.5).then_inc(cond_tanh, 1)
            act.wait_ge(ld_const, 16 * 10)
            link(A.activation(der[:, D_TMP, :], par[:, LAM, :], ACT.Abs))
            link(A.activation(der[:, D_TMP, :], der[:, D_TMP, :], ACT.Exp, scale=-1.0))
            A.activation(der[:, D_TMP, :], der[:, D_TMP, :], ACT.Ln, bias=ones[:, 0:1]).then_inc(lam_ln, 1)
            for i, (r0, rt) in enumerate(TILES):
                act.wait_ge(var_ready, i + 1)
                if i >= 1:
                    act.wait_ge(xn_ready, i)
                A.activation(sd[0:rt], mv[0:rt, 1:2], ACT.Sqrt, bias=eps[0:rt, 0:1]).then_inc(sd_ready, 1)
                if i < 8:
                    if i == 0:
                        act.wait_ge(mod_out, 8)
                    act.wait_ge(xn_turned, i + 1)
                    for k in range(4, 8):
                        last = A.activation(hT[:, k, r0:r0 + rt], ps[:, 3 + 2 * (i % 2), P * (k - 4):P * (k - 3)],
                                            ACT.Identity, bias=modT[:, k, 0:1], scale=modT[:, 8 + k, 0:1])
                    last.then_inc(ht_act, 1)

            def project_out(n, dst):
                for c, (c0, w) in enumerate(COLS):
                    act.wait_ge(win_mm, 3 * n + c + 1)
                    A.activation(dst[:, PAD + c0:PAD + c0 + w], ps[0:dst.shape[0], c, 0:w], ACT.Copy).then_inc(win_out, 1)

            project_out(0, pwa)
            project_out(1, pgd)
            act.wait_ge(lora_shifted, 1)
            A.activation(pwa[0:32, PAD:PAD + NTOK], pwa[0:32, PAD:PAD + NTOK], ACT.Tanh).then_inc(lora_tanh, 1)
            A.activation(pgd[:, PAD:PAD + NTOK], pgd[:, PAD:PAD + NTOK], ACT.Tanh, scale=0.5).then_inc(lora_tanh, 1)
            act.wait_ge(params_ready, 1)
            for j in range(NJ):
                if j:
                    act.wait_ge(HV["half_done"], 2 * j)
                for q, dst in enumerate((pk, pr, pv, prec, pgate)):
                    if q == 3 and j:
                        act.wait_ge(outs, 16 * (2 + j))
                    project_out(2 + 5 * j + q, dst)
                for hf in range(2):
                    it = 2 * j + hf
                    o = PAD + hf * HALF
                    cols = slice(o, o + HALF)
                    if it:
                        act.wait_ge(HV["half_done"], it)
                    act.wait_ge(HV["up_mm"], it + 1)
                    A.activation(lam, ps[:, 3, :], ACT.Tanh, scale=0.5, bias=dcol(D_W0, j)).then_inc(HV["tw_ready"], 1)
                    A.activation(aa, ps[:, 4, :], ACT.Tanh, scale=0.5, bias=dcol(D_A0, j)).then_inc(HV["ta_ready"], 1)
                    A.activation(gg, ps[:, 5, :], ACT.Copy).then_inc(HV["g_ready"], 1)
                    act.wait_ge(HV["shifted"], j + 1)
                    A.activation(tmp, pk[:, cols], ACT.Square, scale=pcol(K_K, j)).then_inc(HV["sq_ready"], 1)
                    act.wait_ge(HV["norm_mm"], it + 1)
                    A.activation(kk, ps[:, 6, :], ACT.Sqrt).then_inc(HV["nrm_ready"], 1)
                    act.wait_ge(HV["gate_mm"], it + 1)
                    link(A.activation(tr, ps[:, 0, :], ACT.Tanh, scale=0.5, bias=dcol(D_RG, j)))
                    A.activation(ti, ps[:, 1, :], ACT.Tanh, scale=0.5, bias=dcol(D_IG, j)).then_inc(HV["gates_tanh"], 1)
                    link(A.activation(t2, tr, ACT.Tanh, scale=dcol(D_ML, j), bias=dcol(D_ML, j)))
                    A.activation(tr, tr, ACT.Exp, scale=dcol(D_NML, j), bias=dcol(D_NML, j)).then_inc(HV["lru_exp"], 1)
                    act.wait_ge(HV["cum_ready"], it + 1)
                    A.activation(eP, cum, ACT.Exp)
                    A.activation(lam, lam, ACT.Exp)
                    A.activation(eN, cum, ACT.Exp, scale=-1.0).then_inc(HV["exp_ready"], 1)
                    act.wait_ge(HV["q_ready"], it + 1)
                    A.activation(t2, t2, ACT.Sqrt).then_inc(HV["lru_mult"], 1)
                    A.activation(pgate[:, cols], pgate[:, cols], ACT.Gelu_apprx_tanh).then_inc(HV["gelu_ready"], 1)

                    def out(g, name, wait, dst, src):
                        act.wait_ge(HV[wait], 2 * it + g + 1)
                        A.activation(dst, src, ACT.Copy).then_inc(HV[name], 1)

                    def two(g, b):
                        return ps[:, 4 * g + b:4 * g + b + 2, :].rearrange("p b x -> p (b x)")

                    for g in range(2):
                        q = grp[g]
                        act.wait_ge(HV["turned"], 2 * it + g + 1)
                        A.activation(q.vb, q.bank(3), ACT.Copy)
                        A.activation(q.kflat, q.bank(2)[:, 256:512], ACT.Copy)
                        A.activation(q.z_flat[:, 0:256], q.bank(2)[:, 0:256], ACT.Copy).then_inc(HV["tok_out"], 1)
                    for g in range(2):
                        q = grp[g]
                        out(g, "akv_out", "akv_mm", q.z_flat[:, 256:512], q.bank(3)[:, 0:256])
                    for g in range(2):
                        out(g, "d2_out", "d2_mm", grp[g].ab_flat, two(g, 0))
                    for g in range(2):
                        out(g, "d4_out", "p2_mm", grp[g].ab_flat, two(g, 0))
                    for g in range(2):
                        out(g, "d8_out", "p3_mm", grp[g].ab_flat[:, 0:512], grp[g].bank(0))
                    for g in range(2):
                        out(g, "f_out", "f_mm", grp[g].ab_flat, two(g, 0))
                    for g in range(2):
                        out(g, "f2_out", "z1_mm", grp[g].ab_flat[:, 0:512], grp[g].bank(0))
                    for g in range(2):
                        q = grp[g]
                        act.wait_ge(state_mm, 4 * (2 * it + g + 1))
                        A.activation(Y[:, q.c0:q.c0 + GRP], q.bank(1)[:, 0:GRP], ACT.Copy).then_inc(HV["y_out"], 1)
                    act.wait_ge(HV["centred"], it + 1)
                    A.activation(tmp, Y, ACT.Square).then_inc(HV["ysq_ready"], 1)
                    act.wait_ge(HV["var_mm"], it + 1)
                    A.activation(eP, ps[:, 1, :], ACT.Sqrt, bias=eps[:, 1:2]).then_inc(HV["gsd_ready"], 1)


            def tile_act(dst, src, f, scale, bias):
                for j in range(NJ):
                    s_ = dcol(scale, j) if isinstance(scale, int) else scale
                    last = A.activation(dst[:, j, :], src(j), f, scale=s_, bias=dcol(bias, j))
                return last

            def pcols(b_):
                return lambda j: ps[:, b_, DEC * j:DEC * j + DEC]

            act.wait_ge(*SAMP["s_up"])
            tile_act(s_lam, pcols(0), ACT.Tanh, 0.5, D_W0)
            tile_act(s_a, pcols(1), ACT.Tanh, 0.5, D_A0)
            A.activation(s_g, ps[:, 2, 0:SN].rearrange("p (j b) -> p j b", j=NJ), ACT.Copy).then_inc(SAMP["s_wa"][0], 1)
            act.wait_ge(*SAMP["s_gates"])
            tile_act(s_tr, pcols(3), ACT.Tanh, 0.5, D_RG)
            link(tile_act(s_ti, pcols(4), ACT.Tanh, 0.5, D_IG))
            link(tile_act(s_t2, lambda j: s_tr[:, j, :], ACT.Tanh, D_ML, D_ML))
            tile_act(s_tr, lambda j: s_tr[:, j, :], ACT.Exp, D_NML, D_NML).then_inc(SAMP["s_lexp"][0], 1)
            act.wait_ge(*SAMP["s_lam"])
            A.activation(s_vecs[:, 1], s_lam, ACT.Exp).then_inc(SAMP["s_w"][0], 1)
            act.wait_ge(*SAMP["s_norm"])
            A.activation(s_t.rearrange("p j b -> p (j b)"), ps[:, 5, 0:SN], ACT.Sqrt).then_inc(SAMP["s_nrm"][0], 1)
            act.wait_ge(*SAMP["s_q"])
            A.activation(s_t2, s_t2, ACT.Sqrt).then_inc(SAMP["s_mult"][0], 1)
            A.activation(s_mu, pgs, ACT.Gelu_apprx_tanh).then_inc(SAMP["s_gelu"][0], 1)
            act.wait_ge(*SAMP["s_cent"])
            A.activation(s_t, s_y, ACT.Square).then_inc(SAMP["s_sqr"][0], 1)
            act.wait_ge(*SAMP["s_var"])
            A.activation(s_t1.rearrange("p j b -> p (j b)"), ps[:, 4, 0:SN], ACT.Sqrt, bias=eps[:, 1:2]).then_inc(SAMP["s_gsd"][0], 1)

            for i, (r0, rt) in enumerate(TILES):
                act.wait_ge(v1_ready, i + 1)
                A.activation(sd[0:rt], mv[0:rt, 1:2], ACT.Sqrt, bias=eps[0:rt, 0:1]).then_inc(v1_sd, 1)
                act.wait_ge(v2_ready, i + 1)
                A.activation(sd[0:rt], mv[0:rt, 1:2], ACT.Sqrt, bias=eps[0:rt, 0:1]).then_inc(v2_sd, 1)
            act.wait_ge(lg_ready, 1)
            A.activation(rt_a[0], rt_a[0], ACT.Exp).then_inc(ex_ready, 1)
            act.wait_ge(lg2_ready, 1)
            A.activation(rt_s[3], rt_s[3], ACT.Exp).then_inc(ex2_ready, 1)
            for n in range(6 * NEXP):
                wi = MCOLS[n % 3][1]
                act.wait_ge(gu_mm, n + 1)
                if n >= 2:
                    act.wait_ge(hid_out, n - 1)
                A.activation(sil[:, n % 2, 0:wi], ps[:, 2 * (n % 2), 0:wi], ACT.Silu).then_inc(silu_out, 1)
            for i, (r0, rt) in enumerate(TILES):
                act.wait_ge(v3_ready, i + 1)
                A.activation(sd[0:rt], mv[0:rt, 1:2], ACT.Sqrt, bias=eps[0:rt, 0:1]).then_inc(v3_sd, 1)

        @block.vector
        def _(dve):
            def link(ins):
                chain_v.on(ins)
                dve.wait_ge(chain_v.sem, chain_v.n)

            def done(ins, s_, n):
                ins.then_inc(s_, 1)
                dve.wait_ge(s_, n)

            TT, TS, STT = V.tensor_tensor, V.tensor_scalar, V.scalar_tensor_tensor

            dve.wait_ge(cond_tanh, 1)
            link(STT(out=csg, in0=csg, scalar=1.0, in1=cs, op0=ALU.add, op1=ALU.mult))
            done(TS(csg, csg, 0.5, None, ALU.mult), silu_ready, 1)
            dve.wait_ge(ld_const, 16 * 10)
            dve.wait_ge(consts_ready, 1)
            link(TS(bada[:, 8:24], bada[:, 8:24], 1.0, None, ALU.add))
            link(TS(bada[:, 32:48], bada[:, 32:48], 1.0, None, ALU.add))
            for d_, q_, m_ in ((D_W0, W0, 0.5), (D_A0, A0, 0.5), (D_RG, B_RG, 0.5), (D_IG, B_IG, 0.5)):
                link(TS(der[:, d_, :], par[:, q_, :], m_, None, ALU.mult))
            link(TS(der[:, D_OKA, :], par[:, K_A, :], -1.0, 1.0, ALU.mult, ALU.add))
            dve.wait_ge(lam_ln, 1)
            link(TS(der[:, D_ML, :], par[:, LAM, :], -1.0, 0.0, ALU.mult, ALU.max))
            link(TT(der[:, D_ML, :], der[:, D_ML, :], der[:, D_TMP, :], ALU.add))
            link(TS(der[:, D_ML, :], der[:, D_ML, :], 4.0, None, ALU.mult))
            done(TS(der[:, D_NML, :], der[:, D_ML, :], -1.0, None, ALU.mult), params_ready, 1)

            def moments(src, rt, s_, n):
                link(V.bn_stats(st[0:rt, 0, :], src[:, 0:512]))
                link(V.bn_stats(st[0:rt, 1, :], src[:, 512:1024]))
                done(V.bn_aggr(mv[0:rt], st[0:rt]), s_, n)

            def mod_rows(n):
                dve.wait_ge(mod_mm, n + 1)
                src = ps[:, n % 2, 0:32].rearrange("p (m b) -> p m b", m=2)[:, :, 0:9]
                TT(modT[:, 2 * n:2 * n + 2, :], src, bada[:, 2 * n:2 * n + 2].unsqueeze(2).to_broadcast([P, 2, 9]),
                   ALU.add).then_inc(mod_out, 1)

            for n in range(24):
                mod_rows(n)
            dve.wait_ge(mod_out, 24)

            def ht_tile(i):
                r0, rt = TILES[i]
                dve.wait_ge(xn_turned, i + 1)
                if i < 8:
                    for k in range(4):
                        last = TS(hT[:, k, r0:r0 + rt], ps[:, 2 + 2 * (i % 2), P * k:P * k + P],
                                  modT[:, 8 + k, 0:1], modT[:, k, 0:1], ALU.mult, ALU.add)
                else:
                    for b_ in range(2):
                        src = ps[:, 2 + 2 * (i % 2) + b_, :].rearrange("p (k t) -> p k t", k=4)[:, :, 0:DEC]
                        dst = hT[:, 4 * b_:4 * b_ + 4, SEQ:NTOK]
                        link(TT(dst, src, modT[:, 8 + 4 * b_:12 + 4 * b_, 1:9], ALU.mult))
                        last = TT(dst, dst, modT[:, 4 * b_:4 * b_ + 4, 1:9], ALU.add)
                last.then_inc(ht_dve, 1)

            for i, (r0, rt) in enumerate(TILES):
                dve.wait_ge(ld_x[i % 3], 16 * (i // 3 + 1))
                x_ = xr[i % 3][0:rt]
                moments(x_, rt, var_ready, i + 1)
                dve.wait_ge(sd_ready, i + 1)
                link(V.reciprocal(rs[0:rt], sd[0:rt]))
                if i >= 2:
                    dve.wait_ge(xn_turned, i - 1)
                done(TS(xn[i % 2][0:rt], x_, mv[0:rt, 0:1], rs[0:rt], ALU.subtract, ALU.mult), xn_ready, i + 1)
                if i:
                    ht_tile(i - 1)
            ht_tile(8)

            def shift(b_, o, n, mu, rows=P):
                link(TT(tmp[0:rows, 0:n], b_[:, o - 1:o - 1 + n], b_[:, o:o + n], ALU.subtract))
                return STT(out=b_[:, o:o + n], in0=tmp[0:rows, 0:n], scalar=mu, in1=b_[:, o:o + n],
                           op0=ALU.mult, op1=ALU.add)

            S0, S1 = PAD + SEQ, PAD + NTOK
            dve.wait_ge(win_out, 6)
            for b_, mu, rows in ((pwa, mu_wa, 64), (pgd, mu_gd, 96)):
                link(shift(b_, PAD + HALF, HALF, mu, rows))
                link(shift(b_, PAD, HALF, mu, rows))
                link(TT(tmp[0:rows, 0:DEC], b_[:, S1:S1 + DEC], b_[:, S0:S1], ALU.subtract))
                link(STT(out=b_[:, S0:S1], in0=tmp[0:rows, 0:DEC], scalar=mu, in1=b_[:, S0:S1], op0=ALU.mult,
                         op1=ALU.add))
            V.memset(rs, 0.0).then_inc(lora_shifted, 1)
            dve.wait_ge(lora_tanh, 2)
            done(TS(pgd[:, PAD:S1], pgd[:, PAD:S1], 0.5, 0.5, ALU.mult, ALU.add), lora_ready, 1)

            for j in range(NJ):
                dve.wait_ge(win_out, 6 + 15 * j + 9)
                for q, (b_, mu) in enumerate(((pk, MU_K), (pr, MU_R), (pv, MU_V))):
                    link(shift(b_, PAD + HALF, HALF, pcol(mu, j)))
                    link(shift(b_, PAD, HALF, pcol(mu, j)))
                    link(TT(tmp[:, 0:DEC], b_[:, S1:S1 + DEC], b_[:, S0:S1], ALU.subtract))
                    link(STT(out=psm[:, q, j, :], in0=tmp[:, 0:DEC], scalar=pcol(mu, j), in1=b_[:, S0:S1],
                             op0=ALU.mult, op1=ALU.add))
                dve.wait_ge(win_out, 6 + 15 * j + 15)
                link(V.tensor_copy(pxs[:, j, :], prec[:, S0:S1]))
                done(V.tensor_copy(pgs[:, j, :], pgate[:, S0:S1]), HV["shifted"], j + 1)
                V.memset(S[:, 0, :], 0.0).then_inc(s_zero, 1)
                for hf in range(2):
                    it = 2 * j + hf
                    n1 = it + 1
                    o = PAD + hf * HALF
                    cols = slice(o, o + HALF)
                    link(TS(xc, prec[:, o - 3:o - 3 + HALF], pcol(CW0, j), pcol(C_BIAS, j), ALU.mult, ALU.add))
                    for m in (1, 2):
                        link(STT(out=xc, in0=prec[:, o - 3 + m:o - 3 + m + HALF], scalar=pcol(CW0 + m, j), in1=xc,
                                 op0=ALU.mult, op1=ALU.add))
                    done(STT(out=xc, in0=prec[:, cols], scalar=pcol(CW3, j), in1=xc, op0=ALU.mult, op1=ALU.add),
                         HV["conv_ready"], n1)
                    dve.wait_ge(HV["ta_ready"], n1)
                    link(TS(lam, lam, -0.5 * DECAY, -0.5 * DECAY, ALU.mult, ALU.add))
                    link(TS(aa, aa, 0.5, 0.5, ALU.mult, ALU.add))
                    link(V.tensor_tensor_scan(cum, reset, lam, 0.0, ALU.mult, ALU.add))
                    done(TT(lam, cum, lam, ALU.subtract), HV["cum_ready"], n1)
                    dve.wait_ge(HV["nrm_ready"], n1)
                    link(TS(kk, kk, 1e-12, None, ALU.max))
                    link(V.reciprocal(kk, kk))
                    link(STT(out=kk, in0=pk[:, cols], scalar=pcol(K_K, j), in1=kk, op0=ALU.mult, op1=ALU.mult))
                    link(TS(tmp, aa, pcol(K_A, j), dcol(D_OKA, j), ALU.mult, ALU.add))
                    link(TT(k2, pk[:, cols], tmp, ALU.mult))
                    done(STT(out=rkp, in0=pr[:, cols], scalar=pcol(R_K, j), in1=k2, op0=ALU.mult, op1=ALU.mult),
                         HV["rkp_ready"], n1)
                    link(TT(bb, kk, aa, ALU.mult))
                    dve.wait_ge(HV["exp_ready"], n1)
                    link(STT(out=AR0, in0=kk, scalar=-1.0, in1=lam, op0=ALU.mult, op1=ALU.mult))
                    link(TT(AR1, pr[:, cols], eP, ALU.mult))
                    link(TT(bb, bb, eN, ALU.mult))
                    link(TT(k2, k2, eN, ALU.mult))
                    ends = eP.rearrange("p (c t) -> p c t", t=CHUNK)[:, :, CHUNK - 1:CHUNK].to_broadcast([P, HALF // CHUNK, CHUNK])
                    link(TT(Bh.rearrange("p (c t) -> p c t", t=CHUNK), bb.rearrange("p (c t) -> p c t", t=CHUNK), ends, ALU.mult))
                    done(TT(Kh.rearrange("p (c t) -> p c t", t=CHUNK), k2.rearrange("p (c t) -> p c t", t=CHUNK), ends, ALU.mult),
                         HV["prep_done"], n1)
                    dve.wait_ge(HV["bonus_mm"], n1)
                    done(TT(rkp, ps[:, 7, :], pv[:, cols], ALU.mult), HV["bonus_out"], n1)
                    dve.wait_ge(HV["lru_exp"], n1)
                    link(TS(ti, ti, 0.5, 0.5, ALU.mult, ALU.add))
                    link(TT(ti, ti, xc, ALU.mult))
                    link(TS(hs, t2, 1.0, None, ALU.add))
                    link(V.reciprocal(hs, hs))
                    done(STT(out=t2, in0=t2, scalar=2.0, in1=hs, op0=ALU.mult, op1=ALU.mult), HV["q_ready"], n1)
                    dve.wait_ge(HV["lru_mult"], n1)
                    link(TT(ti, ti, t2, ALU.mult))
                    link(V.tensor_tensor_scan(hs, tr, ti, lru_last[:, j, 0:1] if hf else 0.0, ALU.mult, ALU.add))
                    link(V.tensor_copy(lru_last[:, j, 0:1], hs[:, HALF - 1:HALF]))
                    dve.wait_ge(HV["gelu_ready"], n1)
                    link(TT(yT[:, NJ + j, HALF * hf:HALF * hf + HALF], hs, pgate[:, cols], ALU.mult))

                    def banks2(g, b_, w):
                        return ps[:, 4 * g + b_:4 * g + b_ + 2, 0:w]

                    def four(m):
                        return m.unsqueeze(1).to_broadcast([P, 4, P])

                    def v4(ap):
                        return ap.rearrange("p h a t -> p (h a) t")

                    for g in range(2):
                        q = grp[g]
                        gi = 2 * it + g + 1
                        dve.wait_ge(HV["gram_b"], gi)
                        done(TT(q.dtg.rearrange("p h a w t -> p (h a) (w t)"),
                                banks2(g, 0, 512).rearrange("p b (a x) -> p (b a) x", a=2),
                                mask_dt.rearrange("p w t -> p (w t)").unsqueeze(1).to_broadcast([P, 4, 256]), ALU.mult),
                             HV["dt_out"], gi)
                    for g in range(2):
                        q = grp[g]
                        gi = 2 * it + g + 1
                        dve.wait_ge(HV["gram_k"], gi)
                        done(TT(q.ak.rearrange("p h a w t -> p (h a) (w t)"),
                                banks2(g, 2, 512).rearrange("p b (a x) -> p (b a) x", a=2),
                                mask_ak.rearrange("p w t -> p (w t)").unsqueeze(1).to_broadcast([P, 4, 256]), ALU.mult),
                             HV["ak_out"], gi)
                        done(TT(v4(q.p), q.dtg[:, :, :, 0, :].rearrange("p h a t -> p (h a) t"), four(ident), ALU.add),
                             HV["p1_out"], gi)
                    for g in range(2):
                        q = grp[g]
                        gi = 2 * it + g + 1
                        dve.wait_ge(HV["gram_l"], gi)
                        src = banks2(g, 0, 256).rearrange("p b (a t) -> p b a t", a=2)
                        m4 = [m.unsqueeze(1).unsqueeze(1).to_broadcast([P, 2, 2, P]) for m in (mask_d, mask_e)]
                        link(TT(q.d, src, m4[0], ALU.mult))
                        done(TT(q.e, src, m4[1], ALU.mult), HV["de_out"], gi)
                    for mm_, out_, b_ in (("p2_mm", "p2_out", 2), ("p3_mm", "p3_out", 2), ("p4_mm", "nt_out", 2)):
                        for g in range(2):
                            gi = 2 * it + g + 1
                            dve.wait_ge(HV[mm_], gi)
                            done(TT(grp[g].p_flat, grp[g].p_flat, grp[g].bank(b_), ALU.add), HV[out_], gi)
                    for g in range(2):
                        gi = 2 * it + g + 1
                        dve.wait_ge(HV["f_mm"], gi)
                        done(V.tensor_copy(grp[g].z_flat, grp[g].bank(2)), HV["z0_out"], gi)
                    for mm_, out_, b_ in (("z1_mm", "z1_out", 2), ("z2_mm", "z2_out", 1)):
                        for g in range(2):
                            gi = 2 * it + g + 1
                            dve.wait_ge(HV[mm_], gi)
                            done(TT(grp[g].z_flat, grp[g].z_flat, grp[g].bank(b_), ALU.add), HV[out_], gi)
                    for g in range(2):
                        q = grp[g]
                        gi = 2 * it + g + 1
                        dve.wait_ge(HV["rt_mm"], gi)
                        done(TT(q.rh, AR1[:, q.c0:q.c0 + GRP], q.bank(0)[:, 0:GRP], ALU.add), HV["rh_out"], gi)
                        link(TT(q.tt, banks2(g, 2, 256).rearrange("p c (a t) -> p c a t", a=2),
                                blk_ones.unsqueeze(1).unsqueeze(1).to_broadcast([P, 2, 2, P]), ALU.mult))
                        for n in range(4):
                            t_ = q.tt[:, n % 2, n // 2, :]
                            end = q.c0 + CHUNK * n + CHUNK - 1
                            last = STT(out=t_, in0=ident, scalar=eP[:, end:end + 1], in1=t_, op0=ALU.mult, op1=ALU.add)
                        done(last, HV["tt_out"], gi)
                    for g in range(2):
                        q = grp[g]
                        for n in range(4):
                            cur = 4 * (2 * it + g) + n + 1
                            dve.wait_ge(state_mm, cur)
                            done(TT(S[:, (n + 1) % 2, :], q.bank(2 + n % 2)[:, 256:384], blk_ones, ALU.mult),
                                 state_out, cur)
                    dve.wait_ge(HV["mean_mm"], n1)
                    done(TT(Y, Y, ps[:, 0, :], ALU.subtract), HV["centred"], n1)
                    dve.wait_ge(HV["gsd_ready"], n1)
                    link(V.reciprocal(eP, eP))
                    link(TT(Y, Y, eP, ALU.mult))
                    link(TS(Y, Y, pcol(LNX_G, j), pcol(LNX_B, j), ALU.mult, ALU.add))
                    link(TT(Y, Y, rkp, ALU.add))
                    dve.wait_ge(HV["g_ready"], n1)
                    if hf:
                        link(V.tensor_copy(sfin[:, j, :], S[:, 0, :]))
                    done(TT(yT[:, j, HALF * hf:HALF * hf + HALF], Y, gg, ALU.mult), HV["half_done"], n1)

            def pb(q):
                return par[:, q, :].unsqueeze(2).to_broadcast([P, NJ, DEC])

            dve.wait_ge(ld_samp, 16 * 3)
            link(TT(s_xc, s_conv[:, :, 0, :], pb(CW0), ALU.mult))
            for m in (1, 2, 3):
                link(TT(s_kk, s_conv[:, :, m, :] if m < 3 else pxs, pb(CW0 + m), ALU.mult))
                link(TT(s_xc, s_xc, s_kk, ALU.add))
            done(TT(s_xc, s_xc, pb(C_BIAS), ALU.add), *SAMP["s_conv"])
            k_, r_, v_ = psm[:, 0], psm[:, 1], psm[:, 2]
            link(TT(s_kk, k_, pb(K_K), ALU.mult))
            done(TT(s_t, s_kk, s_kk, ALU.mult), *SAMP["s_sq"])
            dve.wait_ge(*SAMP["s_wa"])
            link(TS(s_lam, s_lam, -0.5 * DECAY, -0.5 * DECAY, ALU.mult, ALU.add))
            done(TS(s_a, s_a, 0.5, 0.5, ALU.mult, ALU.add), *SAMP["s_lam"])
            dve.wait_ge(*SAMP["s_nrm"])
            link(TS(s_t, s_t, 1e-12, None, ALU.max))
            link(V.reciprocal(s_t, s_t))
            link(TT(s_kk, s_kk, s_t, ALU.mult))
            link(TT(s_t, s_a, pb(K_A), ALU.mult))
            link(TT(s_t, s_t, der[:, D_OKA, :].unsqueeze(2).to_broadcast([P, NJ, DEC]), ALU.add))
            link(TT(s_vecs[:, 2], k_, s_t, ALU.mult))
            link(TT(s_t1, r_, pb(R_K), ALU.mult))
            done(TT(s_t1, s_t1, s_vecs[:, 2], ALU.mult), *SAMP["s_bon"])
            V.tensor_copy(s_vecs[:, 0], r_)
            V.tensor_copy(s_vecs[:, 3], v_)
            TS(s_vecs[:, 4], s_kk, -1.0, None, ALU.mult)
            dve.wait_ge(*SAMP["s_w"])
            TT(s_vecs[:, 5], s_kk, s_a, ALU.mult).then_inc(SAMP["s_vec"][0], 1)
            dve.wait_ge(*SAMP["s_lexp"])
            link(TS(s_ti, s_ti, 0.5, 0.5, ALU.mult, ALU.add))
            link(TT(s_ti, s_ti, s_xc, ALU.mult))
            link(TS(s_gl, s_t2, 1.0, None, ALU.add))
            link(V.reciprocal(s_gl, s_gl))
            done(STT(out=s_t2, in0=s_t2, scalar=2.0, in1=s_gl, op0=ALU.mult, op1=ALU.mult), *SAMP["s_q"])
            dve.wait_ge(*SAMP["s_mult"])
            link(TT(s_ti, s_ti, s_t2, ALU.mult))
            link(TT(s_hs, s_tr, s_lru0, ALU.mult))
            link(TT(s_hs, s_hs, s_ti, ALU.add))
            link(V.tensor_copy(lru_last[:, :, 1:9], s_hs))
            dve.wait_ge(*SAMP["s_gelu"])
            link(TT(yT[:, NJ:2 * NJ, SEQ:NTOK], s_hs, s_mu, ALU.mult))
            dve.wait_ge(*SAMP["s_turn"])
            link(V.tensor_copy(s_qt[:, 0:512], ps[0:32, 0, :]))
            done(V.tensor_copy(s_qt[:, 512:768], ps[0:32, 1, 0:256]), *SAMP["s_vrow"])
            dve.wait_ge(*SAMP["s_bonmm"])
            link(TT(s_bon, ps[:, 6, 0:SN].rearrange("p (j b) -> p j b", j=NJ), v_, ALU.mult))
            dve.wait_ge(HV["s_rows"], 16 * 6)

            def krow(n):
                return s_row[:, n, :].unsqueeze(1).to_broadcast([P, 32, HEAD])

            def vrow(x_):
                return x_.unsqueeze(2).to_broadcast([P, 32, HEAD])

            link(TT(s_T, s_S, krow(3), ALU.mult))
            link(V.tensor_reduce(s_sa, s_T, AX_X, ALU.add))
            link(TT(s_S, s_S, krow(1), ALU.mult))
            link(TT(s_T, vrow(s_sa), krow(4), ALU.mult))
            link(TT(s_S, s_S, s_T, ALU.add))
            link(TT(s_T, vrow(s_vr), krow(2), ALU.mult))
            link(TT(s_S, s_S, s_T, ALU.add))
            link(TT(s_T, s_S, krow(0), ALU.mult))
            done(V.tensor_reduce(s_yr, s_T, AX_X, ALU.add), *SAMP["s_y"])
            dve.wait_ge(*SAMP["s_yturn"])
            done(V.tensor_copy(s_y.rearrange("p j b -> p (j b)"), ps[:, 2, 0:SN]), *SAMP["s_yc"])
            dve.wait_ge(*SAMP["s_mean"])
            done(TT(s_y, s_y, ps[:, 3, 0:SN].rearrange("p (j b) -> p j b", j=NJ), ALU.subtract), *SAMP["s_cent"])
            dve.wait_ge(*SAMP["s_gsd"])
            link(V.reciprocal(s_t1, s_t1))
            link(TT(s_y, s_y, s_t1, ALU.mult))
            link(TT(s_y, s_y, pb(LNX_G), ALU.mult))
            link(TT(s_y, s_y, pb(LNX_B), ALU.add))
            link(TT(s_y, s_y, s_bon, ALU.add))
            done(TT(yT[:, 0:NJ, SEQ:NTOK], s_y, s_g, ALU.mult), *SAMP["s_done"])

            dve.wait_ge(outs, 16 * 9)
            for k in range(2 * KC):
                if k >= 8:
                    dve.wait_ge(row_mm, k - 7)
                done(TS(diag[:, k % 8, :], ident, modT[:, (16 if k < 8 else 40) + k % 8, 0:1], None, ALU.mult),
                     row_diag, k + 1)
                if k >= 1:
                    rows_out = k - 1
                    dve.wait_ge(row_mm, k)
                    gb, gs = (g1b, g1s) if rows_out < 8 else (g2b, g2s)
                    c_ = slice(P * (rows_out % 8), P * (rows_out % 8) + P)
                    V.tensor_copy(gb[:, c_], ps[:, 5 + rows_out % 2, 0:P])
                    V.tensor_copy(gs[0:DEC, c_], ps[0:DEC, 5 + rows_out % 2, P:2 * P]).then_inc(row_out, 1)
            dve.wait_ge(row_mm, 16)
            V.tensor_copy(g2b[:, 896:1024], ps[:, 6, 0:P])
            done(V.tensor_copy(g2s[0:DEC, 896:1024], ps[0:DEC, 6, P:2 * P]), row_out, 16)

            def norm(dst, src, rt, s_sd, n):
                dve.wait_ge(s_sd, n)
                link(V.reciprocal(rs[0:rt], sd[0:rt]))
                return TS(dst, src, mv[0:rt, 0:1], rs[0:rt], ALU.subtract, ALU.mult)

            def h2_tile(i):
                r0, rt = TILES[i]
                dve.wait_ge(n2_turned, i + 1)
                if i < 8:
                    for k in range(8):
                        last = TS(h2T[:, k, r0:r0 + rt], ps[:, 4 + k // 4, P * (k % 4):P * (k % 4) + P],
                                  modT[:, 32 + k, 0:1], modT[:, 24 + k, 0:1], ALU.mult, ALU.add)
                else:
                    for b_ in range(2):
                        src = ps[:, 4 + b_, :].rearrange("p (k t) -> p k t", k=4)[:, :, 0:DEC]
                        dst = h2T[:, 4 * b_:4 * b_ + 4, SEQ:NTOK]
                        link(TT(dst, src, modT[:, 32 + 4 * b_:36 + 4 * b_, 1:9], ALU.mult))
                        last = TT(dst, dst, modT[:, 24 + 4 * b_:28 + 4 * b_, 1:9], ALU.add)
                last.then_inc(h2_out, 1)

            dve.wait_ge(ld_late, 16 * 6)
            for i, (r0, rt) in enumerate(TILES):
                gb = g1b if i < 8 else g1s
                dve.wait_ge(wo_mm, 2 * i + 2)
                z_ = zz[0:rt]
                done(TT(z_, ps[0:rt, 2 * (i % 2):2 * (i % 2) + 2, :].rearrange("p b x -> p (b x)"), gb[0:rt], ALU.mult),
                     wo_out, i + 1)
                dve.wait_ge(ld_x2[i % 2], 16 * (i // 2 + 1))
                link(STT(out=z_, in0=xr2[0:rt, i % 2, :], scalar=ALPHA, in1=z_, op0=ALU.mult, op1=ALU.add))
                moments(z_, rt, v1_ready, i + 1)
                x_ = x1[0:rt, i, :]
                link(norm(x_, z_, rt, v1_sd, i + 1))
                link(TT(x_, x_, lnr[0:rt, 0, :], ALU.mult))
                link(TT(x_, x_, lnr[0:rt, 1, :], ALU.add))
                moments(x_, rt, v2_ready, i + 1)
                if i >= 2:
                    dve.wait_ge(n2_turned, i - 1)
                done(norm(n2[0:rt, i % 2, :], x_, rt, v2_sd, i + 1), n2_ready, i + 1)
                if i:
                    h2_tile(i - 1)
            h2_tile(8)

            link(V.memset(lgt, 0.0))
            dve.wait_ge(router_mm, 1)
            for i, (r0, rt) in enumerate(TILES):
                link(TT(lgt[0:rt, i, :], ps[0:rt, 6, 20 * i:20 * i + 20], brt[0:rt], ALU.add))

            def b4(x_):
                return x_.unsqueeze(2).to_broadcast([P, 9, 4])

            def first_of_max(o_, eq, left):
                link(V.memset(left, 1.0))
                for m in range(4):
                    link(TT(o_[:, :, m], eq[:, :, m], left, ALU.mult))
                    link(TT(left, left, o_[:, :, m], ALU.subtract))

            gl = lgt[:, :, 0:4]
            e_, oh, el, f1, f2, t4, c4, eq = rt_a
            gmax, gsum, em, ee, left, w1, w2, pg = rt_s
            link(V.tensor_reduce(gmax, gl, AX_X, ALU.max))
            done(TT(e_, gl, b4(gmax), ALU.subtract), lg_ready, 1)
            link(TT(eq, gl, b4(gmax), ALU.is_equal))
            first_of_max(oh, eq, left)
            dve.wait_ge(ex_ready, 1)
            link(V.tensor_reduce(gsum, e_, AX_X, ALU.add))
            link(V.reciprocal(pg, gsum))
            for m in range(4):
                src = lgt[:, :, 4 + 4 * m:8 + 4 * m]
                om = b4(oh[:, :, m])
                if m == 0:
                    link(TT(el, src, om, ALU.mult))
                else:
                    link(TT(t4, src, om, ALU.mult))
                    link(TT(el, el, t4, ALU.add))
            link(V.tensor_reduce(em, el, AX_X, ALU.max))
            link(TT(eq, el, b4(em), ALU.is_equal))
            first_of_max(f1, eq, left)
            link(TS(t4, f1, -1e30, None, ALU.mult))
            link(TT(el, el, t4, ALU.add))
            link(V.tensor_reduce(w1, el, AX_X, ALU.max))
            link(TT(eq, el, b4(w1), ALU.is_equal))
            first_of_max(f2, eq, left)
            done(TT(ee, w1, em, ALU.subtract), lg2_ready, 1)
            dve.wait_ge(ex2_ready, 1)
            link(TS(w1, ee, 1.0, None, ALU.add))
            link(V.reciprocal(w1, w1))
            link(TT(w1, w1, pg, ALU.mult))
            link(TT(w2, w1, ee, ALU.mult))
            link(TT(c4, f1, b4(w1), ALU.mult))
            link(TT(t4, f2, b4(w2), ALU.mult))
            link(TT(c4, c4, t4, ALU.add))
            for m in range(4):
                link(TT(comb[:, :, 4 * m:4 * m + 4], c4, b4(oh[:, :, m]), ALU.mult))

            for e in range(NEXP):
                for f in range(2):
                    for c, (c0, wi) in enumerate(MCOLS):
                        n = 6 * e + 3 * f + c
                        if n % 6 == 0 and e:
                            dve.wait_ge(dn_mm, 18 * e)
                        dve.wait_ge(silu_out, n + 1)
                        done(TT(hid[:, f, c0:c0 + wi], sil[:, n % 2, 0:wi], ps[:, 2 * (n % 2) + 1, 0:wi], ALU.mult),
                             hid_out, n + 1)
                for i, (r0, rt) in enumerate(TILES):
                    for n in range(2):
                        m = 18 * e + 2 * i + n
                        dve.wait_ge(dn_mm, m + 1)
                        a_ = acc[0:rt, i, 512 * n:512 * n + 512]
                        src = ps[0:rt, 4 + m % 4, :]
                        cw = comb[0:rt, i, e:e + 1]
                        if e == 0:
                            done(TS(a_, src, cw, None, ALU.mult), dn_out, m + 1)
                        else:
                            done(STT(out=a_, in0=src, scalar=cw, in1=a_, op0=ALU.mult, op1=ALU.add), dn_out, m + 1)
            for i, (r0, rt) in enumerate(TILES):
                gb = g2b if i < 8 else g2s
                z_ = fz[0:rt, i % 2, :]
                if i >= 2:
                    dve.wait_ge(y_stored[i % 2], 16 * (i // 2))
                link(TT(z_, acc[0:rt, i, :], gb[0:rt], ALU.mult))
                link(STT(out=z_, in0=x1[0:rt, i, :], scalar=ALPHA, in1=z_, op0=ALU.mult, op1=ALU.add))
                moments(z_, rt, v3_ready, i + 1)
                link(norm(z_, z_, rt, v3_sd, i + 1))
                link(TT(z_, z_, lnr[0:rt, 2, :], ALU.mult))
                done(TT(z_, z_, lnr[0:rt, 3, :], ALU.add), y_ready, i + 1)


def kernel(x_prompt, x_sample, c_prompt, c_sample, state_wkv, state_shift, state_conv, state_lru,
           w_ada, b_ada, w_in, mu_shift, w0, w_decay_up, a0, w_a_up, w_g_up, k_k, k_a, r_k,
           lnx_gain, lnx_bias, conv_w, conv_b, w_rgate, b_rgate, w_igate, b_igate, lru_lambda,
           w_out, ln1_gain, ln1_bias, w_router_group, b_router_group, w_router_expert,
           b_router_expert, w_exp_gate, w_exp_up, w_exp_down, ln2_gain, ln2_bias):
    import concourse.bacc as _bacc
    from concourse.bass_utils import run_bass_kernel_spmd as _run

    def tiles(v):
        return np.asarray(v).reshape(-1, P).T

    def rows(w):
        w = np.asarray(w)
        return w.reshape(KC, P, -1).transpose(1, 0, 2)

    x = np.concatenate([np.asarray(x_prompt)[0], np.asarray(x_sample)[:, 0]], 0)
    c = np.concatenate([np.asarray(c_prompt), np.asarray(c_sample)], 0)
    wi = np.asarray(w_in)[0]
    ca = 512
    sh = 3 * ca + 160
    at = {"k": ca, "r": 0, "v": 2 * ca, "rec": sh + ca, "gate": sh}
    mu = np.asarray(mu_shift)[0]
    st = np.asarray(state_wkv)[0].reshape(DEC, NJ, 2, HEAD, HEAD)
    d = {
        "x_all": x,
        "c_t": c.reshape(9, KC, P).transpose(2, 1, 0),
        "shift_t": np.asarray(state_shift)[0].reshape(DEC, KC, P).transpose(2, 1, 0),
        "wkv0": st.transpose(1, 0, 2, 3, 4).reshape(P, 2048),
        "conv0": np.asarray(state_conv)[0].reshape(DEC, 3, NJ, P).transpose(3, 2, 1, 0),
        "lru0": np.asarray(state_lru)[0].reshape(DEC, NJ, P).transpose(2, 1, 0),
        "state_conv": np.asarray(state_conv)[0],
        "w_ada": np.asarray(w_ada)[0].reshape(KC, P, 24, 256).transpose(2, 1, 0, 3).reshape(24, P, 2048),
        "b_ada": tiles(b_ada[0]),
        "w_in": np.stack([rows(wi[:, at[q] + P * j:at[q] + P * j + P]).reshape(P, KC * P)
                          for j in range(NJ) for q in ("k", "r", "v", "rec", "gate")]),
        "w_lo": rows(wi[:, 3 * ca:sh]).reshape(P, KC * 160),
        "prm": np.stack([tiles(v) for v in (
            mu[0:ca], mu[ca:2 * ca], mu[2 * ca:3 * ca], w0[0], a0[0], k_k[0], k_a[0], np.asarray(r_k)[0].reshape(-1),
            lnx_gain[0], lnx_bias[0], conv_w[0][0], conv_w[0][1], conv_w[0][2], conv_w[0][3], conv_b[0],
            b_rgate[0], b_igate[0], lru_lambda[0])], 1),
        "mu_lo": mu[3 * ca:].reshape(160, 1),
        "w_wa_up": np.concatenate([np.asarray(w_decay_up)[0], np.asarray(w_a_up)[0]], 0),
        "w_g_up": np.asarray(w_g_up)[0],
        "w_rg": np.asarray(w_rgate)[0].reshape(NJ, P, HEAD),
        "w_ig": np.asarray(w_igate)[0].reshape(NJ, P, HEAD),
        "w_out": np.asarray(w_out)[0].reshape(KC, P, D_MODEL),
        "ln_rows": np.stack([np.asarray(v)[0] for v in (ln1_gain, ln1_bias, ln2_gain, ln2_bias)]),
        "w_rt": rows(np.concatenate([np.asarray(w_router_group)[0], np.asarray(w_router_expert)[0]], 1)),
        "b_rt": np.concatenate([np.asarray(b_router_group)[0], np.asarray(b_router_expert)[0]]).reshape(1, 20),
        "w_gu": np.stack([np.asarray(w_exp_gate)[0], np.asarray(w_exp_up)[0]], 1)
                  .reshape(NEXP, 2, KC, P, DEXP).transpose(0, 3, 1, 2, 4).reshape(NEXP, P, 4096),
        "w_dn": np.asarray(w_exp_down)[0].reshape(NEXP, 2, P, D_MODEL).transpose(0, 2, 1, 3).reshape(NEXP, P, 2048),
    }
    outs = {"y_all": (NTOK, D_MODEL), "wkvp_o": (NJ, P, P), "wkvs_o": (P, 2048), "shift_o": (P, KC, 9),
            "conv_o": (NJ, P, 11), "convs_o": (DEC, 2, 512), "lru_o": (P, NJ, 9)}
    nc = _bacc.Bacc("TRN2", target_bir_lowering=False, num_devices=1)
    arrays, args = {}, {}
    for name, a in d.items():
        a = np.ascontiguousarray(a)
        arrays[f"in_{name}"] = a
        args[name] = nc.dram_tensor(f"in_{name}", a.shape, mybir.dt.from_np(a.dtype), kind="ExternalInput").ap()
    for name, shape in outs.items():
        args[name] = nc.dram_tensor(f"out_{name}", shape, F32, kind="ExternalOutput").ap()
    build(nc, **args)
    r = _run(nc, [arrays], core_ids=[0]).results[0]
    o = {name: r[f"out_{name}"] for name in outs}
    y = o["y_all"]
    sb_ = o["wkvp_o"].reshape(NJ, 2, HEAD, 2, HEAD)
    wkv_p = np.stack([sb_[:, q, :, q, :] for q in range(2)], 1).transpose(0, 1, 3, 2).reshape(1, 1, 8, HEAD, HEAD)
    wkv_s = o["wkvs_o"].reshape(NJ, DEC, 2, HEAD, HEAD).transpose(1, 0, 2, 3, 4).reshape(1, DEC, 8, HEAD, HEAD)
    shf = o["shift_o"].transpose(2, 1, 0).reshape(9, D_MODEL)
    cv = o["conv_o"].transpose(2, 0, 1).reshape(11, 512)
    conv_s = np.concatenate([o["convs_o"], cv[3:, None, :]], 1)
    lr = o["lru_o"].transpose(2, 1, 0).reshape(9, 512)
    cc = np.ascontiguousarray
    return (cc(y[None, :SEQ]), cc(y[SEQ:, None]), cc(wkv_p), cc(shf[None, 0:1]), cc(cv[None, None, 0:3]),
            cc(lr[None, 0:1]), cc(wkv_s), cc(shf[None, 1:]), cc(conv_s[None]), cc(lr[None, 1:]))
```

```python
from contextlib import ExitStack

import numpy as np
import concourse.bass as bass
from concourse import mybir

ALU = mybir.AluOpType
ACT = mybir.ActivationFunctionType
F32 = mybir.dt.float32
I32 = mybir.dt.int32
U32 = mybir.dt.uint32
AX_X = mybir.AxisListType.X

P = 128
D_MODEL = 1024
KC = D_MODEL // P
SEQ = 1024
DEC = 8
NTOK = SEQ + DEC
NCOL = NTOK + DEC
NJ = 4
HEAD = 64
CHUNK = 64
HALF = 512
GRP = 256
PAD = 3
NEXP = 16
DEXP = 256
ALPHA = 2 ** 0.25
DECAY = float(np.exp(-0.5))
LN_EPS = 1e-5
GN_EPS = 64e-5
COLS = [(0, 348), (348, 348), (696, 344)]
MOD0 = 8
STEPS = 32
TILES = [(i * P, P) for i in range(SEQ // P)] + [(SEQ, DEC)]
(MU_R, MU_K, MU_V, W0, A0, K_K, K_A, R_K, LNX_G, LNX_B, CW0, CW1, CW2, CW3, C_BIAS, B_RG, B_IG,
 LAM) = range(18)
NPRM = 18
ARENA = 53000


class Signal:

    def __init__(self, ctx, nc, name):
        self.sem = ctx.enter_context(nc.semaphore(name))
        self.n = 0

    def on(self, ins, k=1):
        ins.then_inc(self.sem, k)
        self.n += k


def build(nc, x_all, c_t, shift_t, wkv0, conv0, lru0, state_conv, w_ada, b_ada, w_in, w_lo, prm, mu_lo,
          w_wa_up, w_g_up, w_rg, w_ig, w_out, ln_rows, w_rt, b_rt, w_gu, w_dn,
          y_all, wkvp_o, wkvs_o, shift_o, conv_o, convs_o, lru_o):
    q_scr = nc.dram_tensor("q_scr", (6, 32, P), F32, kind="Internal").ap()
    y_scr = nc.dram_tensor("y_scr", (32, P), F32, kind="Internal").ap()
    h2_scr = nc.dram_tensor("h2_scr", (NTOK, D_MODEL), F32, kind="Internal").ap()
    slot_scr = nc.dram_tensor("slot_scr", (STEPS * P, D_MODEL), F32, kind="Internal").ap()

    with ExitStack() as ctx:
        def sb(name, shape, stack=ctx):
            return stack.enter_context(nc.sbuf_tensor(name, shape, F32))

        def sem(name):
            return ctx.enter_context(nc.semaphore(name))

        ps = ctx.enter_context(nc.psum_tensor("ps", [P, 8, 512], F32))

        arena = ctx.enter_context(nc.sbuf_tensor("arena", [P, ARENA], F32))
        at = [0]

        def take(n):
            at[0] += n
            assert at[0] <= ARENA
            return arena[:, at[0] - n:at[0]]

        def v3(ap, a):
            return ap.rearrange("p (a b) -> p a b", a=a)

        hT = v3(take(KC * NCOL), KC)
        yT_at = at[0]
        yT = v3(take(KC * NTOK), KC)
        modT = v3(take(48 * 9), 48)
        ident = take(P)
        blk_ones = take(P)
        blk_mean = take(P)
        ones = take(P)
        mask_dt = v3(take(2 * P), 2)
        mask_ak = v3(take(2 * P), 2)
        mask_d = take(P)
        mask_e = take(P)
        before = take(P)
        iota_p = take(P)
        iota_s = take(STEPS)
        iota_t = take(STEPS + 1)
        tok_id = take(9)
        valid = take(9)
        par = v3(take(NPRM * NJ), NPRM)
        der = v3(take(12 * NJ), 12)
        mu_wa = take(1)[0:64]
        mu_gd = take(1)[0:96]
        bada = take(48)
        eps = take(2)
        S = v3(take(2 * P), 2)
        sfin = v3(take(NJ * P), NJ)
        lru_last = v3(take(NJ * 9), NJ)
        st = v3(take(12), 2)
        mv = take(2)
        sd = take(1)
        rs = take(1)
        psm = take(3 * NJ * DEC).rearrange("p (q j b) -> p q j b", q=3, j=NJ)
        pgs = v3(take(NJ * DEC), NJ)
        pxs = v3(take(NJ * DEC), NJ)
        base = at[0]

        ld_const = sem("ld_const")
        ld_cs = sem("ld_cs")
        ld_prev = sem("ld_prev")
        ld_samp = sem("ld_samp")
        ld_ada = [sem(f"ld_ada{i}") for i in range(2)]
        ld_x = [sem(f"ld_x{i}") for i in range(3)]
        ld_win = [sem(f"ld_win{i}") for i in range(3)]
        ld_lo = sem("ld_lo")
        consts_ready = sem("consts_ready")
        silu_ready = sem("silu_ready")
        cond_tanh = sem("cond_tanh")
        mod_mm = sem("mod_mm")
        mod_out = sem("mod_out")
        var_ready = sem("var_ready")
        sd_ready = sem("sd_ready")
        xn_ready = sem("xn_ready")
        xn_turned = sem("xn_turned")
        ht_dve = sem("ht_dve")
        ht_act = sem("ht_act")
        params_ready = sem("params_ready")
        lam_ln = sem("lam_ln")
        win_mm = sem("win_mm")
        win_out = sem("win_out")
        lora_shifted = sem("lora_shifted")
        lora_tanh = sem("lora_tanh")
        lora_ready = sem("lora_ready")
        outs = sem("outs")

        def names(*ns):
            return {n: sem(n) for n in ns}

        h = names("up_mm", "gate_mm", "norm_mm", "bonus_mm", "mean_mm", "var_mm",
                  "ta_ready", "g_ready", "sq_ready", "nrm_ready", "exp_ready", "gates_tanh",
                  "lru_exp", "lru_mult", "gelu_ready", "conv_ready", "cum_ready", "q_ready",
                  "rkp_ready", "prep_done", "shifted", "bonus_out", "centred", "ysq_ready", "gsd_ready", "half_done")
        g_ = names("gram_b", "gram_k", "gram_l", "turned", "akv_mm", "d2_mm", "p2_mm", "p3_mm", "p4_mm",
                   "f_mm", "z1_mm", "z2_mm", "rt_mm",
                   "dt_out", "ak_out", "de_out", "tok_out", "akv_out", "d2_out", "d4_out", "d8_out",
                   "p1_out", "p2_out", "p3_out", "nt_out", "f_out", "z0_out", "f2_out", "z1_out",
                   "z2_out", "rh_out", "tt_out", "y_out")
        state_mm = sem("state_mm")
        state_out = sem("state_out")
        s_zero = sem("s_zero")
        SAMP = {}
        for who, steps in (("pe", ("s_up", "s_gates", "s_norm", "s_bonmm", "s_turn", "s_yturn", "s_mean", "s_var")),
                           ("act", ("s_wa", "s_lexp", "s_w", "s_nrm", "s_mult", "s_gelu", "s_sqr", "s_gsd")),
                           ("dve", ("s_conv", "s_sq", "s_lam", "s_bon", "s_vec", "s_q", "s_vrow", "s_y", "s_yc",
                                    "s_cent", "s_done"))):
            steps_done = sem(f"sample_steps_{who}")
            SAMP.update({n: (steps_done, i + 1) for i, n in enumerate(steps)})
        samp = names("s_stored", "s_rows", "s_ystored", "s_yrow")
        ld_late = sem("ld_late")
        ld_wout = sem("ld_wout")
        ld_x2 = [sem(f"ld_x2{i}") for i in range(2)]
        row_diag = sem("row_diag")
        row_mm = sem("row_mm")
        row_out = sem("row_out")
        wo_mm = sem("wo_mm")
        wo_out = sem("wo_out")
        n2_ready = sem("n2_ready")
        h2_ready = sem("h2_ready")
        h2_stored = [sem(f"h2_stored{i}") for i in range(2)]
        h2_turned = sem("h2_turned")
        h2t_out = sem("h2t_out")
        router_mm = sem("router_mm")
        lg_ready = sem("lg_ready")
        ex_ready = sem("ex_ready")
        lg2_ready = sem("lg2_ready")
        ex2_ready = sem("ex2_ready")
        assigned = sem("assigned")
        rank_mm = sem("rank_mm")
        hot_ready = sem("hot_ready")
        hot_used = sem("hot_used")
        route_ready = sem("route_ready")
        ld_gu = [sem(f"ld_gu{i}") for i in range(2)]
        ld_dn = [sem(f"ld_dn{i}") for i in range(2)]
        ld_xg = [sem(f"ld_xg{i}") for i in range(2)]
        xg_turned = sem("xg_turned")
        xgt_out = sem("xgt_out")
        gu_mm = sem("gu_mm")
        silu_out = sem("silu_out")
        hid_out = sem("hid_out")
        hid_turned = sem("hid_turned")
        hidt_out = sem("hidt_out")
        dn_mm = sem("dn_mm")
        ys_out = sem("ys_out")
        slot_stored = [sem(f"slot_stored{i}") for i in range(2)]
        ld_yg = [sem(f"ld_yg{i}") for i in range(2)]
        yg_used = sem("yg_used")
        y_ready = sem("y_ready")
        y_stored = [sem(f"y_stored{i}") for i in range(2)]
        chain_v = Signal(ctx, nc, "chain_v")
        chain_a = Signal(ctx, nc, "chain_a")
        chain_p = Signal(ctx, nc, "chain_p")

        pk, pr, pv, prec, pgate = (take(PAD + NCOL) for _ in range(5))
        pwa = take(PAD + NCOL)[0:64]
        pgd = take(PAD + NCOL)[0:96]
        win = v3(take(3 * KC * P), 3)
        wa_up = take(512)[0:64]
        g_up = take(512)[0:96]
        rg = v3(take(NJ * P), NJ)
        ig = v3(take(NJ * P), NJ)
        reset = take(HALF)
        work = take(16 * HALF)
        (tmp, lam, cum, eP, eN, aa, kk, k2, bb, AR0, AR1, Bh, Kh, rkp, gg, Y) = (
            work[:, i * HALF:(i + 1) * HALF] for i in range(16))
        AR = work[:, 9 * HALF:11 * HALF].rearrange("p (w t) -> p w t", w=2)
        GB = 5888
        grpb = take(2 * GB)
        xc, tr, ti, t2, hs = (grpb[:, i * HALF:(i + 1) * HALF] for i in range(5))
        wlo = grpb[:, 4096:4096 + KC * 160].rearrange("p (k m) -> p k m", k=KC)

        class Grp:
            def __init__(self, g):
                o = g * GB
                self.c0 = g * GRP
                self.b = 4 * g

                def take(n):
                    nonlocal o
                    o += n
                    return grpb[:, o - n:o]
                self.dtg = take(1024).rearrange("p (h a w t) -> p h a w t", h=2, a=2, w=2)
                self.ak = take(1024).rearrange("p (h a w t) -> p h a w t", h=2, a=2, w=2)
                self.ab_flat = take(1024)
                self.a = self.ab_flat[:, 0:512].rearrange("p (h a t) -> p h a t", h=2, a=2)
                self.bt = self.ab_flat[:, 512:1024].rearrange("p (h a t) -> p h a t", h=2, a=2)
                d = take(512)
                self.d = d.rearrange("p (h a t) -> p h a t", h=2, a=2)
                self.tt = d.rearrange("p (c a t) -> p c a t", c=2, a=2)
                self.e = take(512).rearrange("p (h a t) -> p h a t", h=2, a=2)
                self.p_flat = take(512)
                self.p = self.p_flat.rearrange("p (h a t) -> p h a t", h=2, a=2)
                self.z_flat = take(512)
                self.z = self.z_flat.rearrange("p (w a h t) -> p w a h t", w=2, a=2, h=2)
                self.zt = self.z_flat.rearrange("p (w a t) -> p w a t", w=2, a=2)
                self.vb = take(512)
                self.vtok = self.vb[:, 0:256].rearrange("p (a t) -> p a t", a=2)
                self.btok = self.vb[:, 256:512].rearrange("p (a t) -> p a t", a=2)
                self.kflat = take(256)
                self.ktok = self.kflat.rearrange("p (a t) -> p a t", a=2)
                self.rh = self.p_flat[:, 0:256]

            def bank(self, i):
                return ps[:, self.b + i, :]
        grp = [Grp(0), Grp(1)]

        ada = [grpb[:, 2048 * i:2048 * (i + 1)].rearrange("p (k m) -> p k m", k=KC) for i in range(2)]
        xn = ([work[:, D_MODEL * i:D_MODEL * (i + 1)] for i in range(5)] +
              [grpb[:, GB + D_MODEL * i:GB + D_MODEL * (i + 1)] for i in range(4)])
        cs = work[:, 5 * D_MODEL:5 * D_MODEL + 72].rearrange("p (k b) -> p k b", k=KC)
        csg = work[:, 5 * D_MODEL + 72:5 * D_MODEL + 144].rearrange("p (k b) -> p k b", k=KC)

        SN = NJ * DEC
        sq_ = [grpb[:, 4096 + SN * i:4096 + SN * (i + 1)].rearrange("p (j b) -> p j b", j=NJ) for i in range(24)]
        (s_lam, s_a, s_kk, s_t, s_t1, s_g, s_bon, s_y, s_xc, s_tr, s_ti, s_t2, s_hs, s_gl, s_mu) = sq_[:15]
        s_vecs = grpb[:, 5120:5120 + 6 * SN].rearrange("p (q j b) -> p q j b", q=6, j=NJ)
        s_vflat = grpb[:, 5120:5120 + 6 * SN]
        s_qt = grpb[0:32, 5400:5400 + 6 * P]
        s_row = grpb[:, 6200:6200 + 5 * HEAD].rearrange("p (q k) -> p q k", q=5)
        s_vr = grpb[:, 6600:6632]
        s_sa = grpb[:, 6640:6672]
        s_yr = grpb[:, 6680:6712]
        s_yrow = grpb[0:32, 6720:6848]
        s_conv = grpb[:, 6900:6900 + 96].rearrange("p (j r b) -> p j r b", j=NJ, r=3)
        s_lru0 = grpb[:, 7000:7032].rearrange("p (j b) -> p j b", j=NJ)
        s_S = work[:, 0:2048].rearrange("p (v k) -> p v k", v=32)
        s_T = work[:, 2048:4096].rearrange("p (v k) -> p v k", v=32)
        s_Sf = work[:, 0:2048]

        at[0] = base
        x1 = v3(take(9 * D_MODEL), 9)
        rowb = v3(take(4 * D_MODEL), 4)
        rows_s = v3(arena[:, 0:4 * D_MODEL], 4)
        lnr = v3(arena[:, 4 * D_MODEL:8 * D_MODEL], 4)
        lgt = v3(take(9 * 20), 9)
        rt_a = [v3(take(9 * 4), 9) for _ in range(8)]
        rt_s = [take(9) for _ in range(8)]
        pos1, pos2, pp1, pp2, psn = (take(9) for _ in range(5))
        posu = v3(take(18).bitcast(U32), 2)
        e1 = v3(take(9 * NEXP), 9)
        e2 = v3(take(9 * NEXP), 9)
        asg = v3(take(9 * NEXP), 9)
        rank = v3(take(9 * NEXP), 9)
        carry = v3(take(10 * NEXP), 10)
        ntile, tend, tbase = (take(NEXP) for _ in range(3))
        texp_f = take(STEPS)
        texp = take(STEPS).bitcast(I32)
        perm = take(STEPS).bitcast(U32)
        wrt = v3(take(KC * 20), KC)
        brt = take(20)
        late = at[0]
        wout = v3(take(KC * D_MODEL), KC)
        xr2 = v3(take(2 * D_MODEL), 2)
        zz = take(D_MODEL)
        n2 = v3(take(2 * D_MODEL), 2)
        diag = v3(take(8 * P), 8)
        h2t = v3(take(KC * P), KC)
        at[0] = late
        ge = take(9 * (STEPS + 1)).rearrange("p (i s) -> p i s", i=9)
        wt = take(2 * 9 * STEPS).rearrange("p (a i s) -> p a i s", a=2, i=9)
        uu = v3(take(4 * P), 4)
        tcmp = v3(take(STEPS * NEXP), STEPS)
        at[0] = late
        exgu = [v3(arena[:, yT_at + 4096 * b:yT_at + 4096 * (b + 1)], KC) for b in range(2)]
        exdn = [v3(take(2048), 2) for _ in range(2)]
        xg = v3(take(2 * D_MODEL), 2)
        xgt = [v3(take(D_MODEL), KC) for _ in range(2)]
        sil = take(DEXP)
        hid = v3(take(2 * DEXP), 2)
        hidt = [v3(take(DEXP), 2) for _ in range(2)]
        ys = v3(take(2 * D_MODEL), 2)
        yg = [v3(take(2 * D_MODEL), 2) for _ in range(2)]
        fz = v3(take(2 * D_MODEL), 2)

        block = ctx.enter_context(nc.Block())
        V, A, T, G = nc.vector, nc.scalar, nc.tensor, nc.gpsimd
        HV = {**h, **g_, **samp}

        ROWS2 = (16, 32, 24, 40)

        def pcol(q, j):
            return par[:, q, j:j + 1]

        D_W0, D_A0, D_OKA, D_RG, D_IG, D_ML, D_NML, D_TMP = range(8)

        def dcol(q, j):
            return der[:, q, j:j + 1]

        @block.sync
        def _(sp):
            sp.dma_start(cs, c_t).then_inc(ld_cs, 16)
            for dst, src in ((par, prm), (mu_wa, mu_lo[0:64]), (mu_gd, mu_lo[64:160]), (bada, b_ada),
                             (wa_up, w_wa_up), (g_up, w_g_up)):
                sp.dma_start(dst, src).then_inc(ld_const, 16)

            def load_rows(g):
                for i in range(3 * g, 3 * g + 3):
                    r0, rt = TILES[i]
                    sp.dma_start(xn[i][0:rt], x_all[r0:r0 + rt, :]).then_inc(ld_x[g], 16)

            def load_mod(n):
                if n >= 2:
                    sp.wait_ge(mod_mm, n - 1)
                sp.dma_start(ada[n % 2].rearrange("p k m -> p (k m)"), w_ada[n]).then_inc(ld_ada[n % 2], 16)

            load_rows(0)
            load_mod(0)
            load_mod(1)
            load_rows(1)
            load_rows(2)
            for n in range(2, MOD0):
                load_mod(n)
            sp.dma_start(wlo.rearrange("p k m -> p (k m)"), w_lo).then_inc(ld_lo, 16)
            sp.dma_start(hT[:, :, NTOK:NCOL], shift_t).then_inc(ld_prev, 16)
            for n in range(3):
                sp.dma_start(win[:, n % 3, :], w_in[n]).then_inc(ld_win[n % 3], 16)
                load_mod(MOD0 + n)
            for n in range(MOD0 + 3, 24):
                load_mod(n)
            for n in range(3, 5 * NJ):
                sp.wait_ge(win_mm, 3 * (n - 3 + 2) + 3)
                sp.dma_start(win[:, n % 3, :], w_in[n]).then_inc(ld_win[n % 3], 16)
            for i, (r0, rt) in enumerate(TILES):
                sp.wait_ge(h2_ready, i + 1)
                sp.dma_start(h2_scr[r0:r0 + rt, :], n2[0:rt, i % 2, :]).then_inc(h2_stored[i % 2], 16)

            def load_expert(s, b, gu_used=None, dn_used=None):
                ex = sp.value_load(texp[0:1, bass.ds(s, 1)], min_val=0, max_val=NEXP - 1)
                if gu_used is not None:
                    sp.wait_ge(gu_mm, gu_used)
                sp.dma_start(exgu[b].rearrange("p k f -> p (k f)"),
                             w_gu[bass.ds(ex, 1)].rearrange("a p n -> (a p) n")).then_inc(ld_gu[b], 16)
                if dn_used is not None:
                    sp.wait_ge(dn_mm, dn_used)
                sp.dma_start(exdn[b].rearrange("p c d -> p (c d)"),
                             w_dn[bass.ds(ex, 1)].rearrange("a p n -> (a p) n")).then_inc(ld_dn[b], 16)

            sp.wait_ge(route_ready, 1)
            load_expert(0, 0)
            load_expert(1, 1)
            with sp.Fori(1, STEPS // 2) as i:
                for b in range(2):
                    load_expert(2 * i + b, b, 2 * i + (b - 1), 2 * i + (b - 1))

        @block.gpsimd
        def _(pool):
            def link(ins):
                chain_p.on(ins)
                pool.wait_ge(chain_p.sem, chain_p.n)

            def select(t, pattern, op, base, cm):
                link(G.affine_select(out=t, in_=t, compare_op=op, fill=0.0, base=base, pattern=pattern,
                                     channel_multiplier=cm))

            def same_block(t, size):
                v = t.rearrange("p (n c) -> p n c", c=size)
                select(v, [[-size, P // size], [0, size]], ALU.is_ge, 0, 1)
                select(v, [[size, P // size], [0, size]], ALU.is_ge, size - 1, -1)

            def later_block(t, size):
                v = t.rearrange("p (n c) -> p n c", c=size)
                select(v, [[-size, P // size], [0, size]], ALU.is_ge, -size, 1)

            for t in (rg, ig):
                link(G.memset(t, 0.0))
            for n in range(2):
                for dst, src in ((rg, w_rg), (ig, w_ig)):
                    r0 = slice(64 * n, 64 * n + 64)
                    pool.dma_start(dst[r0, :, r0], src[:, r0, :].rearrange("j c d -> c j d")).then_inc(ld_samp, 16)
            link(G.memset(ones, 1.0))
            link(G.memset(eps[:, 1:2], GN_EPS))
            G.memset(eps[:, 0:1], LN_EPS).then_inc(consts_ready, 1)
            for t in (ident, blk_ones, mask_dt[:, 0], mask_dt[:, 1], mask_ak[:, 0], mask_d, mask_e, before, valid):
                link(G.memset(t, 1.0))
            link(G.memset(reset, 1.0))
            link(G.memset(reset.rearrange("p (c t) -> p c t", t=CHUNK)[:, :, 0:1], 0.0))
            for t in (pk, pr, pv, prec, pwa, pgd):
                link(G.memset(t[:, 0:PAD], 0.0))
            select(ident, [[-1, P]], ALU.is_equal, 0, 1)
            same_block(blk_ones, HEAD)
            same_block(mask_dt[:, 0], 16)
            select(mask_dt[:, 0], [[1, P]], ALU.is_gt, 0, -1)
            same_block(mask_dt[:, 1], CHUNK)
            select(mask_dt[:, 1], [[1, P]], ALU.is_ge, 0, -1)
            same_block(mask_ak[:, 0], CHUNK)
            select(mask_ak[:, 0], [[1, P]], ALU.is_gt, 0, -1)
            link(G.tensor_copy(mask_ak[:, 1], mask_dt[:, 1]))
            same_block(mask_d, 16)
            select(mask_d, [[-1, P]], ALU.is_gt, 0, 1)
            same_block(mask_e, CHUNK)
            later_block(mask_e, 16)
            select(before, [[1, P]], ALU.is_gt, 0, -1)
            link(G.iota(iota_p, [[1, P]], base=0, channel_multiplier=0, allow_small_or_imprecise_dtypes=True))
            link(G.iota(iota_s, [[1, STEPS]], base=0, channel_multiplier=0, allow_small_or_imprecise_dtypes=True))
            link(G.iota(iota_t, [[P, STEPS + 1]], base=0, channel_multiplier=0, allow_small_or_imprecise_dtypes=True))
            link(G.iota(tok_id, [[P, 9]], base=0, channel_multiplier=1, allow_small_or_imprecise_dtypes=True))
            select(valid[:, 8:9], [[1, 1]], ALU.is_ge, DEC - 1, -1)
            select(tok_id[:, 8:9], [[1, 1]], ALU.is_ge, DEC - 1, -1)
            G.tensor_scalar(blk_mean, blk_ones, 1.0 / HEAD, None, ALU.mult).then_inc(consts_ready, 1)
            pool.wait_ge(ht_dve, 9)
            pool.wait_ge(ht_act, 8)
            pool.dma_start(shift_o, hT[:, :, SEQ - 1:NTOK]).then_inc(outs, 16)
            pool.dma_start(convs_o, state_conv[:, 1:3, :]).then_inc(outs, 16)
            for j in range(NJ):
                pool.wait_ge(win_out, 6 + 15 * j + 12)
                pool.dma_start(conv_o[j], prec[:, PAD + SEQ - 3:PAD + NTOK]).then_inc(outs, 16)
            pool.wait_ge(HV["half_done"], 2 * NJ)
            pool.wait_ge(HV["y_out"], 16)
            pool.dma_start(s_Sf, wkv0).then_inc(ld_samp, 16)
            pool.dma_start(s_conv, conv0).then_inc(ld_samp, 16)
            pool.dma_start(s_lru0, lru0).then_inc(ld_samp, 16)
            pool.wait_ge(*SAMP["s_vrow"])
            pool.dma_start(q_scr.rearrange("q r c -> r q c"), s_qt.rearrange("r (q c) -> r q c", q=6)).then_inc(HV["s_stored"], 16)
            pool.wait_ge(HV["s_stored"], 16)
            flat = q_scr.rearrange("q r c -> q (r c)")
            for n, q in enumerate((0, 1, 2, 4, 5)):
                src = flat[q].rearrange("(r k) -> r k", k=HEAD).unsqueeze(1).to_broadcast([64, 2, HEAD])
                pool.dma_start(s_row[:, n, :], src).then_inc(HV["s_rows"], 16)
            pool.dma_start(s_vr, flat[3].rearrange("(r k) -> r k", k=32)).then_inc(HV["s_rows"], 16)
            pool.wait_ge(*SAMP["s_y"])
            pool.dma_start(wkvs_o, s_Sf).then_inc(outs, 16)
            pool.dma_start(y_scr.rearrange("r c -> (r c)").rearrange("(p v) -> p v", v=32), s_yr).then_inc(HV["s_ystored"], 16)
            pool.wait_ge(HV["s_ystored"], 16)
            pool.dma_start(s_yrow, y_scr).then_inc(HV["s_yrow"], 16)
            pool.dma_start(wkvp_o.rearrange("j p v -> p j v"), sfin).then_inc(outs, 16)
            pool.wait_ge(*SAMP["s_done"])
            pool.dma_start(lru_o, lru_last).then_inc(outs, 16)
            pool.wait_ge(outs, 16 * 9)
            for k in range(KC):
                pool.dma_start(wout[:, k, :], w_out[k]).then_inc(ld_wout, 16)
            for n in range(4):
                pool.dma_start(lnr[:, n, :], ln_rows[n:n + 1, :].partition_broadcast(P)).then_inc(ld_late, 16)
            pool.dma_start(wrt, w_rt).then_inc(ld_late, 16)
            pool.dma_start(brt, b_rt.partition_broadcast(P)).then_inc(ld_late, 16)

            def modulate(i):
                rt = TILES[i][1]
                src = rowb if i < 8 else rows_s
                pool.wait_ge(n2_ready, i + 1)
                link(G.tensor_tensor(n2[0:rt, i % 2, :], n2[0:rt, i % 2, :], src[0:rt, 1, :], ALU.mult))
                G.tensor_tensor(n2[0:rt, i % 2, :], n2[0:rt, i % 2, :], src[0:rt, 2, :], ALU.add).then_inc(h2_ready, 1)

            for i, (r0, rt) in enumerate(TILES):
                if i >= 2:
                    pool.wait_ge(var_ready, 9 + 2 * (i - 2) + 1)
                pool.dma_start(xr2[0:rt, i % 2, :], x_all[r0:r0 + rt, :]).then_inc(ld_x2[i % 2], 16)
                if i:
                    modulate(i - 1)
            modulate(8)
            for b in range(2):
                pool.wait_ge(h2_stored[b], 16 * (5 - b))
            pool.wait_ge(route_ready, 1)

            def gather(s, b):
                pool.indirect_dma_start(xg[:, b, :], None, h2_scr,
                                        bass.IndirectOffsetOnAxis(perm[:, s:s + 1], 0)).then_inc(ld_xg[b], 16)

            for s in range(STEPS):
                if s >= 2:
                    pool.wait_ge(xg_turned, s - 1)
                gather(s, s % 2)
            for b in range(2):
                pool.wait_ge(slot_stored[b], 16 * (STEPS // 2))
            for i, (r0, rt) in enumerate(TILES):
                if i >= 2:
                    pool.wait_ge(yg_used, i - 1)
                for a in range(2):
                    pool.indirect_dma_start(yg[i % 2][0:rt, a, :], None, slot_scr,
                                            bass.IndirectOffsetOnAxis(posu[0:rt, a, i:i + 1], 0)).then_inc(ld_yg[i % 2], 16)
            pool.wait_ge(outs, 16 * 9)

        @block.tensor
        def _(pe):
            bank = [ps[:, i, :] for i in range(8)]
            pe.wait_ge(silu_ready, 1)
            def mod_mms(n, bank_):
                pe.wait_ge(ld_ada[n % 2], 16 * (n // 2 + 1))
                for m in range(2):
                    for k in range(KC):
                        mm = T.matmul(ps[:, bank_, 16 * m:16 * m + 9], ada[n % 2][:, k, P * m:P * m + P],
                                      csg[:, k, :], start=(k == 0), stop=(k == KC - 1))
                mm.then_inc(mod_mm, 1)

            for n in range(MOD0):
                mod_mms(n, n)
            pe.wait_ge(consts_ready, 2)
            pe.wait_ge(mod_out, MOD0)
            for i, (r0, rt) in enumerate(TILES):
                pe.wait_ge(xn_ready, i + 1)
                if i >= 4:
                    pe.wait_ge(ht_dve, i - 3)
                    pe.wait_ge(ht_act, i - 3)
                for k in range(KC):
                    tr_ = T.transpose(ps[:, 2 * (i % 4) + k // 4, P * (k % 4):P * (k % 4) + rt],
                                      xn[i][0:rt, P * k:P * k + P], ident[0:rt, 0:rt])
                tr_.then_inc(xn_turned, 1)
            pe.wait_ge(ht_dve, 9)
            pe.wait_ge(ht_act, 8)
            pe.wait_ge(ld_prev, 16)

            def project(n, lhs, rows):
                for c, (c0, w) in enumerate(COLS):
                    if n:
                        pe.wait_ge(win_out, 3 * (n - 1) + c + 1)
                    for k in range(KC):
                        mm = T.matmul(ps[0:rows, c, 0:w], lhs(k), hT[:, k, c0:c0 + w],
                                      start=(k == 0), stop=(k == KC - 1))
                    mm.then_inc(win_mm, 1)
                    m = MOD0 + 3 * n + c
                    if m < 24:
                        if m >= MOD0 + 2:
                            pe.wait_ge(mod_out, m - 1)
                        mod_mms(m, 3 + m % 2)

            pe.wait_ge(ld_lo, 16)
            project(0, lambda k: wlo[:, k, 0:64], 64)
            project(1, lambda k: wlo[:, k, 64:160], 96)
            pe.wait_ge(ld_const, 16 * 6)
            pe.wait_ge(ld_samp, 16 * 4)
            for j in range(NJ):
                if j:
                    pe.wait_ge(HV["half_done"], 2 * j)
                for q in range(5):
                    n = 5 * j + q
                    pe.wait_ge(ld_win[n % 3], 16 * (n // 3 + 1))
                    project(n + 2, lambda k: win[:, n % 3, P * k:P * k + P], P)
                for hf in range(2):
                    it = 2 * j + hf
                    t0 = PAD + hf * HALF
                    js = slice(P * j, P * j + P)
                    if it == 0:
                        pe.wait_ge(lora_ready, 1)
                    if it:
                        pe.wait_ge(HV["half_done"], it)
                    pe.wait_ge(win_out, 3 * (5 * j + 7))
                    T.matmul(bank[3], wa_up[0:32, js], pwa[0:32, t0:t0 + HALF], start=True, stop=True)
                    T.matmul(bank[4], wa_up[32:64, js], pwa[32:64, t0:t0 + HALF], start=True, stop=True)
                    T.matmul(bank[5], g_up[:, js], pgd[:, t0:t0 + HALF], start=True, stop=True).then_inc(HV["up_mm"], 1)
                    pe.wait_ge(HV["sq_ready"], it + 1)
                    T.matmul(bank[6], blk_ones, tmp, start=True, stop=True).then_inc(HV["norm_mm"], 1)
                    pe.wait_ge(HV["conv_ready"], it + 1)
                    T.matmul(bank[0], rg[:, j, :], xc, start=True, stop=True)
                    T.matmul(bank[1], ig[:, j, :], xc, start=True, stop=True).then_inc(HV["gate_mm"], 1)
                    pe.wait_ge(HV["rkp_ready"], it + 1)
                    T.matmul(bank[7], blk_ones, rkp, start=True, stop=True).then_inc(HV["bonus_mm"], 1)
                    pe.wait_ge(HV["prep_done"], it + 1)
                    pe.wait_ge(HV["bonus_out"], it + 1)

                    def heads():
                        for hh in range(2):
                            for a in range(2):
                                yield hh, a, slice(HEAD * hh, HEAD * hh + HEAD)

                    def stage(g, name, waits, products):
                        gi = 2 * it + g
                        for w in waits:
                            pe.wait_ge(HV[w], gi + 1)
                        for out, lhs, rhs in products:
                            mm = T.matmul(out, lhs, rhs, start=True, stop=True)
                        mm.then_inc(HV[name], 1)

                    def unit(g, b):
                        return grp[g].bank(b).rearrange("p (h a t) -> p h a t", h=2, a=2)

                    def zunit(g, b):
                        return grp[g].bank(b).rearrange("p (w a h t) -> p w a h t", w=2, a=2, h=2)

                    def toks(g, a):
                        return slice(grp[g].c0 + P * a, grp[g].c0 + P * a + P)

                    for g in range(2):
                        q = grp[g]
                        stage(g, "gram_b", (), [(q.bank(hh)[:, 256 * a:256 * a + 256], bb[r, toks(g, a)],
                                                 AR[r, :, toks(g, a)]) for hh, a, r in heads()])
                    for g in range(2):
                        q = grp[g]
                        stage(g, "gram_k", (), [(q.bank(2 + hh)[:, 256 * a:256 * a + 256], k2[r, toks(g, a)],
                                                 AR[r, :, toks(g, a)]) for hh, a, r in heads()])
                    for g in range(2):
                        q = grp[g]
                        stage(g, "gram_l", ("dt_out",), [(q.bank(hh)[:, P * a:P * a + P], AR0[r, toks(g, a)],
                                                          bb[r, toks(g, a)]) for hh, a, r in heads()])
                    for g in range(2):
                        q = grp[g]
                        pe.wait_ge(HV["ak_out"], 2 * it + g + 1)
                        for a in range(2):
                            for b_, o, src in ((2, 0, AR0[:, toks(g, a)]), (2, 256, Kh[:, toks(g, a)]),
                                               (3, 0, pv[:, t0 + q.c0 + P * a:t0 + q.c0 + P * a + P]),
                                               (3, 256, Bh[:, toks(g, a)])):
                                mm = T.transpose(q.bank(b_)[:, o + P * a:o + P * a + P], src, ident)
                        mm.then_inc(HV["turned"], 1)
                    for g in range(2):
                        q = grp[g]
                        stage(g, "akv_mm", ("tok_out",),
                              [(q.bank(3)[:, P * a + HEAD * hh:P * a + HEAD * hh + HEAD], q.ak[:, hh, a, 0, :],
                                q.vtok[:, a, HEAD * hh:HEAD * hh + HEAD]) for hh, a, r in heads()])
                    for g in range(2):
                        q = grp[g]
                        stage(g, "d2_mm", ("de_out",),
                              [(unit(g, 0)[:, hh, a], q.dtg[:, hh, a, 0, :], q.d[:, hh, a]) for hh, a, r in heads()] +
                              [(unit(g, 1)[:, hh, a], q.d[:, hh, a], q.dtg[:, hh, a, 0, :]) for hh, a, r in heads()])
                    for g in range(2):
                        q = grp[g]
                        stage(g, "p2_mm", ("d2_out", "p1_out"),
                              [(unit(g, 2)[:, hh, a], q.a[:, hh, a], q.p[:, hh, a]) for hh, a, r in heads()] +
                              [(unit(g, 0)[:, hh, a], q.bt[:, hh, a], q.a[:, hh, a]) for hh, a, r in heads()] +
                              [(unit(g, 1)[:, hh, a], q.a[:, hh, a], q.bt[:, hh, a]) for hh, a, r in heads()])
                    for g in range(2):
                        q = grp[g]
                        stage(g, "p3_mm", ("d4_out", "p2_out"),
                              [(unit(g, 2)[:, hh, a], q.a[:, hh, a], q.p[:, hh, a]) for hh, a, r in heads()] +
                              [(unit(g, 0)[:, hh, a], q.bt[:, hh, a], q.a[:, hh, a]) for hh, a, r in heads()])
                    for g in range(2):
                        q = grp[g]
                        stage(g, "p4_mm", ("d8_out", "p3_out"),
                              [(unit(g, 2)[:, hh, a], q.a[:, hh, a], q.p[:, hh, a]) for hh, a, r in heads()])
                    for g in range(2):
                        q = grp[g]
                        stage(g, "f_mm", ("nt_out", "akv_out"),
                              [(unit(g, 0)[:, hh, a], q.p[:, hh, a], q.e[:, hh, a]) for hh, a, r in heads()] +
                              [(unit(g, 1)[:, hh, a], q.e[:, hh, a], q.p[:, hh, a]) for hh, a, r in heads()] +
                              [(zunit(g, 2)[:, :, a, hh], q.p[:, hh, a], q.z[:, :, a, hh]) for hh, a, r in heads()])
                    for g in range(2):
                        q = grp[g]
                        stage(g, "z1_mm", ("f_out", "z0_out"),
                              [(unit(g, 0)[:, hh, a], q.a[:, hh, a], q.bt[:, hh, a]) for hh, a, r in heads()] +
                              [(zunit(g, 2)[:, :, a, hh], q.bt[:, hh, a], q.z[:, :, a, hh]) for hh, a, r in heads()])
                    for g in range(2):
                        q = grp[g]
                        stage(g, "z2_mm", ("f2_out", "z1_out"),
                              [(zunit(g, 1)[:, :, a, hh], q.a[:, hh, a], q.z[:, :, a, hh]) for hh, a, r in heads()])
                    for g in range(2):
                        q = grp[g]
                        stage(g, "rt_mm", ("z2_out",),
                              [(q.bank(0)[r, P * a:P * a + P], q.z[:, 0, a, hh, :], q.dtg[:, hh, a, 1, :])
                               for hh, a, r in heads()] +
                              [(q.bank(2 + c)[:, P * a:P * a + P], q.zt[HEAD * c:HEAD * c + HEAD, 0, a, :],
                                q.btok[HEAD * c:HEAD * c + HEAD, a, :]) for a in range(2) for c in range(2)])
                    for g in range(2):
                        q = grp[g]
                        gi = 2 * it + g
                        for hh, a, r in heads():
                            T.matmul(q.bank(1)[r, P * a:P * a + P], q.z[:, 1, a, hh, :], q.dtg[:, hh, a, 1, :],
                                     start=(a == 0), stop=False, skip_group_check=True)
                            T.matmul(q.bank(1)[r, P * a:P * a + P], q.vtok[:, a, r], q.ak[:, hh, a, 1, :],
                                     start=False, stop=False, skip_group_check=True)
                        pe.wait_ge(HV["tt_out"], gi + 1)
                        pe.wait_ge(HV["rh_out"], gi + 1)
                        for n in range(4):
                            a, c = n // 2, n % 2
                            r = slice(HEAD * c, HEAD * c + HEAD)
                            out = q.bank(2 + c)[:, 256:384]
                            if 4 * gi + n >= 2:
                                pe.wait_ge(state_out, 4 * gi + n - 1)
                            T.matmul(out, q.btok[r, a, :], q.zt[r, 1, a, :], start=True, stop=False)
                            T.matmul(out, q.ktok[r, a, :], q.vtok[r, a, :], start=False, stop=False)
                            cur = 4 * gi + n
                            if 4 * (gi % 4) + n == 0:
                                pe.wait_ge(s_zero, j + 1)
                            if cur:
                                pe.wait_ge(state_out, cur)
                            t_ = slice(P * a + HEAD * c, P * a + HEAD * c + HEAD)
                            T.matmul(q.bank(1)[:, t_], S[:, n % 2, :], q.rh[:, t_], start=False,
                                     stop=(n == 3), skip_group_check=True)
                            T.matmul(out, q.tt[:, c, a, :], S[:, n % 2, :], start=False, stop=True).then_inc(state_mm, 1)
                    pe.wait_ge(HV["y_out"], 2 * it + 2)
                    T.matmul(bank[0], blk_mean, Y, start=True, stop=True).then_inc(HV["mean_mm"], 1)
                    pe.wait_ge(HV["ysq_ready"], it + 1)
                    T.matmul(bank[1], blk_mean, tmp, start=True, stop=True).then_inc(HV["var_mm"], 1)

            pe.wait_ge(HV["half_done"], 2 * NJ)
            for b_, lhs, rhs in ((0, wa_up[0:32], pwa[0:32]), (1, wa_up[32:64], pwa[32:64]), (2, g_up, pgd)):
                for j in range(NJ):
                    mm = T.matmul(bank[b_][:, DEC * j:DEC * j + DEC], lhs[:, P * j:P * j + P],
                                  rhs[:, PAD + SEQ:PAD + NTOK], start=True, stop=True)
            mm.then_inc(SAMP["s_up"][0], 1)
            pe.wait_ge(*SAMP["s_conv"])
            for b_, w_ in ((3, rg), (4, ig)):
                for j in range(NJ):
                    mm = T.matmul(bank[b_][:, DEC * j:DEC * j + DEC], w_[:, j, :], s_xc[:, j, :],
                                  start=True, stop=True)
            mm.then_inc(SAMP["s_gates"][0], 1)
            pe.wait_ge(*SAMP["s_sq"])
            T.matmul(bank[5][:, 0:SN], blk_ones, s_t.rearrange("p j b -> p (j b)"), start=True,
                     stop=True).then_inc(SAMP["s_norm"][0], 1)
            pe.wait_ge(*SAMP["s_bon"])
            T.matmul(bank[6][:, 0:SN], blk_ones, s_t1.rearrange("p j b -> p (j b)"), start=True,
                     stop=True).then_inc(SAMP["s_bonmm"][0], 1)
            pe.wait_ge(*SAMP["s_vec"])
            for q in range(6):
                mm = T.transpose(bank[q // 4][0:SN, P * (q % 4):P * (q % 4) + P], s_vflat[:, SN * q:SN * q + SN], ident)
            mm.then_inc(SAMP["s_turn"][0], 1)
            pe.wait_ge(HV["s_yrow"], 16)
            T.transpose(bank[2][:, 0:SN], s_yrow, ident[0:SN, 0:SN]).then_inc(SAMP["s_yturn"][0], 1)
            pe.wait_ge(*SAMP["s_yc"])
            T.matmul(bank[3][:, 0:SN], blk_mean, s_y.rearrange("p j b -> p (j b)"), start=True,
                     stop=True).then_inc(SAMP["s_mean"][0], 1)
            pe.wait_ge(*SAMP["s_sqr"])
            T.matmul(bank[4][:, 0:SN], blk_mean, s_t.rearrange("p j b -> p (j b)"), start=True,
                     stop=True).then_inc(SAMP["s_var"][0], 1)

            for k in range(4 * KC):
                pe.wait_ge(row_diag, k + 1)
                if k >= 2:
                    pe.wait_ge(row_out, k - 1)
                T.matmul(bank[5 + k % 2][:, 0:P], ones, diag[:, k % 8, :], start=True, stop=True)
                T.transpose(bank[5 + k % 2][0:DEC, P:2 * P], modT[:, ROWS2[k // 8] + k % 8, 1:9],
                            ident).then_inc(row_mm, 1)
            pe.wait_ge(ld_wout, 16 * KC)
            pe.wait_ge(*SAMP["s_done"])

            def turn_h2(i):
                r0, rt = TILES[i]
                pe.wait_ge(h2_ready, i + 1)
                if i:
                    pe.wait_ge(h2t_out, i)
                for k in range(KC):
                    mm = T.transpose(ps[:, 4 + k // 4, P * (k % 4):P * (k % 4) + rt],
                                     n2[0:rt, i % 2, P * k:P * k + P], ident[0:rt, 0:rt])
                mm.then_inc(h2_turned, 1)
                pe.wait_ge(h2t_out, i + 1)
                for k in range(KC):
                    mm = T.matmul(ps[0:rt, 6, 20 * i:20 * i + 20], h2t[:, k, 0:rt], wrt[:, k, :],
                                  start=(k == 0), stop=(k == KC - 1))
                mm.then_inc(router_mm, 1)

            pe.wait_ge(ld_late, 16 * 6)
            pe.wait_ge(row_out, 4 * KC)
            for i, (r0, rt) in enumerate(TILES):
                for n in range(2):
                    if i >= 2:
                        pe.wait_ge(wo_out, i - 1)
                    for k in range(KC):
                        mm = T.matmul(ps[0:rt, 2 * (i % 2) + n, :], yT[:, k, r0:r0 + rt],
                                      wout[:, k, 512 * n:512 * n + 512], start=(k == 0), stop=(k == KC - 1))
                    mm.then_inc(wo_mm, 1)
                if i:
                    turn_h2(i - 1)
            turn_h2(8)
            pe.wait_ge(assigned, 1)
            T.matmul(bank[0][:, 0:9 * NEXP], before, asg.rearrange("p i e -> p (i e)"), start=True, stop=True)
            T.matmul(bank[1][:, 0:9 * NEXP], ones, asg.rearrange("p i e -> p (i e)"), start=True,
                     stop=True).then_inc(rank_mm, 1)
            for n in range(18):
                pe.wait_ge(hot_ready, n + 1)
                T.matmul(bank[2][:, 0:STEPS], uu[:, n % 4, :], wt[:, n // 9, n % 9, :], start=(n == 0),
                         stop=(n == 17)).then_inc(hot_used, 1)

            def turn_rows(s, b):
                for k in range(KC):
                    mm = T.transpose(ps[:, k // 4, P * (k % 4):P * (k % 4) + P], xg[:, b, P * k:P * k + P], ident)
                mm.then_inc(xg_turned, 1)

            def gate_up(s, b):
                for k in range(KC):
                    mm = T.matmul(ps[:, 2 + b, :], xgt[b][:, k, :], exgu[b][:, k, :], start=(k == 0), stop=(k == KC - 1))
                mm.then_inc(gu_mm, 1)

            def turn_hidden(s, b):
                for c in range(2):
                    mm = T.transpose(ps[:, 4 + b, P * c:P * c + P], hid[:, b, P * c:P * c + P], ident)
                mm.then_inc(hid_turned, 1)

            def down(s, b):
                for n in range(2):
                    for c in range(2):
                        mm = T.matmul(ps[:, 6 + n, :], hidt[b][:, c, :], exdn[b][:, c, 512 * n:512 * n + 512],
                                      start=(c == 0), stop=(c == 1))
                mm.then_inc(dn_mm, 1)

            pe.wait_ge(route_ready, 1)
            pe.wait_ge(ld_xg[0], 16)
            turn_rows(0, 0)
            pe.wait_ge(xgt_out, 1)
            pe.wait_ge(ld_gu[0], 16)
            gate_up(0, 0)
            pe.wait_ge(ld_xg[1], 16)
            turn_rows(1, 1)
            pe.wait_ge(hid_out, 1)
            turn_hidden(0, 0)

            def step(s, i, b, more):
                pe.wait_ge(xgt_out, s + 1)
                pe.wait_ge(ld_gu[b], 16 * i + 16)
                gate_up(s, b)
                pe.wait_ge(hidt_out, s)
                if not (isinstance(s, int) and s == 1):
                    pe.wait_ge(ys_out, s - 1)
                pe.wait_ge(ld_dn[1 - b], 16 * i + 16 * b)
                down(s, 1 - b)
                if more:
                    pe.wait_ge(ld_xg[1 - b], 16 * i + 16 * (1 + b))
                    turn_rows(s, 1 - b)
                pe.wait_ge(hid_out, s + 1)
                turn_hidden(s, b)

            step(1, 0, 1, True)
            with pe.Fori(1, STEPS // 2 - 1) as i:
                for b in range(2):
                    step(2 * i + b, i, b, True)
            step(STEPS - 2, STEPS // 2 - 1, 0, True)
            step(STEPS - 1, STEPS // 2 - 1, 1, False)
            pe.wait_ge(hidt_out, STEPS)
            pe.wait_ge(ys_out, STEPS - 1)
            pe.wait_ge(ld_dn[1], 16 * (STEPS // 2))
            down(STEPS, 1)

        @block.scalar
        def _(act):
            def link(ins):
                chain_a.on(ins)
                act.wait_ge(chain_a.sem, chain_a.n)

            act.wait_ge(ld_cs, 16)
            A.activation(csg, cs, ACT.Tanh, scale=0.5).then_inc(cond_tanh, 1)
            act.wait_ge(ld_const, 16 * 6)
            link(A.activation(der[:, D_TMP, :], par[:, LAM, :], ACT.Abs))
            link(A.activation(der[:, D_TMP, :], der[:, D_TMP, :], ACT.Exp, scale=-1.0))
            act.wait_ge(consts_ready, 1)
            A.activation(der[:, D_TMP, :], der[:, D_TMP, :], ACT.Ln, bias=ones[:, 0:1]).then_inc(lam_ln, 1)
            for i, (r0, rt) in enumerate(TILES):
                act.wait_ge(var_ready, i + 1)
                if i >= 1:
                    act.wait_ge(xn_ready, i)
                A.activation(sd[0:rt], mv[0:rt, 1:2], ACT.Sqrt, bias=eps[0:rt, 0:1]).then_inc(sd_ready, 1)
            act.wait_ge(mod_out, MOD0)
            for i, (r0, rt) in enumerate(TILES):
                if i < 8:
                    act.wait_ge(xn_turned, i + 1)
                    for k in range(4, 8):
                        last = A.activation(hT[:, k, r0:r0 + rt], ps[:, 1 + 2 * (i % 4), P * (k - 4):P * (k - 3)],
                                            ACT.Identity, bias=modT[:, k, 0:1], scale=modT[:, 8 + k, 0:1])
                    last.then_inc(ht_act, 1)

            def project_out(n, dst):
                for c, (c0, w) in enumerate(COLS):
                    act.wait_ge(win_mm, 3 * n + c + 1)
                    A.activation(dst[:, PAD + c0:PAD + c0 + w], ps[0:dst.shape[0], c, 0:w], ACT.Copy).then_inc(win_out, 1)
                    m = MOD0 + 3 * n + c
                    if m < 24:
                        act.wait_ge(mod_mm, m + 1)
                        for a in range(2):
                            last = A.activation(modT[:, 2 * m + a, :], ps[:, 3 + m % 2, 16 * a:16 * a + 9],
                                                ACT.Identity, bias=bada[:, 2 * m + a:2 * m + a + 1])
                        last.then_inc(mod_out, 1)

            project_out(0, pwa)
            project_out(1, pgd)
            act.wait_ge(lora_shifted, 1)
            A.activation(pwa[0:32, PAD:PAD + NTOK], pwa[0:32, PAD:PAD + NTOK], ACT.Tanh).then_inc(lora_tanh, 1)
            A.activation(pgd[:, PAD:PAD + NTOK], pgd[:, PAD:PAD + NTOK], ACT.Tanh, scale=0.5).then_inc(lora_tanh, 1)
            act.wait_ge(params_ready, 1)
            for j in range(NJ):
                if j:
                    act.wait_ge(HV["half_done"], 2 * j)
                for q, dst in enumerate((pk, pr, pv, prec, pgate)):
                    if q == 3 and j:
                        act.wait_ge(outs, 16 * (2 + j))
                    project_out(2 + 5 * j + q, dst)
                for hf in range(2):
                    it = 2 * j + hf
                    o = PAD + hf * HALF
                    cols = slice(o, o + HALF)
                    if it:
                        act.wait_ge(HV["half_done"], it)
                    act.wait_ge(HV["up_mm"], it + 1)
                    A.activation(lam, ps[:, 3, :], ACT.Tanh, scale=0.5, bias=dcol(D_W0, j))
                    A.activation(aa, ps[:, 4, :], ACT.Tanh, scale=0.5, bias=dcol(D_A0, j)).then_inc(HV["ta_ready"], 1)
                    A.activation(gg, ps[:, 5, :], ACT.Copy).then_inc(HV["g_ready"], 1)
                    act.wait_ge(HV["shifted"], j + 1)
                    A.activation(tmp, pk[:, cols], ACT.Square, scale=pcol(K_K, j)).then_inc(HV["sq_ready"], 1)
                    act.wait_ge(HV["norm_mm"], it + 1)
                    A.activation(kk, ps[:, 6, :], ACT.Sqrt).then_inc(HV["nrm_ready"], 1)
                    act.wait_ge(HV["gate_mm"], it + 1)
                    link(A.activation(tr, ps[:, 0, :], ACT.Tanh, scale=0.5, bias=dcol(D_RG, j)))
                    A.activation(ti, ps[:, 1, :], ACT.Tanh, scale=0.5, bias=dcol(D_IG, j)).then_inc(HV["gates_tanh"], 1)
                    link(A.activation(t2, tr, ACT.Tanh, scale=dcol(D_ML, j), bias=dcol(D_ML, j)))
                    A.activation(tr, tr, ACT.Exp, scale=dcol(D_NML, j), bias=dcol(D_NML, j)).then_inc(HV["lru_exp"], 1)
                    act.wait_ge(HV["cum_ready"], it + 1)
                    A.activation(eP, cum, ACT.Exp)
                    A.activation(lam, lam, ACT.Exp)
                    A.activation(eN, cum, ACT.Exp, scale=-1.0).then_inc(HV["exp_ready"], 1)
                    act.wait_ge(HV["q_ready"], it + 1)
                    A.activation(t2, t2, ACT.Sqrt).then_inc(HV["lru_mult"], 1)
                    A.activation(pgate[:, cols], pgate[:, cols], ACT.Gelu_apprx_tanh).then_inc(HV["gelu_ready"], 1)

                    def out(g, name, wait, dst, src):
                        act.wait_ge(HV[wait], 2 * it + g + 1)
                        A.activation(dst, src, ACT.Copy).then_inc(HV[name], 1)

                    def two(g, b):
                        return ps[:, 4 * g + b:4 * g + b + 2, :].rearrange("p b x -> p (b x)")

                    for g in range(2):
                        q = grp[g]
                        act.wait_ge(HV["turned"], 2 * it + g + 1)
                        A.activation(q.vb, q.bank(3), ACT.Copy)
                        A.activation(q.kflat, q.bank(2)[:, 256:512], ACT.Copy)
                        A.activation(q.z_flat[:, 0:256], q.bank(2)[:, 0:256], ACT.Copy).then_inc(HV["tok_out"], 1)
                    for g in range(2):
                        q = grp[g]
                        out(g, "akv_out", "akv_mm", q.z_flat[:, 256:512], q.bank(3)[:, 0:256])
                    for g in range(2):
                        out(g, "d2_out", "d2_mm", grp[g].ab_flat, two(g, 0))
                    for g in range(2):
                        out(g, "d4_out", "p2_mm", grp[g].ab_flat, two(g, 0))
                    for g in range(2):
                        out(g, "d8_out", "p3_mm", grp[g].ab_flat[:, 0:512], grp[g].bank(0))
                    for g in range(2):
                        out(g, "f_out", "f_mm", grp[g].ab_flat, two(g, 0))
                    for g in range(2):
                        out(g, "f2_out", "z1_mm", grp[g].ab_flat[:, 0:512], grp[g].bank(0))
                    for g in range(2):
                        q = grp[g]
                        act.wait_ge(state_mm, 4 * (2 * it + g + 1))
                        A.activation(Y[:, q.c0:q.c0 + GRP], q.bank(1)[:, 0:GRP], ACT.Copy).then_inc(HV["y_out"], 1)
                    act.wait_ge(HV["centred"], it + 1)
                    A.activation(tmp, Y, ACT.Square).then_inc(HV["ysq_ready"], 1)
                    act.wait_ge(HV["var_mm"], it + 1)
                    A.activation(eP, ps[:, 1, :], ACT.Sqrt, bias=eps[:, 1:2]).then_inc(HV["gsd_ready"], 1)


            def tile_act(dst, src, f, scale, bias):
                for j in range(NJ):
                    s_ = dcol(scale, j) if isinstance(scale, int) else scale
                    last = A.activation(dst[:, j, :], src(j), f, scale=s_, bias=dcol(bias, j))
                return last

            def pcols(b_):
                return lambda j: ps[:, b_, DEC * j:DEC * j + DEC]

            act.wait_ge(*SAMP["s_up"])
            tile_act(s_lam, pcols(0), ACT.Tanh, 0.5, D_W0)
            tile_act(s_a, pcols(1), ACT.Tanh, 0.5, D_A0)
            A.activation(s_g, ps[:, 2, 0:SN].rearrange("p (j b) -> p j b", j=NJ), ACT.Copy).then_inc(SAMP["s_wa"][0], 1)
            act.wait_ge(*SAMP["s_gates"])
            tile_act(s_tr, pcols(3), ACT.Tanh, 0.5, D_RG)
            link(tile_act(s_ti, pcols(4), ACT.Tanh, 0.5, D_IG))
            link(tile_act(s_t2, lambda j: s_tr[:, j, :], ACT.Tanh, D_ML, D_ML))
            tile_act(s_tr, lambda j: s_tr[:, j, :], ACT.Exp, D_NML, D_NML).then_inc(SAMP["s_lexp"][0], 1)
            act.wait_ge(*SAMP["s_lam"])
            A.activation(s_vecs[:, 1], s_lam, ACT.Exp).then_inc(SAMP["s_w"][0], 1)
            act.wait_ge(*SAMP["s_norm"])
            A.activation(s_t.rearrange("p j b -> p (j b)"), ps[:, 5, 0:SN], ACT.Sqrt).then_inc(SAMP["s_nrm"][0], 1)
            act.wait_ge(*SAMP["s_q"])
            A.activation(s_t2, s_t2, ACT.Sqrt).then_inc(SAMP["s_mult"][0], 1)
            A.activation(s_mu, pgs, ACT.Gelu_apprx_tanh).then_inc(SAMP["s_gelu"][0], 1)
            act.wait_ge(*SAMP["s_cent"])
            A.activation(s_t, s_y, ACT.Square).then_inc(SAMP["s_sqr"][0], 1)
            act.wait_ge(*SAMP["s_var"])
            A.activation(s_t1.rearrange("p j b -> p (j b)"), ps[:, 4, 0:SN], ACT.Sqrt, bias=eps[:, 1:2]).then_inc(SAMP["s_gsd"][0], 1)

            def h2t_copy(i):
                rt = TILES[i][1]
                act.wait_ge(h2_turned, i + 1)
                if i:
                    act.wait_ge(router_mm, i)
                for n in range(2):
                    last = A.activation(h2t[:, 4 * n:4 * n + 4, 0:rt],
                                        ps[:, 4 + n, :].rearrange("p (k t) -> p k t", k=4)[:, :, 0:rt], ACT.Copy)
                last.then_inc(h2t_out, 1)

            for i, (r0, rt) in enumerate(TILES):
                act.wait_ge(var_ready, 9 + 2 * i + 1)
                A.activation(sd[0:rt], mv[0:rt, 1:2], ACT.Sqrt, bias=eps[0:rt, 0:1]).then_inc(sd_ready, 1)
                act.wait_ge(var_ready, 9 + 2 * i + 2)
                A.activation(sd[0:rt], mv[0:rt, 1:2], ACT.Sqrt, bias=eps[0:rt, 0:1]).then_inc(sd_ready, 1)
                if i:
                    h2t_copy(i - 1)
            h2t_copy(8)
            act.wait_ge(lg_ready, 1)
            A.activation(rt_a[0], rt_a[0], ACT.Exp).then_inc(ex_ready, 1)
            act.wait_ge(lg2_ready, 1)
            A.activation(rt_s[3], rt_s[3], ACT.Exp).then_inc(ex2_ready, 1)
            act.wait_ge(route_ready, 1)

            def rows_copy(s, b):
                act.wait_ge(xg_turned, s + 1)
                A.activation(xgt[b].rearrange("p k t -> p (k t)"), ps[:, 0:2, :].rearrange("p b x -> p (b x)"),
                             ACT.Copy).then_inc(xgt_out, 1)

            def hidden(s, b):
                act.wait_ge(gu_mm, s + 1)
                A.activation(sil, ps[:, 2 + b, 0:DEXP], ACT.Silu).then_inc(silu_out, 1)

            def hidden_copy(s, b):
                act.wait_ge(hid_turned, s + 1)
                A.activation(hidt[b].rearrange("p c t -> p (c t)"), ps[:, 4 + b, 0:DEXP], ACT.Copy).then_inc(hidt_out, 1)

            def store(s, b):
                act.wait_ge(ys_out, s + 1)
                act.dma_start(slot_scr.rearrange("(s p) d -> s p d", p=P)[bass.ds(s, 1)].rearrange("s p d -> (s p) d"),
                              ys[:, b, :]).then_inc(slot_stored[b], 16)

            rows_copy(0, 0)
            hidden(0, 0)
            rows_copy(1, 1)
            hidden_copy(0, 0)

            def act_step(s, b, more):
                hidden(s, b)
                if more:
                    rows_copy(s + 1, 1 - b)
                hidden_copy(s, b)
                store(s - 1, 1 - b)

            act_step(1, 1, True)
            with act.Fori(1, STEPS // 2 - 1) as i:
                for b in range(2):
                    act_step(2 * i + b, b, True)
            act_step(STEPS - 2, 0, True)
            act_step(STEPS - 1, 1, False)
            store(STEPS - 1, 1)
            for i, (r0, rt) in enumerate(TILES):
                act.wait_ge(var_ready, 27 + i + 1)
                A.activation(sd[0:rt], mv[0:rt, 1:2], ACT.Sqrt, bias=eps[0:rt, 0:1]).then_inc(sd_ready, 1)
                act.wait_ge(y_ready, i + 1)
                act.dma_start(y_all[r0:r0 + rt, :], fz[0:rt, i % 2, :]).then_inc(y_stored[i % 2], 16)
            act.wait_ge(y_stored[0], 16 * 5)
            act.wait_ge(y_stored[1], 16 * 4)

        @block.vector
        def _(dve):
            def link(ins):
                chain_v.on(ins)
                dve.wait_ge(chain_v.sem, chain_v.n)

            def done(ins, s_, n):
                ins.then_inc(s_, 1)
                dve.wait_ge(s_, n)

            TT, TS, STT = V.tensor_tensor, V.tensor_scalar, V.scalar_tensor_tensor

            dve.wait_ge(cond_tanh, 1)
            link(STT(out=csg, in0=csg, scalar=1.0, in1=cs, op0=ALU.add, op1=ALU.mult))
            done(TS(csg, csg, 0.5, None, ALU.mult), silu_ready, 1)
            dve.wait_ge(ld_const, 16 * 6)
            dve.wait_ge(consts_ready, 1)
            link(TS(bada[:, 8:24], bada[:, 8:24], 1.0, None, ALU.add))
            link(TS(bada[:, 32:48], bada[:, 32:48], 1.0, None, ALU.add))
            for d_, q_, m_ in ((D_W0, W0, 0.5), (D_A0, A0, 0.5), (D_RG, B_RG, 0.5), (D_IG, B_IG, 0.5)):
                link(TS(der[:, d_, :], par[:, q_, :], m_, None, ALU.mult))
            link(TS(der[:, D_OKA, :], par[:, K_A, :], -1.0, 1.0, ALU.mult, ALU.add))
            dve.wait_ge(lam_ln, 1)
            link(TS(der[:, D_ML, :], par[:, LAM, :], -1.0, 0.0, ALU.mult, ALU.max))
            link(TT(der[:, D_ML, :], der[:, D_ML, :], der[:, D_TMP, :], ALU.add))
            link(TS(der[:, D_ML, :], der[:, D_ML, :], 4.0, None, ALU.mult))
            done(TS(der[:, D_NML, :], der[:, D_ML, :], -1.0, None, ALU.mult), params_ready, 1)

            def moments(src, rt, s_, n):
                link(V.bn_stats(st[0:rt, 0, :], src[:, 0:512]))
                link(V.bn_stats(st[0:rt, 1, :], src[:, 512:1024]))
                done(V.bn_aggr(mv[0:rt], st[0:rt]), s_, n)

            def mod_rows(n):
                dve.wait_ge(mod_mm, n + 1)
                src = ps[:, n, 0:32].rearrange("p (m b) -> p m b", m=2)[:, :, 0:9]
                TT(modT[:, 2 * n:2 * n + 2, :], src, bada[:, 2 * n:2 * n + 2].unsqueeze(2).to_broadcast([P, 2, 9]),
                   ALU.add).then_inc(mod_out, 1)


            def ht_tile(i):
                r0, rt = TILES[i]
                dve.wait_ge(xn_turned, i + 1)
                if i < 8:
                    for k in range(4):
                        last = TS(hT[:, k, r0:r0 + rt], ps[:, 2 * (i % 4), P * k:P * k + P],
                                  modT[:, 8 + k, 0:1], modT[:, k, 0:1], ALU.mult, ALU.add)
                else:
                    for b_ in range(2):
                        src = ps[:, 2 * (i % 4) + b_, :].rearrange("p (k t) -> p k t", k=4)[:, :, 0:DEC]
                        dst = hT[:, 4 * b_:4 * b_ + 4, SEQ:NTOK]
                        link(TT(dst, src, modT[:, 8 + 4 * b_:12 + 4 * b_, 1:9], ALU.mult))
                        last = TT(dst, dst, modT[:, 4 * b_:4 * b_ + 4, 1:9], ALU.add)
                last.then_inc(ht_dve, 1)

            for i, (r0, rt) in enumerate(TILES):
                dve.wait_ge(ld_x[i // 3], 16 * 3)
                x_ = xn[i][0:rt]
                moments(x_, rt, var_ready, i + 1)
                dve.wait_ge(sd_ready, i + 1)
                link(V.reciprocal(rs[0:rt], sd[0:rt]))
                done(TS(x_, x_, mv[0:rt, 0:1], rs[0:rt], ALU.subtract, ALU.mult), xn_ready, i + 1)
            for n in range(MOD0):
                mod_rows(n)
            dve.wait_ge(mod_out, MOD0)
            for i in range(9):
                ht_tile(i)

            def shift(b_, o, n, mu, rows=P):
                link(TT(tmp[0:rows, 0:n], b_[:, o - 1:o - 1 + n], b_[:, o:o + n], ALU.subtract))
                return STT(out=b_[:, o:o + n], in0=tmp[0:rows, 0:n], scalar=mu, in1=b_[:, o:o + n],
                           op0=ALU.mult, op1=ALU.add)

            S0, S1 = PAD + SEQ, PAD + NTOK
            dve.wait_ge(win_out, 6)
            for b_, mu, rows in ((pwa, mu_wa, 64), (pgd, mu_gd, 96)):
                link(shift(b_, PAD + HALF, HALF, mu, rows))
                link(shift(b_, PAD, HALF, mu, rows))
                link(TT(tmp[0:rows, 0:DEC], b_[:, S1:S1 + DEC], b_[:, S0:S1], ALU.subtract))
                link(STT(out=b_[:, S0:S1], in0=tmp[0:rows, 0:DEC], scalar=mu, in1=b_[:, S0:S1], op0=ALU.mult,
                         op1=ALU.add))
            V.memset(rs, 0.0).then_inc(lora_shifted, 1)
            dve.wait_ge(lora_tanh, 2)
            done(TS(pgd[:, PAD:S1], pgd[:, PAD:S1], 0.5, 0.5, ALU.mult, ALU.add), lora_ready, 1)

            for j in range(NJ):
                dve.wait_ge(win_out, 6 + 15 * j + 9)
                for q, (b_, mu) in enumerate(((pk, MU_K), (pr, MU_R), (pv, MU_V))):
                    link(shift(b_, PAD + HALF, HALF, pcol(mu, j)))
                    link(shift(b_, PAD, HALF, pcol(mu, j)))
                    link(TT(tmp[:, 0:DEC], b_[:, S1:S1 + DEC], b_[:, S0:S1], ALU.subtract))
                    link(STT(out=psm[:, q, j, :], in0=tmp[:, 0:DEC], scalar=pcol(mu, j), in1=b_[:, S0:S1],
                             op0=ALU.mult, op1=ALU.add))
                dve.wait_ge(win_out, 6 + 15 * j + 15)
                link(V.tensor_copy(pxs[:, j, :], prec[:, S0:S1]))
                done(V.tensor_copy(pgs[:, j, :], pgate[:, S0:S1]), HV["shifted"], j + 1)
                V.memset(S[:, 0, :], 0.0).then_inc(s_zero, 1)
                for hf in range(2):
                    it = 2 * j + hf
                    n1 = it + 1
                    o = PAD + hf * HALF
                    cols = slice(o, o + HALF)
                    link(TS(xc, prec[:, o - 3:o - 3 + HALF], pcol(CW0, j), pcol(C_BIAS, j), ALU.mult, ALU.add))
                    for m in (1, 2):
                        link(STT(out=xc, in0=prec[:, o - 3 + m:o - 3 + m + HALF], scalar=pcol(CW0 + m, j), in1=xc,
                                 op0=ALU.mult, op1=ALU.add))
                    done(STT(out=xc, in0=prec[:, cols], scalar=pcol(CW3, j), in1=xc, op0=ALU.mult, op1=ALU.add),
                         HV["conv_ready"], n1)
                    dve.wait_ge(HV["ta_ready"], n1)
                    link(TS(lam, lam, -0.5 * DECAY, -0.5 * DECAY, ALU.mult, ALU.add))
                    link(TS(aa, aa, 0.5, 0.5, ALU.mult, ALU.add))
                    link(V.tensor_tensor_scan(cum, reset, lam, 0.0, ALU.mult, ALU.add))
                    done(TT(lam, cum, lam, ALU.subtract), HV["cum_ready"], n1)
                    dve.wait_ge(HV["nrm_ready"], n1)
                    link(TS(kk, kk, 1e-12, None, ALU.max))
                    link(V.reciprocal(kk, kk))
                    link(STT(out=kk, in0=pk[:, cols], scalar=pcol(K_K, j), in1=kk, op0=ALU.mult, op1=ALU.mult))
                    link(TS(tmp, aa, pcol(K_A, j), dcol(D_OKA, j), ALU.mult, ALU.add))
                    link(TT(k2, pk[:, cols], tmp, ALU.mult))
                    done(STT(out=rkp, in0=pr[:, cols], scalar=pcol(R_K, j), in1=k2, op0=ALU.mult, op1=ALU.mult),
                         HV["rkp_ready"], n1)
                    link(TT(bb, kk, aa, ALU.mult))
                    dve.wait_ge(HV["exp_ready"], n1)
                    link(STT(out=AR0, in0=kk, scalar=-1.0, in1=lam, op0=ALU.mult, op1=ALU.mult))
                    link(TT(AR1, pr[:, cols], eP, ALU.mult))
                    link(TT(bb, bb, eN, ALU.mult))
                    link(TT(k2, k2, eN, ALU.mult))
                    ends = eP.rearrange("p (c t) -> p c t", t=CHUNK)[:, :, CHUNK - 1:CHUNK].to_broadcast([P, HALF // CHUNK, CHUNK])
                    link(TT(Bh.rearrange("p (c t) -> p c t", t=CHUNK), bb.rearrange("p (c t) -> p c t", t=CHUNK), ends, ALU.mult))
                    done(TT(Kh.rearrange("p (c t) -> p c t", t=CHUNK), k2.rearrange("p (c t) -> p c t", t=CHUNK), ends, ALU.mult),
                         HV["prep_done"], n1)
                    dve.wait_ge(HV["bonus_mm"], n1)
                    done(TT(rkp, ps[:, 7, :], pv[:, cols], ALU.mult), HV["bonus_out"], n1)
                    dve.wait_ge(HV["lru_exp"], n1)
                    link(TS(ti, ti, 0.5, 0.5, ALU.mult, ALU.add))
                    link(TT(ti, ti, xc, ALU.mult))
                    link(TS(hs, t2, 1.0, None, ALU.add))
                    link(V.reciprocal(hs, hs))
                    done(STT(out=t2, in0=t2, scalar=2.0, in1=hs, op0=ALU.mult, op1=ALU.mult), HV["q_ready"], n1)
                    dve.wait_ge(HV["lru_mult"], n1)
                    link(TT(ti, ti, t2, ALU.mult))
                    link(V.tensor_tensor_scan(hs, tr, ti, lru_last[:, j, 0:1] if hf else 0.0, ALU.mult, ALU.add))
                    link(V.tensor_copy(lru_last[:, j, 0:1], hs[:, HALF - 1:HALF]))
                    dve.wait_ge(HV["gelu_ready"], n1)
                    link(TT(yT[:, NJ + j, HALF * hf:HALF * hf + HALF], hs, pgate[:, cols], ALU.mult))

                    def banks2(g, b_, w):
                        return ps[:, 4 * g + b_:4 * g + b_ + 2, 0:w]

                    def four(m):
                        return m.unsqueeze(1).to_broadcast([P, 4, P])

                    def v4(ap):
                        return ap.rearrange("p h a t -> p (h a) t")

                    for g in range(2):
                        q = grp[g]
                        gi = 2 * it + g + 1
                        dve.wait_ge(HV["gram_b"], gi)
                        done(TT(q.dtg.rearrange("p h a w t -> p (h a) (w t)"),
                                banks2(g, 0, 512).rearrange("p b (a x) -> p (b a) x", a=2),
                                mask_dt.rearrange("p w t -> p (w t)").unsqueeze(1).to_broadcast([P, 4, 256]), ALU.mult),
                             HV["dt_out"], gi)
                    for g in range(2):
                        q = grp[g]
                        gi = 2 * it + g + 1
                        dve.wait_ge(HV["gram_k"], gi)
                        done(TT(q.ak.rearrange("p h a w t -> p (h a) (w t)"),
                                banks2(g, 2, 512).rearrange("p b (a x) -> p (b a) x", a=2),
                                mask_ak.rearrange("p w t -> p (w t)").unsqueeze(1).to_broadcast([P, 4, 256]), ALU.mult),
                             HV["ak_out"], gi)
                        done(TT(v4(q.p), q.dtg[:, :, :, 0, :].rearrange("p h a t -> p (h a) t"), four(ident), ALU.add),
                             HV["p1_out"], gi)
                    for g in range(2):
                        q = grp[g]
                        gi = 2 * it + g + 1
                        dve.wait_ge(HV["gram_l"], gi)
                        src = banks2(g, 0, 256).rearrange("p b (a t) -> p b a t", a=2)
                        m4 = [m.unsqueeze(1).unsqueeze(1).to_broadcast([P, 2, 2, P]) for m in (mask_d, mask_e)]
                        link(TT(q.d, src, m4[0], ALU.mult))
                        done(TT(q.e, src, m4[1], ALU.mult), HV["de_out"], gi)
                    for mm_, out_, b_ in (("p2_mm", "p2_out", 2), ("p3_mm", "p3_out", 2), ("p4_mm", "nt_out", 2)):
                        for g in range(2):
                            gi = 2 * it + g + 1
                            dve.wait_ge(HV[mm_], gi)
                            done(TT(grp[g].p_flat, grp[g].p_flat, grp[g].bank(b_), ALU.add), HV[out_], gi)
                    for g in range(2):
                        gi = 2 * it + g + 1
                        dve.wait_ge(HV["f_mm"], gi)
                        done(V.tensor_copy(grp[g].z_flat, grp[g].bank(2)), HV["z0_out"], gi)
                    for mm_, out_, b_ in (("z1_mm", "z1_out", 2), ("z2_mm", "z2_out", 1)):
                        for g in range(2):
                            gi = 2 * it + g + 1
                            dve.wait_ge(HV[mm_], gi)
                            done(TT(grp[g].z_flat, grp[g].z_flat, grp[g].bank(b_), ALU.add), HV[out_], gi)
                    for g in range(2):
                        q = grp[g]
                        gi = 2 * it + g + 1
                        dve.wait_ge(HV["rt_mm"], gi)
                        done(TT(q.rh, AR1[:, q.c0:q.c0 + GRP], q.bank(0)[:, 0:GRP], ALU.add), HV["rh_out"], gi)
                        link(TT(q.tt, banks2(g, 2, 256).rearrange("p c (a t) -> p c a t", a=2),
                                blk_ones.unsqueeze(1).unsqueeze(1).to_broadcast([P, 2, 2, P]), ALU.mult))
                        for n in range(4):
                            t_ = q.tt[:, n % 2, n // 2, :]
                            end = q.c0 + CHUNK * n + CHUNK - 1
                            last = STT(out=t_, in0=ident, scalar=eP[:, end:end + 1], in1=t_, op0=ALU.mult, op1=ALU.add)
                        done(last, HV["tt_out"], gi)
                    for g in range(2):
                        q = grp[g]
                        for n in range(4):
                            cur = 4 * (2 * it + g) + n + 1
                            dve.wait_ge(state_mm, cur)
                            done(TT(S[:, (n + 1) % 2, :], q.bank(2 + n % 2)[:, 256:384], blk_ones, ALU.mult),
                                 state_out, cur)
                    dve.wait_ge(HV["mean_mm"], n1)
                    done(TT(Y, Y, ps[:, 0, :], ALU.subtract), HV["centred"], n1)
                    dve.wait_ge(HV["gsd_ready"], n1)
                    link(V.reciprocal(eP, eP))
                    link(TT(Y, Y, eP, ALU.mult))
                    link(TS(Y, Y, pcol(LNX_G, j), pcol(LNX_B, j), ALU.mult, ALU.add))
                    link(TT(Y, Y, rkp, ALU.add))
                    dve.wait_ge(HV["g_ready"], n1)
                    if hf:
                        link(V.tensor_copy(sfin[:, j, :], S[:, 0, :]))
                    done(TT(yT[:, j, HALF * hf:HALF * hf + HALF], Y, gg, ALU.mult), HV["half_done"], n1)

            def pb(q):
                return par[:, q, :].unsqueeze(2).to_broadcast([P, NJ, DEC])

            dve.wait_ge(ld_samp, 16 * 7)
            link(TT(s_xc, s_conv[:, :, 0, :], pb(CW0), ALU.mult))
            for m in (1, 2, 3):
                link(TT(s_kk, s_conv[:, :, m, :] if m < 3 else pxs, pb(CW0 + m), ALU.mult))
                link(TT(s_xc, s_xc, s_kk, ALU.add))
            done(TT(s_xc, s_xc, pb(C_BIAS), ALU.add), *SAMP["s_conv"])
            k_, r_, v_ = psm[:, 0], psm[:, 1], psm[:, 2]
            link(TT(s_kk, k_, pb(K_K), ALU.mult))
            done(TT(s_t, s_kk, s_kk, ALU.mult), *SAMP["s_sq"])
            dve.wait_ge(*SAMP["s_wa"])
            link(TS(s_lam, s_lam, -0.5 * DECAY, -0.5 * DECAY, ALU.mult, ALU.add))
            done(TS(s_a, s_a, 0.5, 0.5, ALU.mult, ALU.add), *SAMP["s_lam"])
            dve.wait_ge(*SAMP["s_nrm"])
            link(TS(s_t, s_t, 1e-12, None, ALU.max))
            link(V.reciprocal(s_t, s_t))
            link(TT(s_kk, s_kk, s_t, ALU.mult))
            link(TT(s_t, s_a, pb(K_A), ALU.mult))
            link(TT(s_t, s_t, der[:, D_OKA, :].unsqueeze(2).to_broadcast([P, NJ, DEC]), ALU.add))
            link(TT(s_vecs[:, 2], k_, s_t, ALU.mult))
            link(TT(s_t1, r_, pb(R_K), ALU.mult))
            done(TT(s_t1, s_t1, s_vecs[:, 2], ALU.mult), *SAMP["s_bon"])
            V.tensor_copy(s_vecs[:, 0], r_)
            V.tensor_copy(s_vecs[:, 3], v_)
            TS(s_vecs[:, 4], s_kk, -1.0, None, ALU.mult)
            dve.wait_ge(*SAMP["s_w"])
            TT(s_vecs[:, 5], s_kk, s_a, ALU.mult).then_inc(SAMP["s_vec"][0], 1)
            dve.wait_ge(*SAMP["s_lexp"])
            link(TS(s_ti, s_ti, 0.5, 0.5, ALU.mult, ALU.add))
            link(TT(s_ti, s_ti, s_xc, ALU.mult))
            link(TS(s_gl, s_t2, 1.0, None, ALU.add))
            link(V.reciprocal(s_gl, s_gl))
            done(STT(out=s_t2, in0=s_t2, scalar=2.0, in1=s_gl, op0=ALU.mult, op1=ALU.mult), *SAMP["s_q"])
            dve.wait_ge(*SAMP["s_mult"])
            link(TT(s_ti, s_ti, s_t2, ALU.mult))
            link(TT(s_hs, s_tr, s_lru0, ALU.mult))
            link(TT(s_hs, s_hs, s_ti, ALU.add))
            link(V.tensor_copy(lru_last[:, :, 1:9], s_hs))
            dve.wait_ge(*SAMP["s_gelu"])
            link(TT(yT[:, NJ:2 * NJ, SEQ:NTOK], s_hs, s_mu, ALU.mult))
            dve.wait_ge(*SAMP["s_turn"])
            link(V.tensor_copy(s_qt[:, 0:512], ps[0:32, 0, :]))
            done(V.tensor_copy(s_qt[:, 512:768], ps[0:32, 1, 0:256]), *SAMP["s_vrow"])
            dve.wait_ge(*SAMP["s_bonmm"])
            link(TT(s_bon, ps[:, 6, 0:SN].rearrange("p (j b) -> p j b", j=NJ), v_, ALU.mult))
            dve.wait_ge(HV["s_rows"], 16 * 6)

            def krow(n):
                return s_row[:, n, :].unsqueeze(1).to_broadcast([P, 32, HEAD])

            def vrow(x_):
                return x_.unsqueeze(2).to_broadcast([P, 32, HEAD])

            link(TT(s_T, s_S, krow(3), ALU.mult))
            link(V.tensor_reduce(s_sa, s_T, AX_X, ALU.add))
            link(TT(s_S, s_S, krow(1), ALU.mult))
            link(TT(s_T, vrow(s_sa), krow(4), ALU.mult))
            link(TT(s_S, s_S, s_T, ALU.add))
            link(TT(s_T, vrow(s_vr), krow(2), ALU.mult))
            link(TT(s_S, s_S, s_T, ALU.add))
            link(TT(s_T, s_S, krow(0), ALU.mult))
            done(V.tensor_reduce(s_yr, s_T, AX_X, ALU.add), *SAMP["s_y"])
            dve.wait_ge(*SAMP["s_yturn"])
            done(V.tensor_copy(s_y.rearrange("p j b -> p (j b)"), ps[:, 2, 0:SN]), *SAMP["s_yc"])
            dve.wait_ge(*SAMP["s_mean"])
            done(TT(s_y, s_y, ps[:, 3, 0:SN].rearrange("p (j b) -> p j b", j=NJ), ALU.subtract), *SAMP["s_cent"])
            dve.wait_ge(*SAMP["s_gsd"])
            link(V.reciprocal(s_t1, s_t1))
            link(TT(s_y, s_y, s_t1, ALU.mult))
            link(TT(s_y, s_y, pb(LNX_G), ALU.mult))
            link(TT(s_y, s_y, pb(LNX_B), ALU.add))
            link(TT(s_y, s_y, s_bon, ALU.add))
            done(TT(yT[:, 0:NJ, SEQ:NTOK], s_y, s_g, ALU.mult), *SAMP["s_done"])

            dve.wait_ge(outs, 16 * 9)
            def rows_out(k):
                dve.wait_ge(row_mm, k + 1)
                c_ = slice(P * (k % 8), P * (k % 8) + P)
                V.tensor_copy(rowb[:, k // 8, c_], ps[:, 5 + k % 2, 0:P])
                V.tensor_copy(rows_s[0:DEC, k // 8, c_], ps[0:DEC, 5 + k % 2, P:2 * P]).then_inc(row_out, 1)

            for k in range(4 * KC):
                if k >= 8:
                    dve.wait_ge(row_mm, k - 7)
                done(TS(diag[:, k % 8, :], ident, modT[:, ROWS2[k // 8] + k % 8, 0:1], None, ALU.mult),
                     row_diag, k + 1)
                if k >= 1:
                    rows_out(k - 1)
            rows_out(4 * KC - 1)
            dve.wait_ge(row_out, 4 * KC)

            def norm(dst, src, rt, s_sd, n):
                dve.wait_ge(s_sd, n)
                link(V.reciprocal(rs[0:rt], sd[0:rt]))
                return TS(dst, src, mv[0:rt, 0:1], rs[0:rt], ALU.subtract, ALU.mult)

            dve.wait_ge(ld_late, 16 * 6)
            for i, (r0, rt) in enumerate(TILES):
                gb = (rowb if i < 8 else rows_s)[:, 0, :]
                dve.wait_ge(wo_mm, 2 * i + 2)
                z_ = zz[0:rt]
                done(TT(z_, ps[0:rt, 2 * (i % 2):2 * (i % 2) + 2, :].rearrange("p b x -> p (b x)"), gb[0:rt], ALU.mult),
                     wo_out, i + 1)
                dve.wait_ge(ld_x2[i % 2], 16 * (i // 2 + 1))
                link(STT(out=z_, in0=xr2[0:rt, i % 2, :], scalar=ALPHA, in1=z_, op0=ALU.mult, op1=ALU.add))
                moments(z_, rt, var_ready, 9 + 2 * i + 1)
                x_ = x1[0:rt, i, :]
                link(norm(x_, z_, rt, sd_ready, 9 + 2 * i + 1))
                link(TT(x_, x_, lnr[0:rt, 0, :], ALU.mult))
                link(TT(x_, x_, lnr[0:rt, 1, :], ALU.add))
                moments(x_, rt, var_ready, 9 + 2 * i + 2)
                if i >= 2:
                    dve.wait_ge(h2_turned, i - 1)
                    dve.wait_ge(h2_stored[i % 2], 16 * (i // 2))
                done(norm(n2[0:rt, i % 2, :], x_, rt, sd_ready, 9 + 2 * i + 2), n2_ready, i + 1)

            link(V.memset(lgt, 0.0))
            dve.wait_ge(router_mm, 9)
            for i, (r0, rt) in enumerate(TILES):
                link(TT(lgt[0:rt, i, :], ps[0:rt, 6, 20 * i:20 * i + 20], brt[0:rt], ALU.add))

            def b4(x_):
                return x_.unsqueeze(2).to_broadcast([P, 9, 4])

            def first_of_max(o_, eq, left):
                link(V.memset(left, 1.0))
                for m in range(4):
                    link(TT(o_[:, :, m], eq[:, :, m], left, ALU.mult))
                    link(TT(left, left, o_[:, :, m], ALU.subtract))

            gl = lgt[:, :, 0:4]
            e_, oh, el, f1, f2, t4, c4, eq = rt_a
            gmax, gsum, em, ee, left, w1, w2, pg = rt_s
            link(V.tensor_reduce(gmax, gl, AX_X, ALU.max))
            done(TT(e_, gl, b4(gmax), ALU.subtract), lg_ready, 1)
            link(TT(eq, gl, b4(gmax), ALU.is_equal))
            first_of_max(oh, eq, left)
            dve.wait_ge(ex_ready, 1)
            link(V.tensor_reduce(gsum, e_, AX_X, ALU.add))
            link(V.reciprocal(pg, gsum))
            for m in range(4):
                src = lgt[:, :, 4 + 4 * m:8 + 4 * m]
                om = b4(oh[:, :, m])
                if m == 0:
                    link(TT(el, src, om, ALU.mult))
                else:
                    link(TT(t4, src, om, ALU.mult))
                    link(TT(el, el, t4, ALU.add))
            link(V.tensor_reduce(em, el, AX_X, ALU.max))
            link(TT(eq, el, b4(em), ALU.is_equal))
            first_of_max(f1, eq, left)
            link(TS(t4, f1, -1e30, None, ALU.mult))
            link(TT(el, el, t4, ALU.add))
            link(V.tensor_reduce(w1, el, AX_X, ALU.max))
            link(TT(eq, el, b4(w1), ALU.is_equal))
            first_of_max(f2, eq, left)
            done(TT(ee, w1, em, ALU.subtract), lg2_ready, 1)
            dve.wait_ge(ex2_ready, 1)
            link(TS(w1, ee, 1.0, None, ALU.add))
            link(V.reciprocal(w1, w1))
            link(TT(w1, w1, pg, ALU.mult))
            link(TT(w2, w1, ee, ALU.mult))
            link(TT(f1, f1, b4(valid), ALU.mult))
            link(TT(f2, f2, b4(valid), ALU.mult))
            for m in range(4):
                link(TT(e1[:, :, 4 * m:4 * m + 4], f1, b4(oh[:, :, m]), ALU.mult))
                link(TT(e2[:, :, 4 * m:4 * m + 4], f2, b4(oh[:, :, m]), ALU.mult))
            done(TT(asg, e1, e2, ALU.add), assigned, 1)
            dve.wait_ge(rank_mm, 1)
            tot = ps[:, 1, 0:9 * NEXP].rearrange("p (i e) -> p i e", i=9)
            link(V.memset(carry[:, 0, :], 0.0))
            for i in range(9):
                link(TT(carry[:, i + 1, :], carry[:, i, :], tot[:, i, :], ALU.add))
            link(TT(rank, carry[:, 0:9, :], ps[:, 0, 0:9 * NEXP].rearrange("p (i e) -> p i e", i=9), ALU.add))
            link(V.memset(ntile, 0.0))
            for m in range(9):
                link(STT(out=ntile, in0=carry[:, 9, :], scalar=float(P * m), in1=ntile, op0=ALU.is_gt, op1=ALU.add))
            link(V.tensor_tensor_scan(tend, ones[:, 0:NEXP], ntile, 0.0, ALU.mult, ALU.add))
            link(TT(tbase, tend, ntile, ALU.subtract))
            link(TS(tbase, tbase, float(P), None, ALU.mult))
            link(TT(rank, rank, tbase.unsqueeze(1).to_broadcast([P, 9, NEXP]), ALU.add))
            for a, (e_a, pos, pp) in enumerate(((e1, pos1, pp1), (e2, pos2, pp2))):
                link(TT(e_a, e_a, rank, ALU.mult))
                link(V.tensor_reduce(pos, e_a, AX_X, ALU.add))
                link(V.tensor_copy(posu[:, a, :], pos))
                link(TT(ge, pos.unsqueeze(2).to_broadcast([P, 9, STEPS + 1]),
                        iota_t.unsqueeze(1).to_broadcast([P, 9, STEPS + 1]), ALU.is_ge))
                link(V.tensor_reduce(psn, ge, AX_X, ALU.add))
                link(TS(psn, psn, float(-P), float(P), ALU.mult, ALU.add))
                link(TT(pp, pos, psn, ALU.add))
                link(TT(wt[:, a], ge[:, :, 0:STEPS], ge[:, :, 1:STEPS + 1], ALU.subtract))
                link(TT(wt[:, a], wt[:, a], tok_id.unsqueeze(2).to_broadcast([P, 9, STEPS]), ALU.mult))
            link(TT(tcmp, iota_s.unsqueeze(2).to_broadcast([P, STEPS, NEXP]),
                    tend.unsqueeze(1).to_broadcast([P, STEPS, NEXP]), ALU.is_ge))
            link(V.tensor_reduce(texp_f, tcmp, AX_X, ALU.add))
            link(TS(texp_f, texp_f, float(NEXP - 1), None, ALU.min))
            link(V.tensor_copy(texp, texp_f))
            for n in range(18):
                if n >= 4:
                    dve.wait_ge(hot_used, n - 3)
                pp = (pp1, pp2)[n // 9]
                TS(uu[:, n % 4, :], iota_p, pp[:, n % 9:n % 9 + 1], None, ALU.is_equal).then_inc(hot_ready, 1)
            dve.wait_ge(hot_used, 18)
            done(V.tensor_copy(perm, ps[:, 2, 0:STEPS]), route_ready, 1)

            def dve_hid(s, b):
                dve.wait_ge(silu_out, s + 1)
                V.tensor_tensor(hid[:, b, :], sil, ps[:, 2 + b, DEXP:2 * DEXP], ALU.mult).then_inc(hid_out, 1)

            def dve_ys(s, i, b, first):
                dve.wait_ge(dn_mm, s + 1)
                if not first:
                    dve.wait_ge(slot_stored[b], 16 * i)
                V.tensor_copy(ys[:, b, :], ps[:, 6:8, :].rearrange("p b x -> p (b x)")).then_inc(ys_out, 1)

            dve_hid(0, 0)
            dve_hid(1, 1)
            dve_ys(0, 0, 0, True)
            dve_hid(2, 0)
            dve_ys(1, 0, 1, True)
            with dve.Fori(1, STEPS // 2 - 1) as i:
                dve_hid(2 * i + 1, 1)
                dve_ys(2 * i, i, 0, False)
                dve_hid(2 * i + 2, 0)
                dve_ys(2 * i + 1, i, 1, False)
            i = STEPS // 2 - 1
            dve_hid(2 * i + 1, 1)
            dve_ys(2 * i, i, 0, False)
            dve_ys(2 * i + 1, i, 1, False)

            for i, (r0, rt) in enumerate(TILES):
                gb = (rowb if i < 8 else rows_s)[:, 3, :]
                z_ = fz[0:rt, i % 2, :]
                if i >= 2:
                    dve.wait_ge(y_stored[i % 2], 16 * (i // 2))
                dve.wait_ge(ld_yg[i % 2], 32 * (i // 2 + 1))
                link(TS(z_, yg[i % 2][0:rt, 0, :], w1[0:rt, i:i + 1], None, ALU.mult))
                done(STT(out=z_, in0=yg[i % 2][0:rt, 1, :], scalar=w2[0:rt, i:i + 1], in1=z_, op0=ALU.mult, op1=ALU.add),
                     yg_used, i + 1)
                link(TT(z_, z_, gb[0:rt], ALU.mult))
                link(STT(out=z_, in0=x1[0:rt, i, :], scalar=ALPHA, in1=z_, op0=ALU.mult, op1=ALU.add))
                moments(z_, rt, var_ready, 27 + i + 1)
                link(norm(z_, z_, rt, sd_ready, 27 + i + 1))
                link(TT(z_, z_, lnr[0:rt, 2, :], ALU.mult))
                done(TT(z_, z_, lnr[0:rt, 3, :], ALU.add), y_ready, i + 1)


def kernel(x_prompt, x_sample, c_prompt, c_sample, state_wkv, state_shift, state_conv, state_lru,
           w_ada, b_ada, w_in, mu_shift, w0, w_decay_up, a0, w_a_up, w_g_up, k_k, k_a, r_k,
           lnx_gain, lnx_bias, conv_w, conv_b, w_rgate, b_rgate, w_igate, b_igate, lru_lambda,
           w_out, ln1_gain, ln1_bias, w_router_group, b_router_group, w_router_expert,
           b_router_expert, w_exp_gate, w_exp_up, w_exp_down, ln2_gain, ln2_bias):
    import concourse.bacc as _bacc
    from concourse.bass_utils import run_bass_kernel_spmd as _run

    def tiles(v):
        return np.asarray(v).reshape(-1, P).T

    def rows(w):
        w = np.asarray(w)
        return w.reshape(KC, P, -1).transpose(1, 0, 2)

    x = np.concatenate([np.asarray(x_prompt)[0], np.asarray(x_sample)[:, 0]], 0)
    c = np.concatenate([np.asarray(c_prompt), np.asarray(c_sample)], 0)
    wi = np.asarray(w_in)[0]
    ca = 512
    sh = 3 * ca + 160
    at = {"k": ca, "r": 0, "v": 2 * ca, "rec": sh + ca, "gate": sh}
    mu = np.asarray(mu_shift)[0]
    st = np.asarray(state_wkv)[0].reshape(DEC, NJ, 2, HEAD, HEAD)
    d = {
        "x_all": x,
        "c_t": c.reshape(9, KC, P).transpose(2, 1, 0),
        "shift_t": np.asarray(state_shift)[0].reshape(DEC, KC, P).transpose(2, 1, 0),
        "wkv0": st.transpose(1, 0, 2, 3, 4).reshape(P, 2048),
        "conv0": np.asarray(state_conv)[0].reshape(DEC, 3, NJ, P).transpose(3, 2, 1, 0),
        "lru0": np.asarray(state_lru)[0].reshape(DEC, NJ, P).transpose(2, 1, 0),
        "state_conv": np.asarray(state_conv)[0],
        "w_ada": np.asarray(w_ada)[0].reshape(KC, P, 24, 256).transpose(2, 1, 0, 3).reshape(24, P, 2048),
        "b_ada": tiles(b_ada[0]),
        "w_in": np.stack([rows(wi[:, at[q] + P * j:at[q] + P * j + P]).reshape(P, KC * P)
                          for j in range(NJ) for q in ("k", "r", "v", "rec", "gate")]),
        "w_lo": rows(wi[:, 3 * ca:sh]).reshape(P, KC * 160),
        "prm": np.stack([tiles(v) for v in (
            mu[0:ca], mu[ca:2 * ca], mu[2 * ca:3 * ca], w0[0], a0[0], k_k[0], k_a[0], np.asarray(r_k)[0].reshape(-1),
            lnx_gain[0], lnx_bias[0], conv_w[0][0], conv_w[0][1], conv_w[0][2], conv_w[0][3], conv_b[0],
            b_rgate[0], b_igate[0], lru_lambda[0])], 1),
        "mu_lo": mu[3 * ca:].reshape(160, 1),
        "w_wa_up": np.concatenate([np.asarray(w_decay_up)[0], np.asarray(w_a_up)[0]], 0),
        "w_g_up": np.asarray(w_g_up)[0],
        "w_rg": np.asarray(w_rgate)[0].reshape(NJ, P, HEAD),
        "w_ig": np.asarray(w_igate)[0].reshape(NJ, P, HEAD),
        "w_out": np.asarray(w_out)[0].reshape(KC, P, D_MODEL),
        "ln_rows": np.stack([np.asarray(v)[0] for v in (ln1_gain, ln1_bias, ln2_gain, ln2_bias)]),
        "w_rt": rows(np.concatenate([np.asarray(w_router_group)[0], np.asarray(w_router_expert)[0]], 1)),
        "b_rt": np.concatenate([np.asarray(b_router_group)[0], np.asarray(b_router_expert)[0]]).reshape(1, 20),
        "w_gu": np.stack([np.asarray(w_exp_gate)[0], np.asarray(w_exp_up)[0]], 1)
                  .reshape(NEXP, 2, KC, P, DEXP).transpose(0, 3, 2, 1, 4).reshape(NEXP, P, 4096),
        "w_dn": np.asarray(w_exp_down)[0].reshape(NEXP, 2, P, D_MODEL).transpose(0, 2, 1, 3).reshape(NEXP, P, 2048),
    }
    outs = {"y_all": (NTOK, D_MODEL), "wkvp_o": (NJ, P, P), "wkvs_o": (P, 2048), "shift_o": (P, KC, 9),
            "conv_o": (NJ, P, 11), "convs_o": (DEC, 2, 512), "lru_o": (P, NJ, 9)}
    nc = _bacc.Bacc("TRN2", target_bir_lowering=False, num_devices=1)
    arrays, args = {}, {}
    for name, a in d.items():
        a = np.ascontiguousarray(a)
        arrays[f"in_{name}"] = a
        args[name] = nc.dram_tensor(f"in_{name}", a.shape, mybir.dt.from_np(a.dtype), kind="ExternalInput").ap()
    for name, shape in outs.items():
        args[name] = nc.dram_tensor(f"out_{name}", shape, F32, kind="ExternalOutput").ap()
    build(nc, **args)
    r = _run(nc, [arrays], core_ids=[0]).results[0]
    o = {name: r[f"out_{name}"] for name in outs}
    y = o["y_all"]
    sb_ = o["wkvp_o"].reshape(NJ, 2, HEAD, 2, HEAD)
    wkv_p = np.stack([sb_[:, q, :, q, :] for q in range(2)], 1).transpose(0, 1, 3, 2).reshape(1, 1, 8, HEAD, HEAD)
    wkv_s = o["wkvs_o"].reshape(NJ, DEC, 2, HEAD, HEAD).transpose(1, 0, 2, 3, 4).reshape(1, DEC, 8, HEAD, HEAD)
    shf = o["shift_o"].transpose(2, 1, 0).reshape(9, D_MODEL)
    cv = o["conv_o"].transpose(2, 0, 1).reshape(11, 512)
    conv_s = np.concatenate([o["convs_o"], cv[3:, None, :]], 1)
    lr = o["lru_o"].transpose(2, 1, 0).reshape(9, 512)
    cc = np.ascontiguousarray
    return (cc(y[None, :SEQ]), cc(y[SEQ:, None]), cc(wkv_p), cc(shf[None, 0:1]), cc(cv[None, None, 0:3]),
            cc(lr[None, 0:1]), cc(wkv_s), cc(shf[None, 1:]), cc(conv_s[None]), cc(lr[None, 1:]))
```

```python
from contextlib import ExitStack

import numpy as np
import concourse.bass as bass
from concourse import mybir

ALU = mybir.AluOpType
ACT = mybir.ActivationFunctionType
F32 = mybir.dt.float32
I32 = mybir.dt.int32
U32 = mybir.dt.uint32
AX_X = mybir.AxisListType.X

P = 128
D_MODEL = 1024
KC = D_MODEL // P
SEQ = 1024
DEC = 8
NTOK = SEQ + DEC
NCOL = NTOK + DEC
NJ = 4
HEAD = 64
CHUNK = 64
HALF = 512
GRP = 256
PAD = 3
NEXP = 16
DEXP = 256
ALPHA = 2 ** 0.25
DECAY = float(np.exp(-0.5))
LN_EPS = 1e-5
GN_EPS = 64e-5
COLS = [(0, 348), (348, 348), (696, 344)]
MOD0 = 8
STEPS = 32
TILES = [(i * P, P) for i in range(SEQ // P)] + [(SEQ, DEC)]
(MU_R, MU_K, MU_V, W0, A0, K_K, K_A, R_K, LNX_G, LNX_B, CW0, CW1, CW2, CW3, C_BIAS, B_RG, B_IG,
 LAM) = range(18)
NPRM = 18
ARENA = 53000


class Signal:

    def __init__(self, ctx, nc, name):
        self.sem = ctx.enter_context(nc.semaphore(name))
        self.n = 0

    def on(self, ins, k=1):
        ins.then_inc(self.sem, k)
        self.n += k


def build(nc, x_all, c_t, shift_t, wkv0, conv0, lru0, state_conv, w_ada, b_ada, w_in, w_lo, prm, mu_lo,
          w_wa_up, w_g_up, w_rg, w_ig, w_out, ln_rows, w_rt, b_rt, w_gu, w_dn,
          y_all, wkvp_o, wkvs_o, shift_o, conv_o, convs_o, lru_o):
    q_scr = nc.dram_tensor("q_scr", (6, 32, P), F32, kind="Internal").ap()
    y_scr = nc.dram_tensor("y_scr", (32, P), F32, kind="Internal").ap()
    mod_scr = nc.dram_tensor("mod_scr", (4, 9, D_MODEL), F32, kind="Internal").ap()
    h2_scr = nc.dram_tensor("h2_scr", (NTOK, D_MODEL), F32, kind="Internal").ap()
    slot_scr = nc.dram_tensor("slot_scr", (STEPS * P, D_MODEL), F32, kind="Internal").ap()

    with ExitStack() as ctx:
        def sb(name, shape, stack=ctx):
            return stack.enter_context(nc.sbuf_tensor(name, shape, F32))

        def sem(name):
            return ctx.enter_context(nc.semaphore(name))

        ps = ctx.enter_context(nc.psum_tensor("ps", [P, 8, 512], F32))

        arena = ctx.enter_context(nc.sbuf_tensor("arena", [P, ARENA], F32))
        at = [0]

        def take(n):
            at[0] += n
            assert at[0] <= ARENA
            return arena[:, at[0] - n:at[0]]

        def v3(ap, a):
            return ap.rearrange("p (a b) -> p a b", a=a)

        hT = v3(take(KC * NCOL), KC)
        yT_at = at[0]
        yT = v3(take(KC * NTOK), KC)
        modT = v3(take(48 * 9), 48)
        ident = take(P)
        blk_ones = take(P)
        blk_mean = take(P)
        ones = take(P)
        mask_dt = v3(take(2 * P), 2)
        mask_ak = v3(take(2 * P), 2)
        mask_d = take(P)
        mask_e = take(P)
        before = take(P)
        iota_p = take(P)
        iota_s = take(STEPS)
        iota_t = take(STEPS + 1)
        falling = take(4)
        diff_s = take(DEC)
        tok_id = take(9)
        valid = take(9)
        par = v3(take(NPRM * NJ), NPRM)
        der = v3(take(12 * NJ), 12)
        mu_wa = take(1)[0:64]
        mu_gd = take(1)[0:96]
        bada = take(48)
        eps = take(2)
        S = v3(take(2 * P), 2)
        sfin = v3(take(NJ * P), NJ)
        lru_last = v3(take(NJ * 9), NJ)
        st = v3(take(12), 2)
        mv = take(2)
        sd = take(1)
        rs = take(1)
        psm = take(3 * NJ * DEC).rearrange("p (q j b) -> p q j b", q=3, j=NJ)
        pgs = v3(take(NJ * DEC), NJ)
        pxs = v3(take(NJ * DEC), NJ)
        base = at[0]

        ld_const = sem("ld_const")
        ld_cs = sem("ld_cs")
        ld_prev = sem("ld_prev")
        ld_samp = sem("ld_samp")
        ld_ada = [sem(f"ld_ada{i}") for i in range(2)]
        ld_x = [sem(f"ld_x{i}") for i in range(3)]
        ld_win = [sem(f"ld_win{i}") for i in range(3)]
        ld_lo = sem("ld_lo")
        consts_ready = sem("consts_ready")
        silu_ready = sem("silu_ready")
        mod_mm = sem("mod_mm")
        mod_out = sem("mod_out")
        var_ready = sem("var_ready")
        sd_ready = sem("sd_ready")
        xn_ready = sem("xn_ready")
        xn_turned = sem("xn_turned")
        ht_dve = sem("ht_dve")
        ht_act = sem("ht_act")
        params_ready = sem("params_ready")
        par_tanh = sem("par_tanh")
        win_mm = sem("win_mm")
        win_out = sem("win_out")
        lora_shifted = sem("lora_shifted")
        lora_tanh = sem("lora_tanh")
        lora_ready = sem("lora_ready")
        outs = sem("outs")

        def names(*ns):
            return {n: sem(n) for n in ns}

        h = names("up_mm", "gate_mm", "norm_mm", "bonus_mm", "mean_mm", "var_mm",
                  "ta_ready", "sq_ready", "nrm_ready", "exp_ready", "gates_tanh",
                  "lru_exp", "lru_mult", "conv_ready", "cum_ready", "q_ready",
                  "rkp_ready", "prep_done", "shifted", "bonus_out", "centred", "ysq_ready", "gsd_ready", "half_done")
        g_ = names("gram_b", "gram_k", "gram_l", "turned", "akv_mm", "d2_mm", "p2_mm", "p3_mm", "p4_mm",
                   "f_mm", "z1_mm", "z2_mm", "rt_mm",
                   "dt_out", "ak_out", "de_out", "tok_out", "akv_out", "d2_out", "d4_out", "d8_out",
                   "p1_out", "p2_out", "p3_out", "nt_out", "f_out", "z0_out", "f2_out", "z1_out",
                   "z2_out", "rh_out", "tt_out", "y_out")
        state_mm = sem("state_mm")
        state_out = sem("state_out")
        s_zero = sem("s_zero")
        SAMP = {}
        for who, steps in (("pe", ("s_up", "s_norm", "s_gates", "s_bonmm", "s_turn", "s_yturn", "s_mean", "s_var")),
                           ("act", ("s_wa", "s_nrm", "s_w", "s_lexp", "s_mult", "s_gelu", "s_sqr", "s_gsd")),
                           ("dve", ("s_conv", "s_sq", "s_lam", "s_bon", "s_vec", "s_q", "s_vrow", "s_y", "s_yc",
                                    "s_cent", "s_done"))):
            steps_done = sem(f"sample_steps_{who}")
            SAMP.update({n: (steps_done, i + 1) for i, n in enumerate(steps)})
        samp = names("s_stored", "s_rows", "s_ystored", "s_yrow")
        ld_late = sem("ld_late")
        ld_wout = sem("ld_wout")
        ld_x2 = [sem(f"ld_x2{i}") for i in range(2)]
        row_mm = sem("row_mm")
        row_out = sem("row_out")
        row_stored = sem("row_stored")
        wo_mm = sem("wo_mm")
        wo_out = sem("wo_out")
        n2_ready = sem("n2_ready")
        h2_ready = sem("h2_ready")
        h2_stored = [sem(f"h2_stored{i}") for i in range(2)]
        h2_turned = sem("h2_turned")
        h2t_out = sem("h2t_out")
        router_mm = sem("router_mm")
        lg_ready = sem("lg_ready")
        ex_ready = sem("ex_ready")
        lg2_ready = sem("lg2_ready")
        ex2_ready = sem("ex2_ready")
        assigned = sem("assigned")
        rank_mm = sem("rank_mm")
        hot_ready = sem("hot_ready")
        hot_used = sem("hot_used")
        route_ready = sem("route_ready")
        ld_gu = [sem(f"ld_gu{i}") for i in range(2)]
        ld_dn = [sem(f"ld_dn{i}") for i in range(2)]
        ld_xg = [sem(f"ld_xg{i}") for i in range(2)]
        xg_turned = sem("xg_turned")
        xgt_out = sem("xgt_out")
        gu_mm = sem("gu_mm")
        silu_out = sem("silu_out")
        hid_out = sem("hid_out")
        hid_turned = sem("hid_turned")
        hidt_out = sem("hidt_out")
        dn_mm = sem("dn_mm")
        ys_out = sem("ys_out")
        slot_stored = [sem(f"slot_stored{i}") for i in range(2)]
        ld_yg = [sem(f"ld_yg{i}") for i in range(2)]
        yg_used = sem("yg_used")
        y_ready = sem("y_ready")
        y_first = sem("y_first")
        y_scale = sem("y_scale")
        y_normed = sem("y_normed")
        y_stored = sem("y_stored")
        chain_v = Signal(ctx, nc, "chain_v")
        chain_a = Signal(ctx, nc, "chain_a")
        chain_p = Signal(ctx, nc, "chain_p")

        pk, pr, pv, prec = (take(PAD + NCOL) for _ in range(4))
        pwa = take(PAD + NCOL)[0:64]
        pgd = take(PAD + NCOL)[0:96]
        win = v3(take(3 * KC * P), 3)
        wa_up = take(512)[0:64]
        g_up = take(512)[0:96]
        rg = v3(take(NJ * P), NJ)
        ig = v3(take(NJ * P), NJ)
        reset = take(HALF)
        work = take(18 * HALF)
        tmp, Y = work[:, 0:HALF], work[:, HALF:2 * HALF]
        kept, ARs = [], []
        for n in range(2):
            o = (2 + 8 * n) * HALF
            kept.append([work[:, o + i * HALF:o + (i + 1) * HALF] for i in range(8)])
            ARs.append(work[:, o:o + 2 * HALF].rearrange("p (w t) -> p w t", w=2))
        GB = 5888
        grpb = take(2 * GB)
        gbuf = [grpb[:, i * HALF:(i + 1) * HALF] for i in range(22)]
        lru_bufs = [gbuf[5 * n:5 * n + 5] for n in range(2)]
        prep_bufs = [gbuf[10 + 6 * n:16 + 6 * n] for n in range(2)]
        wlo = grpb[:, 4096:4096 + KC * 160].rearrange("p (k m) -> p k m", k=KC)

        class Grp:
            def __init__(self, g):
                o = g * GB
                self.c0 = g * GRP
                self.b = 4 * g

                def take(n):
                    nonlocal o
                    o += n
                    return grpb[:, o - n:o]
                self.dtg = take(1024).rearrange("p (h a w t) -> p h a w t", h=2, a=2, w=2)
                self.ak = take(1024).rearrange("p (h a w t) -> p h a w t", h=2, a=2, w=2)
                self.ab_flat = take(1024)
                self.a = self.ab_flat[:, 0:512].rearrange("p (h a t) -> p h a t", h=2, a=2)
                self.bt = self.ab_flat[:, 512:1024].rearrange("p (h a t) -> p h a t", h=2, a=2)
                d = take(512)
                self.d = d.rearrange("p (h a t) -> p h a t", h=2, a=2)
                self.tt = d.rearrange("p (c a t) -> p c a t", c=2, a=2)
                self.e = take(512).rearrange("p (h a t) -> p h a t", h=2, a=2)
                self.p_flat = take(512)
                self.p = self.p_flat.rearrange("p (h a t) -> p h a t", h=2, a=2)
                self.z_flat = take(512)
                self.z = self.z_flat.rearrange("p (w a h t) -> p w a h t", w=2, a=2, h=2)
                self.zt = self.z_flat.rearrange("p (w a t) -> p w a t", w=2, a=2)
                self.vb = take(512)
                self.vtok = self.vb[:, 0:256].rearrange("p (a t) -> p a t", a=2)
                self.btok = self.vb[:, 256:512].rearrange("p (a t) -> p a t", a=2)
                self.kflat = take(256)
                self.ktok = self.kflat.rearrange("p (a t) -> p a t", a=2)
                self.rh = self.p_flat[:, 0:256]

            def bank(self, i):
                return ps[:, self.b + i, :]
        grp = [Grp(0), Grp(1)]

        ada = [grpb[:, 2048 * i:2048 * (i + 1)].rearrange("p (k m) -> p k m", k=KC) for i in range(2)]
        xn = ([work[:, D_MODEL * i:D_MODEL * (i + 1)] for i in range(5)] +
              [grpb[:, GB + D_MODEL * i:GB + D_MODEL * (i + 1)] for i in range(4)])
        cs = grpb[:, 22 * HALF:22 * HALF + 72].rearrange("p (k b) -> p k b", k=KC)
        csg = grpb[:, 22 * HALF + 72:22 * HALF + 144].rearrange("p (k b) -> p k b", k=KC)

        at[0] = base
        x1 = v3(take(9 * D_MODEL), 9)
        rowb = v3(take(4 * D_MODEL), 4)
        lgt = v3(take(9 * 20), 9)
        rt_a = [v3(take(9 * 4), 9) for _ in range(8)]
        rt_s = [take(9) for _ in range(8)]
        pos1, pos2, pp1, pp2, psn = (take(9) for _ in range(5))
        posu = v3(take(18).bitcast(U32), 2)
        e1 = v3(take(9 * NEXP), 9)
        e2 = v3(take(9 * NEXP), 9)
        asg = v3(take(9 * NEXP), 9)
        rank = v3(take(9 * NEXP), 9)
        carry = v3(take(10 * NEXP), 10)
        ntile, tend, tbase = (take(NEXP) for _ in range(3))
        texp_f = take(STEPS)
        texp = take(STEPS).bitcast(I32)
        perm = take(STEPS).bitcast(U32)
        wrt = v3(take(KC * 20), KC)
        brt = take(20)
        lnr = v3(take(4 * D_MODEL), 4)
        rows_at = at[0]
        rows_s = v3(take(4 * D_MODEL), 4)
        late = at[0]
        xr2 = v3(take(2 * D_MODEL), 2)
        n2 = v3(take(2 * D_MODEL), 2)
        h2t = v3(take(KC * P), KC)
        wout = v3(arena[:, 0:KC * D_MODEL], KC)

        s_Sf = arena[:, rows_at:rows_at + 2048]
        s_S = s_Sf.rearrange("p (v k) -> p v k", v=32)
        s_T = arena[:, rows_at + 2048:rows_at + 4096].rearrange("p (v k) -> p v k", v=32)
        SN = NJ * DEC
        sq_ = [take(SN).rearrange("p (j b) -> p j b", j=NJ) for i in range(15)]
        (s_lam, s_a, s_kk, s_t, s_t1, s_g, s_bon, s_y, s_xc, s_tr, s_ti, s_t2, s_hs, s_gl, s_mu) = sq_
        s_vflat = take(6 * SN)
        s_vecs = s_vflat.rearrange("p (q j b) -> p q j b", q=6, j=NJ)
        s_qt = take(6 * P)[0:32]
        s_row = take(5 * HEAD).rearrange("p (q k) -> p q k", q=5)
        s_vr, s_sa, s_yr = (take(32) for _ in range(3))
        s_yrow = take(P)[0:32]
        s_conv = arena[:, KC * D_MODEL:KC * D_MODEL + 3 * SN].rearrange("p (j r b) -> p j r b", j=NJ, r=3)
        s_lru0 = arena[:, KC * D_MODEL + 3 * SN:KC * NCOL].rearrange("p (j b) -> p j b", j=NJ)
        mod_rows_sb = take(4 * P)[0:9 * KC]
        at[0] = late
        ge = take(9 * (STEPS + 1)).rearrange("p (i s) -> p i s", i=9)
        wt = take(2 * 9 * STEPS).rearrange("p (a i s) -> p a i s", a=2, i=9)
        ge2 = take(9 * (STEPS + 1)).rearrange("p (i s) -> p i s", i=9)
        psn2 = take(9)
        pick = take(9 * NEXP)
        uu = v3(take(9 * P), 9)
        tcmp = v3(take(STEPS * NEXP), STEPS)
        at[0] = late
        exgu = [v3(arena[:, yT_at + 4096 * b:yT_at + 4096 * (b + 1)], KC) for b in range(2)]
        exdn = [v3(arena[:, 2048 * b:2048 * (b + 1)], 2) for b in range(2)]
        xg = v3(take(2 * D_MODEL), 2)
        xgt = [v3(take(D_MODEL), KC) for _ in range(2)]
        sil = take(DEXP)
        hid = v3(take(2 * DEXP), 2)
        hidt = [v3(take(DEXP), 2) for _ in range(2)]
        ys = v3(take(2 * D_MODEL), 2)
        wdiag = ([xgt[n // 4].rearrange("p k t -> p (k t)")[:, 256 * (n % 4):256 * (n % 4) + 256] for n in range(8)] +
                 [sil])
        yg = [v3(arena[:, 2048 * b:2048 * (b + 1)], 2) for b in range(4)]
        fz = [arena[:, yT_at + D_MODEL * i:yT_at + D_MODEL * (i + 1)] for i in range(8)] + [xg[:, 0, :]]
        y_rs = take(2)

        block = ctx.enter_context(nc.Block())
        V, A, T, G = nc.vector, nc.scalar, nc.tensor, nc.gpsimd
        HV = {**h, **g_, **samp}

        YG = [(ld_yg[0], 0), (ld_yg[1], 0), (ld_xg[0], 16 * STEPS // 2), (ld_xg[1], 16 * STEPS // 2)]
        ROWS2 = (16, 32, 24, 40)

        def pcol(q, j):
            return par[:, q, j:j + 1]

        D_W0, D_A0, D_OKA, D_RG, D_IG, D_ML, D_NML, D_TMP = range(8)

        def dcol(q, j):
            return der[:, q, j:j + 1]

        @block.sync
        def _(sp):
            sp.dma_start(cs, c_t).then_inc(ld_cs, 16)
            for dst, src in ((par, prm), (mu_wa, mu_lo[0:64]), (mu_gd, mu_lo[64:160]), (bada, b_ada),
                             (wa_up, w_wa_up), (g_up, w_g_up)):
                sp.dma_start(dst, src).then_inc(ld_const, 16)

            def load_rows(g):
                for i in range(3 * g, 3 * g + 3):
                    r0, rt = TILES[i]
                    sp.dma_start(xn[i][0:rt], x_all[r0:r0 + rt, :]).then_inc(ld_x[g], 16)

            def load_mod(n):
                if n >= 2:
                    sp.wait_ge(mod_mm, n - 1)
                sp.dma_start(ada[n % 2].rearrange("p k m -> p (k m)"), w_ada[n]).then_inc(ld_ada[n % 2], 16)

            load_rows(0)
            load_mod(0)
            load_mod(1)
            load_rows(1)
            load_rows(2)
            for n in range(2, MOD0):
                load_mod(n)
            sp.dma_start(wlo.rearrange("p k m -> p (k m)"), w_lo).then_inc(ld_lo, 16)
            sp.dma_start(hT[:, :, NTOK:NCOL], shift_t).then_inc(ld_prev, 16)
            for n in range(3):
                sp.dma_start(win[:, n % 3, :], w_in[n]).then_inc(ld_win[n % 3], 16)
                load_mod(MOD0 + n)
            for n in range(MOD0 + 3, 24):
                load_mod(n)
            for n in range(3, 5 * NJ):
                sp.wait_ge(win_mm, 3 * (n - 3 + 2) + 3)
                sp.dma_start(win[:, n % 3, :], w_in[n]).then_inc(ld_win[n % 3], 16)
            sp.wait_ge(win_mm, 3 * (5 * NJ + 2))
            sp.wait_ge(outs, 16 * 5)
            for k in range(KC):
                sp.dma_start(wout[:, k, :], w_out[k]).then_inc(ld_wout, 16)
            sp.wait_ge(HV["half_done"], 2 * NJ)
            sp.wait_ge(HV["y_out"], 4 * NJ)

            def load_x2(i):
                r0, rt = TILES[i]
                sp.dma_start(xr2[0:rt, i % 2, :], x_all[r0:r0 + rt, :]).then_inc(ld_x2[i % 2], 16)

            sp.wait_ge(row_out, 1)
            for n in range(4):
                sp.dma_start(mod_scr[n].rearrange("b (k c) -> k b c", c=P), mod_rows_sb[:, P * n:P * n + P]).then_inc(row_stored, 16)
            load_x2(0)
            load_x2(1)
            for n in range(4):
                sp.dma_start(lnr[:, n, :], ln_rows[n:n + 1, :].partition_broadcast(P)).then_inc(ld_late, 16)
            sp.dma_start(wrt, w_rt).then_inc(ld_late, 16)
            sp.dma_start(brt, b_rt.partition_broadcast(P)).then_inc(ld_late, 16)
            sp.wait_ge(*SAMP["s_gates"])
            sp.wait_ge(row_stored, 16 * 4)
            for n in range(4):
                sp.dma_start(rowb[:, n, :], mod_scr[n, 0:1, :].partition_broadcast(P)).then_inc(ld_late, 16)
            for i, (r0, rt) in enumerate(TILES):
                if i + 2 < 9:
                    sp.wait_ge(var_ready, 9 + 2 * i + 1)
                    load_x2(i + 2)
                if i == 6:
                    sp.wait_ge(outs, 16 * 8)
                    sp.wait_ge(ld_late, 16 * 10)
                    sp.dma_start(rows_s[0:DEC], mod_scr[:, 1:9, :].rearrange("n b c -> b n c")).then_inc(ld_late, 16)
                sp.wait_ge(h2_ready, i + 1)
                sp.dma_start(h2_scr[r0:r0 + rt, :], n2[0:rt, i % 2, :]).then_inc(h2_stored[i % 2], 16)

            def load_expert(s, b, gu_used=None, dn_used=None):
                ex = sp.value_load(texp[0:1, bass.ds(s, 1)], min_val=0, max_val=NEXP - 1)
                if gu_used is not None:
                    sp.wait_ge(gu_mm, gu_used)
                sp.dma_start(exgu[b].rearrange("p k f -> p (k f)"),
                             w_gu[bass.ds(ex, 1)].rearrange("a p n -> (a p) n")).then_inc(ld_gu[b], 16)
                if dn_used is not None:
                    sp.wait_ge(dn_mm, dn_used)
                sp.dma_start(exdn[b].rearrange("p c d -> p (c d)"),
                             w_dn[bass.ds(ex, 1)].rearrange("a p n -> (a p) n")).then_inc(ld_dn[b], 16)

            sp.wait_ge(hot_ready, 1)
            load_expert(0, 0)
            load_expert(1, 1)
            with sp.Fori(1, STEPS // 2) as i:
                for b in range(2):
                    load_expert(2 * i + b, b, 2 * i + (b - 1), 2 * i + (b - 1))
            for i, (r0, rt) in enumerate(TILES):
                sp.wait_ge(y_ready, i + 1)
                sp.dma_start(y_all[r0:r0 + rt, :], fz[i][0:rt]).then_inc(y_stored, 16)
            sp.wait_ge(y_stored, 16 * 9)

        @block.gpsimd
        def _(pool):
            def link(ins):
                chain_p.on(ins)
                pool.wait_ge(chain_p.sem, chain_p.n)

            def select(t, pattern, op, base, cm):
                link(G.affine_select(out=t, in_=t, compare_op=op, fill=0.0, base=base, pattern=pattern,
                                     channel_multiplier=cm))

            def same_block(t, size):
                v = t.rearrange("p (n c) -> p n c", c=size)
                select(v, [[-size, P // size], [0, size]], ALU.is_ge, 0, 1)
                select(v, [[size, P // size], [0, size]], ALU.is_ge, size - 1, -1)

            def later_block(t, size):
                v = t.rearrange("p (n c) -> p n c", c=size)
                select(v, [[-size, P // size], [0, size]], ALU.is_ge, -size, 1)

            for t in (rg, ig):
                link(G.memset(t, 0.0))
            for n in range(2):
                for dst, src in ((rg, w_rg), (ig, w_ig)):
                    r0 = slice(64 * n, 64 * n + 64)
                    pool.dma_start(dst[r0, :, r0], src[:, r0, :].rearrange("j c d -> c j d")).then_inc(ld_samp, 16)
            link(G.memset(ones, 1.0))
            link(G.memset(eps[:, 1:2], GN_EPS))
            G.memset(eps[:, 0:1], LN_EPS).then_inc(consts_ready, 1)
            for t in (ident, blk_ones, mask_dt[:, 0], mask_dt[:, 1], mask_ak[:, 0], mask_d, mask_e, before, valid):
                link(G.memset(t, 1.0))
            link(G.memset(reset, 1.0))
            link(G.memset(reset.rearrange("p (c t) -> p c t", t=CHUNK)[:, :, 0:1], 0.0))
            for t in (pk, pr, pv, prec, pwa, pgd):
                link(G.memset(t[:, 0:PAD], 0.0))
            select(ident, [[-1, P]], ALU.is_equal, 0, 1)
            same_block(blk_ones, HEAD)
            same_block(mask_dt[:, 0], 16)
            select(mask_dt[:, 0], [[1, P]], ALU.is_gt, 0, -1)
            same_block(mask_dt[:, 1], CHUNK)
            select(mask_dt[:, 1], [[1, P]], ALU.is_ge, 0, -1)
            same_block(mask_ak[:, 0], CHUNK)
            select(mask_ak[:, 0], [[1, P]], ALU.is_gt, 0, -1)
            link(G.tensor_copy(mask_ak[:, 1], mask_dt[:, 1]))
            same_block(mask_d, 16)
            select(mask_d, [[-1, P]], ALU.is_gt, 0, 1)
            same_block(mask_e, CHUNK)
            later_block(mask_e, 16)
            select(before, [[1, P]], ALU.is_gt, 0, -1)
            link(G.iota(iota_p, [[1, P]], base=0, channel_multiplier=0, allow_small_or_imprecise_dtypes=True))
            link(G.iota(iota_s, [[1, STEPS]], base=0, channel_multiplier=0, allow_small_or_imprecise_dtypes=True))
            link(G.iota(iota_t, [[P, STEPS + 1]], base=0, channel_multiplier=0, allow_small_or_imprecise_dtypes=True))
            link(G.iota(tok_id, [[P, 9]], base=0, channel_multiplier=1, allow_small_or_imprecise_dtypes=True))
            link(G.iota(falling, [[-1, 4]], base=4, channel_multiplier=0, allow_small_or_imprecise_dtypes=True))
            select(valid[:, 8:9], [[1, 1]], ALU.is_ge, DEC - 1, -1)
            select(tok_id[:, 8:9], [[1, 1]], ALU.is_ge, DEC - 1, -1)
            G.tensor_scalar(blk_mean, blk_ones, 1.0 / HEAD, None, ALU.mult).then_inc(consts_ready, 1)
            pool.wait_ge(ht_dve, 9)
            pool.wait_ge(ht_act, 8)
            pool.dma_start(shift_o, hT[:, :, SEQ - 1:NTOK]).then_inc(outs, 16)
            pool.dma_start(convs_o, state_conv[:, 1:3, :]).then_inc(outs, 16)
            for j in range(NJ):
                pool.wait_ge(win_out, 6 + 15 * j + 9)
                pool.dma_start(conv_o[j], prec[:, PAD + SEQ - 3:PAD + NTOK]).then_inc(outs, 16)
            pool.wait_ge(win_mm, 3 * (5 * NJ + 2))
            pool.dma_start(s_conv, conv0).then_inc(ld_samp, 16)
            pool.dma_start(s_lru0, lru0).then_inc(ld_samp, 16)
            pool.wait_ge(HV["half_done"], 2 * NJ)
            pool.wait_ge(HV["y_out"], 16)
            pool.dma_start(s_Sf, wkv0).then_inc(HV["s_rows"], 16)
            pool.dma_start(wkvp_o.rearrange("j p v -> p j v"), sfin).then_inc(outs, 16)
            pool.wait_ge(*SAMP["s_vrow"])
            pool.dma_start(q_scr.rearrange("q r c -> r q c"), s_qt.rearrange("r (q c) -> r q c", q=6)).then_inc(HV["s_stored"], 16)
            pool.wait_ge(HV["s_stored"], 16)
            flat = q_scr.rearrange("q r c -> q (r c)")
            for n, q in enumerate((0, 1, 2, 4, 5)):
                src = flat[q].rearrange("(r k) -> r k", k=HEAD).unsqueeze(1).to_broadcast([64, 2, HEAD])
                pool.dma_start(s_row[:, n, :], src).then_inc(HV["s_rows"], 16)
            pool.dma_start(s_vr, flat[3].rearrange("(r k) -> r k", k=32)).then_inc(HV["s_rows"], 16)

            def modulate(i):
                rt = TILES[i][1]
                src = rowb if i < 8 else rows_s
                pool.wait_ge(n2_ready, i + 1)
                if i == 0:
                    pool.wait_ge(ld_late, 16 * 10)
                if i == 8:
                    pool.wait_ge(ld_late, 16 * 11)
                link(G.tensor_tensor(n2[0:rt, i % 2, :], n2[0:rt, i % 2, :], src[0:rt, 1, :], ALU.mult))
                G.tensor_tensor(n2[0:rt, i % 2, :], n2[0:rt, i % 2, :], src[0:rt, 2, :], ALU.add).then_inc(h2_ready, 1)

            modulate(0)
            modulate(1)
            pool.wait_ge(outs, 16 * 7)
            pool.wait_ge(*SAMP["s_y"])
            pool.dma_start(wkvs_o, s_Sf).then_inc(outs, 16)
            pool.dma_start(y_scr.rearrange("r c -> (r c)").rearrange("(p v) -> p v", v=32), s_yr).then_inc(HV["s_ystored"], 16)
            pool.wait_ge(HV["s_ystored"], 16)
            pool.dma_start(s_yrow, y_scr).then_inc(HV["s_yrow"], 16)
            for i in range(2, 8):
                modulate(i)
            pool.wait_ge(*SAMP["s_done"])
            pool.wait_ge(outs, 16 * 8)
            pool.dma_start(lru_o, lru_last).then_inc(outs, 16)
            modulate(8)
            for b in range(2):
                pool.wait_ge(h2_stored[b], 16 * (5 - b))
            pool.wait_ge(route_ready, 1)

            def gather(s, b):
                pool.indirect_dma_start(xg[:, b, :], None, h2_scr,
                                        bass.IndirectOffsetOnAxis(perm[:, s:s + 1], 0)).then_inc(ld_xg[b], 16)

            for s in range(STEPS):
                if s >= 2:
                    pool.wait_ge(xg_turned, s - 1)
                gather(s, s % 2)
            for b in range(2):
                pool.wait_ge(slot_stored[b], 16 * (STEPS // 2))
            def finish(i):
                rt = TILES[i][1]
                pool.wait_ge(y_normed, i + 1)
                G.tensor_tensor(fz[i][0:rt], fz[i][0:rt], lnr[0:rt, 3, :], ALU.add).then_inc(y_ready, 1)

            for i, (r0, rt) in enumerate(TILES):
                if i >= 4:
                    pool.wait_ge(yg_used, i - 3)
                for a in range(2):
                    pool.indirect_dma_start(yg[i % 4][0:rt, a, :], None, slot_scr,
                                            bass.IndirectOffsetOnAxis(posu[0:rt, a, i:i + 1], 0)).then_inc(YG[i % 4][0], 16)
                if i >= 4:
                    finish(i - 4)
            for i in range(5, 9):
                finish(i)
            pool.wait_ge(outs, 16 * 9)

        @block.tensor
        def _(pe):
            bank = [ps[:, i, :] for i in range(8)]
            pe.wait_ge(silu_ready, 1)
            def mod_mms(n, bank_):
                pe.wait_ge(ld_ada[n % 2], 16 * (n // 2 + 1))
                for m in range(2):
                    for k in range(KC):
                        mm = T.matmul(ps[:, bank_, 16 * m:16 * m + 9], ada[n % 2][:, k, P * m:P * m + P],
                                      csg[:, k, :], start=(k == 0), stop=(k == KC - 1))
                mm.then_inc(mod_mm, 1)

            for n in range(MOD0):
                mod_mms(n, n)
            pe.wait_ge(consts_ready, 2)
            pe.wait_ge(mod_out, MOD0)
            for i, (r0, rt) in enumerate(TILES):
                pe.wait_ge(xn_ready, i + 1)
                if i >= 4:
                    pe.wait_ge(ht_dve, i - 3)
                    pe.wait_ge(ht_act, i - 3)
                for k in range(KC):
                    tr_ = T.transpose(ps[:, 2 * (i % 4) + k // 4, P * (k % 4):P * (k % 4) + rt],
                                      xn[i][0:rt, P * k:P * k + P], ident[0:rt, 0:rt])
                tr_.then_inc(xn_turned, 1)
            pe.wait_ge(ht_dve, 9)
            pe.wait_ge(ht_act, 8)
            pe.wait_ge(ld_prev, 16)

            def project_chunk(n, c, lhs, rows):
                c0, w = COLS[c]
                if n:
                    pe.wait_ge(win_out, 3 * (n - 1) + c + 1)
                for k in range(KC):
                    mm = T.matmul(ps[0:rows, c, 0:w], lhs(k), hT[:, k, c0:c0 + w],
                                  start=(k == 0), stop=(k == KC - 1))
                mm.then_inc(win_mm, 1)

            def project(n, lhs, rows, beside=None):
                for c in range(3):
                    project_chunk(n, c, lhs, rows)
                    m = MOD0 + 3 * n + c
                    if m < 24:
                        pe.wait_ge(mod_out, m)
                        mod_mms(m, 7)
                    if beside:
                        beside(c)

            def keys_chunk(j, c):
                n = 5 * j
                if c == 0:
                    pe.wait_ge(ld_win[n % 3], 16 * (n // 3 + 1))
                project_chunk(n + 2, c, lambda k: win[:, n % 3, P * k:P * k + P], P)

            pe.wait_ge(ld_lo, 16)
            project(0, lambda k: wlo[:, k, 0:64], 64)
            project(1, lambda k: wlo[:, k, 64:160], 96)
            pe.wait_ge(ld_const, 16 * 6)
            pe.wait_ge(ld_samp, 16 * 4)
            for j in range(NJ):

                js = slice(P * j, P * j + P)

                def project_tile(q, beside=None):
                    n = 5 * j + q
                    pe.wait_ge(ld_win[n % 3], 16 * (n // 3 + 1))
                    project(n + 2, lambda k: win[:, n % 3, P * k:P * k + P], P, beside)

                def norms(c):
                    if c == 0:
                        if j:
                            pe.wait_ge(HV["half_done"], 2 * j)
                        else:
                            pe.wait_ge(lora_ready, 1)
                        for hf in range(2):
                            t0 = PAD + hf * HALF
                            T.matmul(bank[3 + 2 * hf], wa_up[0:32, js], pwa[0:32, t0:t0 + HALF], start=True, stop=True)
                            T.matmul(bank[4 + 2 * hf], wa_up[32:64, js], pwa[32:64, t0:t0 + HALF], start=True,
                                     stop=True).then_inc(HV["up_mm"], 1)
                    if c == 2:
                        for hf in range(2):
                            pe.wait_ge(HV["ta_ready"], 2 * j + hf + 1)
                            pe.wait_ge(HV["sq_ready"], 2 * j + hf + 1)
                            T.matmul(bank[3 + 2 * hf], blk_ones, prep_bufs[hf][0], start=True,
                                     stop=True).then_inc(HV["norm_mm"], 1)

                def bonuses(c):
                    if c == 0:
                        for hf in range(2):
                            pe.wait_ge(HV["gates_tanh"], 2 * j + hf + 1)
                            pe.wait_ge(HV["rkp_ready"], 2 * j + hf + 1)
                            T.matmul(bank[3 + 2 * hf], blk_ones, kept[hf][7], start=True,
                                     stop=True).then_inc(HV["bonus_mm"], 1)

                if j == 0:
                    project_tile(0)
                project_tile(1, norms)
                project_tile(2)
                project_tile(3)
                for hf in range(2):
                    xc = lru_bufs[hf][0]
                    pe.wait_ge(HV["conv_ready"], 2 * j + hf + 1)
                    pe.wait_ge(HV["nrm_ready"], 2 * j + hf + 1)
                    T.matmul(bank[3 + 2 * hf], rg[:, j, :], xc, start=True, stop=True)
                    T.matmul(bank[4 + 2 * hf], ig[:, j, :], xc, start=True, stop=True).then_inc(HV["gate_mm"], 1)
                project_tile(4, bonuses)
                pe.wait_ge(HV["bonus_out"], 2 * j + 2)
                pe.wait_ge(win_out, 3 * (5 * j + 7))
                for hf in range(2):
                    it = 2 * j + hf
                    t0 = PAD + hf * HALF
                    AR0, AR1, bb, k2, Bh, Kh, eP, rkp = kept[hf]
                    AR = ARs[hf]
                    def heads():
                        for hh in range(2):
                            for a in range(2):
                                yield hh, a, slice(HEAD * hh, HEAD * hh + HEAD)

                    def stage(g, name, waits, products):
                        gi = 2 * it + g
                        for w in waits:
                            pe.wait_ge(HV[w], gi + 1)
                        for out, lhs, rhs in products:
                            mm = T.matmul(out, lhs, rhs, start=True, stop=True)
                        mm.then_inc(HV[name], 1)

                    def unit(g, b):
                        return grp[g].bank(b).rearrange("p (h a t) -> p h a t", h=2, a=2)

                    def zunit(g, b):
                        return grp[g].bank(b).rearrange("p (w a h t) -> p w a h t", w=2, a=2, h=2)

                    def toks(g, a):
                        return slice(grp[g].c0 + P * a, grp[g].c0 + P * a + P)

                    def grams(m, n, g, src):
                        q = grp[g]
                        for hh, a, r in heads():
                            mm = T.matmul(q.bank(2 * n + hh)[:, 256 * a:256 * a + 256], src[r, toks(g, a)],
                                          ARs[m][r, :, toks(g, a)], start=True, stop=True)
                        mm.then_inc(HV[("gram_b", "gram_k")[n]], 1)

                    if hf == 0:
                        grams(0, 0, 0, bb)
                        grams(0, 0, 1, bb)
                        grams(0, 1, 0, k2)
                    else:
                        pe.wait_ge(HV["gsd_ready"], it)
                        grams(1, 0, 1, bb)
                        pe.wait_ge(HV["half_done"], it)
                    grams(hf, 1, 1, k2)
                    def gram_a(m, g):
                        AR0_, bb_ = kept[m][0], kept[m][2]
                        pe.wait_ge(HV["dt_out"], 4 * j + 2 * m + g + 1)
                        for hh, a, r in heads():
                            mm = T.matmul(grp[g].bank(hh)[:, P * a:P * a + P], AR0_[r, toks(g, a)], bb_[r, toks(g, a)],
                                          start=True, stop=True)
                        mm.then_inc(HV["gram_l"], 1)

                    def turn(m, g):
                        q = grp[g]
                        AR0_, Bh_, Kh_ = kept[m][0], kept[m][4], kept[m][5]
                        v0 = PAD + m * HALF + q.c0
                        pe.wait_ge(HV["ak_out"], 4 * j + 2 * m + g + 1)
                        for a in range(2):
                            for b_, o, src in ((2, 0, AR0_[:, toks(g, a)]), (2, 256, Kh_[:, toks(g, a)]),
                                               (3, 0, pv[:, v0 + P * a:v0 + P * a + P]),
                                               (3, 256, Bh_[:, toks(g, a)])):
                                mm = T.transpose(q.bank(b_)[:, o + P * a:o + P * a + P], src, ident)
                        mm.then_inc(HV["turned"], 1)

                    for g in range(hf, 2):
                        gram_a(hf, g)
                    if hf == 0:
                        pe.wait_ge(HV["prep_done"], j + 1)
                    for g in range(hf, 2):
                        turn(hf, g)
                    for g in range(2):
                        q = grp[g]
                        stage(g, "d2_mm", ("de_out",),
                              [(unit(g, 0)[:, hh, a], q.dtg[:, hh, a, 0, :], q.d[:, hh, a]) for hh, a, r in heads()] +
                              [(unit(g, 1)[:, hh, a], q.d[:, hh, a], q.dtg[:, hh, a, 0, :]) for hh, a, r in heads()])
                    for g in range(2):
                        q = grp[g]
                        stage(g, "akv_mm", ("tok_out",),
                              [(q.bank(3)[:, P * a + HEAD * hh:P * a + HEAD * hh + HEAD], q.ak[:, hh, a, 0, :],
                                q.vtok[:, a, HEAD * hh:HEAD * hh + HEAD]) for hh, a, r in heads()])
                    for g in range(2):
                        q = grp[g]
                        stage(g, "p2_mm", ("d2_out", "p1_out"),
                              [(unit(g, 2)[:, hh, a], q.a[:, hh, a], q.p[:, hh, a]) for hh, a, r in heads()] +
                              [(unit(g, 0)[:, hh, a], q.bt[:, hh, a], q.a[:, hh, a]) for hh, a, r in heads()] +
                              [(unit(g, 1)[:, hh, a], q.a[:, hh, a], q.bt[:, hh, a]) for hh, a, r in heads()])
                    for g in range(2):
                        q = grp[g]
                        stage(g, "p3_mm", ("d4_out", "p2_out"),
                              [(unit(g, 2)[:, hh, a], q.a[:, hh, a], q.p[:, hh, a]) for hh, a, r in heads()] +
                              [(unit(g, 0)[:, hh, a], q.bt[:, hh, a], q.a[:, hh, a]) for hh, a, r in heads()])
                    for g in range(2):
                        q = grp[g]
                        stage(g, "p4_mm", ("d8_out", "p3_out"),
                              [(unit(g, 2)[:, hh, a], q.a[:, hh, a], q.p[:, hh, a]) for hh, a, r in heads()])
                    for g in range(2):
                        q = grp[g]
                        stage(g, "f_mm", ("nt_out", "akv_out"),
                              [(unit(g, 0)[:, hh, a], q.p[:, hh, a], q.e[:, hh, a]) for hh, a, r in heads()] +
                              [(unit(g, 1)[:, hh, a], q.e[:, hh, a], q.p[:, hh, a]) for hh, a, r in heads()] +
                              [(zunit(g, 2)[:, :, a, hh], q.p[:, hh, a], q.z[:, :, a, hh]) for hh, a, r in heads()])
                    for g in range(2):
                        q = grp[g]
                        stage(g, "z1_mm", ("f_out", "z0_out"),
                              [(unit(g, 0)[:, hh, a], q.a[:, hh, a], q.bt[:, hh, a]) for hh, a, r in heads()] +
                              [(zunit(g, 2)[:, :, a, hh], q.bt[:, hh, a], q.z[:, :, a, hh]) for hh, a, r in heads()])
                    for g in range(2):
                        q = grp[g]
                        stage(g, "z2_mm", ("f2_out", "z1_out"),
                              [(zunit(g, 1)[:, :, a, hh], q.a[:, hh, a], q.z[:, :, a, hh]) for hh, a, r in heads()])
                    for g in range(2):
                        q = grp[g]
                        stage(g, "rt_mm", ("z2_out",),
                              [(q.bank(0)[r, P * a:P * a + P], q.z[:, 0, a, hh, :], q.dtg[:, hh, a, 1, :])
                               for hh, a, r in heads()] +
                              [(q.bank(2 + c)[:, P * a:P * a + P], q.zt[HEAD * c:HEAD * c + HEAD, 0, a, :],
                                q.btok[HEAD * c:HEAD * c + HEAD, a, :]) for a in range(2) for c in range(2)])
                    def y_products(g):
                        q = grp[g]
                        for hh, a, r in heads():
                            T.matmul(q.bank(1)[r, P * a:P * a + P], q.z[:, 1, a, hh, :], q.dtg[:, hh, a, 1, :],
                                     start=(a == 0), stop=False, skip_group_check=True)
                            T.matmul(q.bank(1)[r, P * a:P * a + P], q.vtok[:, a, r], q.ak[:, hh, a, 1, :],
                                     start=False, stop=False, skip_group_check=True)

                    def state_step(g, n):
                        q = grp[g]
                        gi = 2 * it + g
                        if n == 0:
                            pe.wait_ge(HV["tt_out"], gi + 1)
                            pe.wait_ge(HV["rh_out"], gi + 1)
                        a, c = n // 2, n % 2
                        r = slice(HEAD * c, HEAD * c + HEAD)
                        out = q.bank(2 + c)[:, 256:384]
                        cur = 4 * gi + n
                        if cur >= 2:
                            pe.wait_ge(state_out, cur - 1)
                        T.matmul(out, q.btok[r, a, :], q.zt[r, 1, a, :], start=True, stop=False)
                        T.matmul(out, q.ktok[r, a, :], q.vtok[r, a, :], start=False, stop=False)
                        if cur % 16 == 0:
                            pe.wait_ge(s_zero, j + 1)
                        if cur:
                            pe.wait_ge(state_out, cur)
                        t_ = slice(P * a + HEAD * c, P * a + HEAD * c + HEAD)
                        T.matmul(q.bank(1)[:, t_], S[:, n % 2, :], q.rh[:, t_], start=False,
                                 stop=(n == 3), skip_group_check=True)
                        T.matmul(out, q.tt[:, c, a, :], S[:, n % 2, :], start=False, stop=True).then_inc(state_mm, 1)

                    y_products(0)
                    state_step(0, 0)
                    y_products(1)
                    for n in range(1, 4):
                        state_step(0, n)
                    state_step(1, 0)
                    pe.wait_ge(HV["y_out"], 2 * it + 1)
                    if hf == 0:
                        grams(1, 0, 0, kept[1][2])
                    elif j < NJ - 1:
                        keys_chunk(j + 1, 0)
                    state_step(1, 1)
                    state_step(1, 2)
                    if hf == 0:
                        grams(1, 1, 0, kept[1][3])
                    state_step(1, 3)
                    T.matmul(bank[6], g_up[:, js], pgd[:, t0:t0 + HALF], start=True, stop=True)
                    pe.wait_ge(HV["y_out"], 2 * it + 2)
                    T.matmul(bank[4], blk_mean, Y, start=True, stop=True).then_inc(HV["mean_mm"], 1)
                    if hf == 0:
                        gram_a(1, 0)
                    elif j < NJ - 1:
                        keys_chunk(j + 1, 1)
                    pe.wait_ge(HV["ysq_ready"], it + 1)
                    T.matmul(bank[5], blk_mean, tmp, start=True, stop=True).then_inc(HV["var_mm"], 1)
                    if hf == 0:
                        turn(1, 0)
                    if hf and j < NJ - 1:
                        keys_chunk(j + 1, 2)

            pe.wait_ge(HV["half_done"], 2 * NJ)
            for n in range(4):
                mm = T.transpose(bank[0][0:9 * KC, P * n:P * n + P],
                                 modT[:, ROWS2[n]:ROWS2[n] + KC, :].rearrange("p k b -> p (k b)"), ident)
            mm.then_inc(row_mm, 1)
            for b_, lhs, rhs in ((4, wa_up[0:32], pwa[0:32]), (5, wa_up[32:64], pwa[32:64]), (6, g_up, pgd)):
                for j in range(NJ):
                    mm = T.matmul(bank[b_][:, DEC * j:DEC * j + DEC], lhs[:, P * j:P * j + P],
                                  rhs[:, PAD + SEQ:PAD + NTOK], start=True, stop=True)
            mm.then_inc(SAMP["s_up"][0], 1)
            pe.wait_ge(*SAMP["s_sq"])
            T.matmul(bank[3][:, 0:SN], blk_ones, s_t.rearrange("p j b -> p (j b)"), start=True,
                     stop=True).then_inc(SAMP["s_norm"][0], 1)
            for a, w_ in ((0, rg), (1, ig)):
                for j in range(NJ):
                    mm = T.matmul(bank[7][:, SN * a + DEC * j:SN * a + DEC * j + DEC], w_[:, j, :], s_xc[:, j, :],
                                  start=True, stop=True)
            mm.then_inc(SAMP["s_gates"][0], 1)

            def out_half(i, n):
                r0, rt = TILES[i]
                if i >= 2:
                    pe.wait_ge(wo_out, i - 1)
                for k in range(KC):
                    mm = T.matmul(ps[0:rt, 2 * (i % 2) + n, :], yT[:, k, r0:r0 + rt],
                                  wout[:, k, 512 * n:512 * n + 512], start=(k == 0), stop=(k == KC - 1))
                mm.then_inc(wo_mm, 1)

            def turn_h2(i):
                r0, rt = TILES[i]
                pe.wait_ge(h2_ready, i + 1)
                if i:
                    pe.wait_ge(h2t_out, i)
                else:
                    pe.wait_ge(*SAMP["s_vrow"])
                    pe.wait_ge(ld_late, 16 * 10)
                for k in range(KC):
                    mm = T.transpose(ps[:, 4 + k // 4, P * (k % 4):P * (k % 4) + rt],
                                     n2[0:rt, i % 2, P * k:P * k + P], ident[0:rt, 0:rt])
                mm.then_inc(h2_turned, 1)

            def route_h2(i):
                rt = TILES[i][1]
                pe.wait_ge(h2t_out, i + 1)
                for k in range(KC):
                    mm = T.matmul(ps[0:rt, 6, 20 * i:20 * i + 20], h2t[:, k, 0:rt], wrt[:, k, :],
                                  start=(k == 0), stop=(k == KC - 1))
                mm.then_inc(router_mm, 1)

            pe.wait_ge(ld_wout, 16 * KC)
            pe.wait_ge(row_out, 1)
            out_half(0, 0)
            pe.wait_ge(*SAMP["s_bon"])
            T.matmul(bank[5][:, 0:SN], blk_ones, s_t1.rearrange("p j b -> p (j b)"), start=True,
                     stop=True).then_inc(SAMP["s_bonmm"][0], 1)
            pe.wait_ge(*SAMP["s_vec"])
            pe.wait_ge(*SAMP["s_lexp"])
            for q in range(6):
                mm = T.transpose(bank[6 + q // 4][0:SN, P * (q % 4):P * (q % 4) + P], s_vflat[:, SN * q:SN * q + SN], ident)
            mm.then_inc(SAMP["s_turn"][0], 1)
            out_half(0, 1)
            for i in range(1, 9):
                if i == 4:
                    pe.wait_ge(HV["s_yrow"], 16)
                    T.transpose(bank[7][:, 0:SN], s_yrow, ident[0:SN, 0:SN]).then_inc(SAMP["s_yturn"][0], 1)
                if i == 5:
                    pe.wait_ge(*SAMP["s_yc"])
                    T.matmul(bank[7][:, 0:SN], blk_mean, s_y.rearrange("p j b -> p (j b)"), start=True,
                             stop=True).then_inc(SAMP["s_mean"][0], 1)
                if i == 7:
                    pe.wait_ge(*SAMP["s_sqr"])
                    T.matmul(bank[7][:, 0:SN], blk_mean, s_t.rearrange("p j b -> p (j b)"), start=True,
                             stop=True).then_inc(SAMP["s_var"][0], 1)
                if i == 8:
                    pe.wait_ge(*SAMP["s_done"])
                out_half(i, 0)
                if i > 1:
                    turn_h2(i - 2)
                out_half(i, 1)
                if i > 1:
                    route_h2(i - 2)
            for i in (7, 8):
                turn_h2(i)
                route_h2(i)
            pe.wait_ge(assigned, 1)
            T.matmul(bank[0][:, 0:9 * NEXP], before, asg.rearrange("p i e -> p (i e)"), start=True, stop=True)
            for i in range(9):
                mm = T.matmul(bank[1][:, NEXP * (i + 1):NEXP * 10].rearrange("p (i e) -> p i e", e=NEXP), ones,
                              asg[:, i:i + 1, :].to_broadcast([P, 9 - i, NEXP]), start=(i == 0), stop=(i == 8),
                              skip_group_check=True)
            mm.then_inc(rank_mm, 1)
            for n in range(18):
                pe.wait_ge(hot_ready, n + 1)
                T.matmul(bank[2][:, 0:STEPS], uu[:, n % 9, :], wt[:, n // 9, n % 9, :], start=(n == 0),
                         stop=(n == 17)).then_inc(hot_used, 1)

            def turn_rows(s, b):
                for k in range(KC):
                    mm = T.transpose(ps[:, k // 4, P * (k % 4):P * (k % 4) + P], xg[:, b, P * k:P * k + P], ident)
                mm.then_inc(xg_turned, 1)

            def gate_up(s, b):
                for k in range(KC):
                    mm = T.matmul(ps[:, 2 + b, :], xgt[b][:, k, :], exgu[b][:, k, :], start=(k == 0), stop=(k == KC - 1))
                mm.then_inc(gu_mm, 1)

            def turn_hidden(s, b):
                for c in range(2):
                    mm = T.transpose(ps[:, 4 + b, P * c:P * c + P], hid[:, b, P * c:P * c + P], ident)
                mm.then_inc(hid_turned, 1)

            def down(s, b):
                for n in range(2):
                    for c in range(2):
                        mm = T.matmul(ps[:, 6 + n, :], hidt[b][:, c, :], exdn[b][:, c, 512 * n:512 * n + 512],
                                      start=(c == 0), stop=(c == 1))
                mm.then_inc(dn_mm, 1)

            pe.wait_ge(route_ready, 1)
            pe.wait_ge(ld_xg[0], 16)
            turn_rows(0, 0)
            pe.wait_ge(xgt_out, 1)
            pe.wait_ge(ld_gu[0], 16)
            gate_up(0, 0)
            pe.wait_ge(ld_xg[1], 16)
            turn_rows(1, 1)
            pe.wait_ge(hid_out, 1)
            turn_hidden(0, 0)

            def step(s, i, b, more):
                pe.wait_ge(xgt_out, s + 1)
                pe.wait_ge(ld_gu[b], 16 * i + 16)
                gate_up(s, b)
                pe.wait_ge(hidt_out, s)
                if not (isinstance(s, int) and s == 1):
                    pe.wait_ge(ys_out, s - 1)
                pe.wait_ge(ld_dn[1 - b], 16 * i + 16 * b)
                down(s, 1 - b)
                if more:
                    pe.wait_ge(ld_xg[1 - b], 16 * i + 16 * (1 + b))
                    turn_rows(s, 1 - b)
                pe.wait_ge(hid_out, s + 1)
                turn_hidden(s, b)

            step(1, 0, 1, True)
            with pe.Fori(1, STEPS // 2 - 1) as i:
                for b in range(2):
                    step(2 * i + b, i, b, True)
            step(STEPS - 2, STEPS // 2 - 1, 0, True)
            step(STEPS - 1, STEPS // 2 - 1, 1, False)
            pe.wait_ge(hidt_out, STEPS)
            pe.wait_ge(ys_out, STEPS - 1)
            pe.wait_ge(ld_dn[1], 16 * (STEPS // 2))
            down(STEPS, 1)
            for i, (r0, rt) in enumerate(TILES):
                pe.wait_ge(y_first, i + 1)
                pe.wait_ge(YG[i % 4][0], YG[i % 4][1] + 32 * (i // 4 + 1))
                if i >= 4:
                    pe.wait_ge(var_ready, 27 + i - 3)
                for n in range(2):
                    for a in range(2):
                        mm = T.matmul(ps[0:rt, 2 * (i % 4) + n, :], wdiag[i][0:rt, P * a:P * a + rt],
                                      yg[i % 4][0:rt, a, 512 * n:512 * n + 512], start=(a == 0), stop=(a == 1))
                mm.then_inc(yg_used, 1)

        @block.scalar
        def _(act):
            def link(ins):
                chain_a.on(ins)
                act.wait_ge(chain_a.sem, chain_a.n)

            act.wait_ge(ld_cs, 16)
            A.activation(csg, cs, ACT.Tanh, scale=0.5).then_inc(par_tanh, 1)
            act.wait_ge(ld_const, 16 * 6)
            link(A.activation(der[:, D_TMP, :], par[:, LAM, :], ACT.Abs))
            link(A.activation(der[:, D_TMP, :], der[:, D_TMP, :], ACT.Exp, scale=-1.0))
            act.wait_ge(consts_ready, 1)
            A.activation(der[:, D_TMP, :], der[:, D_TMP, :], ACT.Ln, bias=ones[:, 0:1]).then_inc(par_tanh, 1)
            for i, (r0, rt) in enumerate(TILES):
                act.wait_ge(var_ready, i + 1)
                if i >= 1:
                    act.wait_ge(xn_ready, i)
                A.activation(sd[0:rt], mv[0:rt, 1:2], ACT.Sqrt, bias=eps[0:rt, 0:1]).then_inc(sd_ready, 1)
            act.wait_ge(mod_out, MOD0)
            for i, (r0, rt) in enumerate(TILES):
                if i < 8:
                    act.wait_ge(xn_turned, i + 1)
                    for k in range(4, 8):
                        last = A.activation(hT[:, k, r0:r0 + rt], ps[:, 1 + 2 * (i % 4), P * (k - 4):P * (k - 3)],
                                            ACT.Identity, bias=modT[:, k, 0:1], scale=modT[:, 8 + k, 0:1])
                    last.then_inc(ht_act, 1)

            def chunk_out(n, c, dst, gate=None):
                c0, w = COLS[c]
                act.wait_ge(win_mm, 3 * n + c + 1)
                if gate is None:
                    A.activation(dst[:, PAD + c0:PAD + c0 + w], ps[0:dst.shape[0], c, 0:w], ACT.Copy).then_inc(win_out, 1)
                else:
                    if c == 2:
                        A.activation(pgs[:, gate, :], ps[:, c, SEQ - c0:NTOK - c0], ACT.Copy)
                    w = min(w, SEQ - c0)
                    A.activation(yT[:, NJ + gate, c0:c0 + w], ps[:, c, 0:w], ACT.Gelu_apprx_tanh).then_inc(win_out, 1)

            def project_out(n, dst, beside=None, gate=None):
                for c in range(3):
                    chunk_out(n, c, dst, gate)
                    m = MOD0 + 3 * n + c
                    if m < 24:
                        act.wait_ge(mod_mm, m + 1)
                        for a in range(2):
                            last = A.activation(modT[:, 2 * m + a, :], ps[:, 7, 16 * a:16 * a + 9],
                                                ACT.Identity, bias=bada[:, 2 * m + a:2 * m + a + 1])
                        last.then_inc(mod_out, 1)
                    if beside:
                        beside(c)

            project_out(0, pwa)
            project_out(1, pgd)
            act.wait_ge(lora_shifted, 1)
            A.activation(pwa[0:32, PAD:PAD + NTOK], pwa[0:32, PAD:PAD + NTOK], ACT.Tanh).then_inc(lora_tanh, 1)
            A.activation(pgd[:, PAD:PAD + NTOK], pgd[:, PAD:PAD + NTOK], ACT.Tanh, scale=0.5).then_inc(lora_tanh, 1)
            act.wait_ge(params_ready, 1)
            for j in range(NJ):

                def decays_norms(c):
                    if c == 0:
                        for hf in range(2):
                            sq, lam, cum, eN, aa, kk = prep_bufs[hf]
                            act.wait_ge(HV["up_mm"], 2 * j + hf + 1)
                            A.activation(lam, ps[:, 3 + 2 * hf, :], ACT.Tanh, scale=0.5, bias=dcol(D_W0, j))
                            A.activation(aa, ps[:, 4 + 2 * hf, :], ACT.Tanh, scale=0.5,
                                         bias=dcol(D_A0, j)).then_inc(HV["ta_ready"], 1)
                        act.wait_ge(HV["shifted"], j + 1)
                        for hf in range(2):
                            o = PAD + hf * HALF
                            A.activation(prep_bufs[hf][0], pk[:, o:o + HALF], ACT.Square,
                                         scale=pcol(K_K, j)).then_inc(HV["sq_ready"], 1)
                    if c == 2:
                        for hf in range(2):
                            sq, lam, cum, eN, aa, kk = prep_bufs[hf]
                            act.wait_ge(HV["cum_ready"], 2 * j + hf + 1)
                            A.activation(kept[hf][6], cum, ACT.Exp)
                            A.activation(lam, lam, ACT.Exp)
                            A.activation(eN, cum, ACT.Exp, scale=-1.0).then_inc(HV["exp_ready"], 1)
                        for hf in range(2):
                            act.wait_ge(HV["norm_mm"], 2 * j + hf + 1)
                            A.activation(prep_bufs[hf][5], ps[:, 3 + 2 * hf, :], ACT.Sqrt).then_inc(HV["nrm_ready"], 1)

                if j == 0:
                    project_out(2, pk)
                project_out(3 + 5 * j, pr, decays_norms)
                if j:
                    act.wait_ge(outs, 16 * (2 + j))
                project_out(4 + 5 * j, prec)
                project_out(5 + 5 * j, pv)
                for hf in range(2):
                    xc, tr, ti, t2, hs = lru_bufs[hf]
                    act.wait_ge(HV["gate_mm"], 2 * j + hf + 1)
                    link(A.activation(tr, ps[:, 3 + 2 * hf, :], ACT.Tanh, scale=0.5, bias=dcol(D_RG, j)))
                    A.activation(ti, ps[:, 4 + 2 * hf, :], ACT.Tanh, scale=0.5, bias=dcol(D_IG, j)).then_inc(HV["gates_tanh"], 1)
                    link(A.activation(t2, tr, ACT.Tanh, scale=dcol(D_ML, j), bias=dcol(D_ML, j)))
                    A.activation(tr, tr, ACT.Exp, scale=dcol(D_NML, j), bias=dcol(D_NML, j)).then_inc(HV["lru_exp"], 1)

                def multipliers(c):
                    if c == 0:
                        for hf in range(2):
                            act.wait_ge(HV["q_ready"], 2 * j + hf + 1)
                            t2 = lru_bufs[hf][3]
                            A.activation(t2, t2, ACT.Sqrt).then_inc(HV["lru_mult"], 1)

                project_out(6 + 5 * j, None, multipliers, gate=j)
                for hf in range(2):
                    it = 2 * j + hf
                    eP = kept[hf][6]

                    def out(g, name, wait, dst, src):
                        act.wait_ge(HV[wait], 2 * it + g + 1)
                        A.activation(dst, src, ACT.Copy).then_inc(HV[name], 1)

                    def two(g, b):
                        return ps[:, 4 * g + b:4 * g + b + 2, :].rearrange("p b x -> p (b x)")

                    for g in range(2):
                        q = grp[g]
                        act.wait_ge(HV["turned"], 2 * it + g + 1)
                        A.activation(q.vb, q.bank(3), ACT.Copy)
                        A.activation(q.kflat, q.bank(2)[:, 256:512], ACT.Copy)
                        A.activation(q.z_flat[:, 0:256], q.bank(2)[:, 0:256], ACT.Copy).then_inc(HV["tok_out"], 1)
                    for g in range(2):
                        out(g, "d2_out", "d2_mm", grp[g].ab_flat, two(g, 0))
                    for g in range(2):
                        q = grp[g]
                        out(g, "akv_out", "akv_mm", q.z_flat[:, 256:512], q.bank(3)[:, 0:256])
                    for g in range(2):
                        out(g, "d4_out", "p2_mm", grp[g].ab_flat, two(g, 0))
                    for g in range(2):
                        out(g, "d8_out", "p3_mm", grp[g].ab_flat[:, 0:512], grp[g].bank(0))
                    for g in range(2):
                        out(g, "f_out", "f_mm", grp[g].ab_flat, two(g, 0))
                    for g in range(2):
                        out(g, "f2_out", "z1_mm", grp[g].ab_flat[:, 0:512], grp[g].bank(0))
                    for g in range(2):
                        q = grp[g]
                        act.wait_ge(state_mm, 4 * (2 * it + g + 1))
                        A.activation(Y[:, q.c0:q.c0 + GRP], q.bank(1)[:, 0:GRP], ACT.Copy).then_inc(HV["y_out"], 1)
                        if g == 0 and hf and j < NJ - 1:
                            chunk_out(7 + 5 * j, 0, pk)
                    act.wait_ge(HV["centred"], it + 1)
                    A.activation(tmp, Y, ACT.Square).then_inc(HV["ysq_ready"], 1)
                    if hf and j < NJ - 1:
                        chunk_out(7 + 5 * j, 1, pk)
                    act.wait_ge(HV["var_mm"], it + 1)
                    A.activation(eP, ps[:, 5, :], ACT.Sqrt, bias=eps[:, 1:2]).then_inc(HV["gsd_ready"], 1)
                    if hf and j < NJ - 1:
                        chunk_out(7 + 5 * j, 2, pk)


            def tile_act(dst, src, f, scale, bias):
                for j in range(NJ):
                    s_ = dcol(scale, j) if isinstance(scale, int) else scale
                    last = A.activation(dst[:, j, :], src(j), f, scale=s_, bias=dcol(bias, j))
                return last

            def pcols(b_, o=0):
                return lambda j: ps[:, b_, o + DEC * j:o + DEC * j + DEC]

            act.wait_ge(*SAMP["s_up"])
            tile_act(s_lam, pcols(4), ACT.Tanh, 0.5, D_W0)
            tile_act(s_a, pcols(5), ACT.Tanh, 0.5, D_A0)
            A.activation(s_g, ps[:, 6, 0:SN].rearrange("p (j b) -> p j b", j=NJ), ACT.Copy).then_inc(SAMP["s_wa"][0], 1)
            act.wait_ge(*SAMP["s_norm"])
            A.activation(s_t.rearrange("p j b -> p (j b)"), ps[:, 3, 0:SN], ACT.Sqrt).then_inc(SAMP["s_nrm"][0], 1)
            act.wait_ge(*SAMP["s_lam"])
            A.activation(s_vecs[:, 1], s_lam, ACT.Exp).then_inc(SAMP["s_w"][0], 1)
            act.wait_ge(*SAMP["s_gates"])
            tile_act(s_tr, pcols(7), ACT.Tanh, 0.5, D_RG)
            link(tile_act(s_ti, pcols(7, SN), ACT.Tanh, 0.5, D_IG))
            link(tile_act(s_t2, lambda j: s_tr[:, j, :], ACT.Tanh, D_ML, D_ML))
            tile_act(s_tr, lambda j: s_tr[:, j, :], ACT.Exp, D_NML, D_NML).then_inc(SAMP["s_lexp"][0], 1)
            act.wait_ge(*SAMP["s_q"])
            A.activation(s_t2, s_t2, ACT.Sqrt).then_inc(SAMP["s_mult"][0], 1)
            A.activation(s_mu, pgs, ACT.Gelu_apprx_tanh).then_inc(SAMP["s_gelu"][0], 1)
            def h2t_copy(i):
                rt = TILES[i][1]
                act.wait_ge(h2_turned, i + 1)
                if i:
                    act.wait_ge(router_mm, i)
                for n in range(2):
                    last = A.activation(h2t[:, 4 * n:4 * n + 4, 0:rt],
                                        ps[:, 4 + n, :].rearrange("p (k t) -> p k t", k=4)[:, :, 0:rt], ACT.Copy)
                last.then_inc(h2t_out, 1)

            for i, (r0, rt) in enumerate(TILES):
                if i == 5:
                    act.wait_ge(*SAMP["s_cent"])
                    A.activation(s_t, s_y, ACT.Square).then_inc(SAMP["s_sqr"][0], 1)
                if i == 7:
                    act.wait_ge(*SAMP["s_var"])
                    A.activation(s_t1.rearrange("p j b -> p (j b)"), ps[:, 7, 0:SN], ACT.Sqrt,
                                 bias=eps[:, 1:2]).then_inc(SAMP["s_gsd"][0], 1)
                act.wait_ge(var_ready, 9 + 2 * i + 1)
                A.activation(sd[0:rt], mv[0:rt, 1:2], ACT.Sqrt, bias=eps[0:rt, 0:1]).then_inc(sd_ready, 1)
                act.wait_ge(var_ready, 9 + 2 * i + 2)
                A.activation(sd[0:rt], mv[0:rt, 1:2], ACT.Sqrt, bias=eps[0:rt, 0:1]).then_inc(sd_ready, 1)
                if i:
                    h2t_copy(i - 1)
            h2t_copy(8)
            act.wait_ge(lg_ready, 1)
            A.activation(rt_a[0], rt_a[0], ACT.Exp).then_inc(ex_ready, 1)
            act.wait_ge(lg2_ready, 1)
            A.activation(rt_s[3], rt_s[3], ACT.Exp).then_inc(ex2_ready, 1)
            act.wait_ge(route_ready, 1)

            def rows_copy(s, b):
                act.wait_ge(xg_turned, s + 1)
                A.activation(xgt[b].rearrange("p k t -> p (k t)"), ps[:, 0:2, :].rearrange("p b x -> p (b x)"),
                             ACT.Copy).then_inc(xgt_out, 1)

            def hidden(s, b):
                act.wait_ge(gu_mm, s + 1)
                A.activation(sil, ps[:, 2 + b, 0:DEXP], ACT.Silu).then_inc(silu_out, 1)

            def hidden_copy(s, b):
                act.wait_ge(hid_turned, s + 1)
                A.activation(hidt[b].rearrange("p c t -> p (c t)"), ps[:, 4 + b, 0:DEXP], ACT.Copy).then_inc(hidt_out, 1)

            def store(s, b):
                act.wait_ge(ys_out, s + 1)
                act.dma_start(slot_scr.rearrange("(s p) d -> s p d", p=P)[bass.ds(s, 1)].rearrange("s p d -> (s p) d"),
                              ys[:, b, :]).then_inc(slot_stored[b], 16)

            rows_copy(0, 0)
            hidden(0, 0)
            rows_copy(1, 1)
            hidden_copy(0, 0)

            def act_step(s, b, more):
                hidden(s, b)
                if more:
                    rows_copy(s + 1, 1 - b)
                hidden_copy(s, b)
                store(s - 1, 1 - b)

            act_step(1, 1, True)
            with act.Fori(1, STEPS // 2 - 1) as i:
                for b in range(2):
                    act_step(2 * i + b, b, True)
            act_step(STEPS - 2, 0, True)
            act_step(STEPS - 1, 1, False)
            store(STEPS - 1, 1)

            def normalise(i):
                rt = TILES[i][1]
                act.wait_ge(y_scale, i + 1)
                A.activation(fz[i][0:rt], fz[i][0:rt], ACT.Identity, scale=y_rs[0:rt, i % 2:i % 2 + 1]).then_inc(y_normed, 1)

            for i, (r0, rt) in enumerate(TILES):
                for a in range(2):
                    last = A.activation(wdiag[i][:, P * a:P * a + P], ident, ACT.Identity, scale=rt_s[5 + a][:, i:i + 1])
                last.then_inc(y_first, 1)
            for i, (r0, rt) in enumerate(TILES):
                act.wait_ge(var_ready, 27 + i + 1)
                A.activation(sd[0:rt], mv[0:rt, 1:2], ACT.Sqrt, bias=eps[0:rt, 0:1]).then_inc(sd_ready, 1)
                if i:
                    normalise(i - 1)
            normalise(8)

        @block.vector
        def _(dve):
            def link(ins):
                chain_v.on(ins)
                dve.wait_ge(chain_v.sem, chain_v.n)

            def lag(ins):
                chain_v.on(ins)
                dve.wait_ge(chain_v.sem, chain_v.n - 1)

            def last_done():
                dve.wait_ge(chain_v.sem, chain_v.n)

            def done(ins, s_, n):
                ins.then_inc(s_, 1)
                dve.wait_ge(s_, n)

            TT, TS, STT = V.tensor_tensor, V.tensor_scalar, V.scalar_tensor_tensor

            dve.wait_ge(par_tanh, 1)
            link(STT(out=csg, in0=csg, scalar=1.0, in1=cs, op0=ALU.add, op1=ALU.mult))
            done(TS(csg, csg, 0.5, None, ALU.mult), silu_ready, 1)
            dve.wait_ge(ld_const, 16 * 6)
            dve.wait_ge(consts_ready, 1)
            link(TS(bada[:, 8:24], bada[:, 8:24], 1.0, None, ALU.add))
            link(TS(bada[:, 32:48], bada[:, 32:48], 1.0, None, ALU.add))
            for d_, q_, m_ in ((D_W0, W0, 0.5), (D_A0, A0, 0.5), (D_RG, B_RG, 0.5), (D_IG, B_IG, 0.5)):
                link(TS(der[:, d_, :], par[:, q_, :], m_, None, ALU.mult))
            link(TS(der[:, D_OKA, :], par[:, K_A, :], -1.0, 1.0, ALU.mult, ALU.add))
            dve.wait_ge(par_tanh, 2)
            link(TS(der[:, D_ML, :], par[:, LAM, :], -1.0, 0.0, ALU.mult, ALU.max))
            link(TT(der[:, D_ML, :], der[:, D_ML, :], der[:, D_TMP, :], ALU.add))
            link(TS(der[:, D_ML, :], der[:, D_ML, :], 4.0, None, ALU.mult))
            done(TS(der[:, D_NML, :], der[:, D_ML, :], -1.0, None, ALU.mult), params_ready, 1)

            def moments(src, rt, s_, n):
                V.bn_stats(st[0:rt, 0, :], src[:, 0:512])
                link(V.bn_stats(st[0:rt, 1, :], src[:, 512:1024]))
                done(V.bn_aggr(mv[0:rt], st[0:rt]), s_, n)

            def mod_rows(n):
                dve.wait_ge(mod_mm, n + 1)
                src = ps[:, n, 0:32].rearrange("p (m b) -> p m b", m=2)[:, :, 0:9]
                TT(modT[:, 2 * n:2 * n + 2, :], src, bada[:, 2 * n:2 * n + 2].unsqueeze(2).to_broadcast([P, 2, 9]),
                   ALU.add).then_inc(mod_out, 1)


            def ht_tile(i):
                r0, rt = TILES[i]
                dve.wait_ge(xn_turned, i + 1)
                if i < 8:
                    for k in range(4):
                        last = TS(hT[:, k, r0:r0 + rt], ps[:, 2 * (i % 4), P * k:P * k + P],
                                  modT[:, 8 + k, 0:1], modT[:, k, 0:1], ALU.mult, ALU.add)
                else:
                    for b_ in range(2):
                        src = ps[:, 2 * (i % 4) + b_, :].rearrange("p (k t) -> p k t", k=4)[:, :, 0:DEC]
                        dst = hT[:, 4 * b_:4 * b_ + 4, SEQ:NTOK]
                        link(TT(dst, src, modT[:, 8 + 4 * b_:12 + 4 * b_, 1:9], ALU.mult))
                        last = TT(dst, dst, modT[:, 4 * b_:4 * b_ + 4, 1:9], ALU.add)
                last.then_inc(ht_dve, 1)

            for i, (r0, rt) in enumerate(TILES):
                dve.wait_ge(ld_x[i // 3], 16 * 3)
                x_ = xn[i][0:rt]
                moments(x_, rt, var_ready, i + 1)
                dve.wait_ge(sd_ready, i + 1)
                link(V.reciprocal(rs[0:rt], sd[0:rt]))
                done(TS(x_, x_, mv[0:rt, 0:1], rs[0:rt], ALU.subtract, ALU.mult), xn_ready, i + 1)
            for n in range(MOD0):
                mod_rows(n)
            dve.wait_ge(mod_out, MOD0)
            for i in range(9):
                ht_tile(i)

            def shift(b_, o, n, mu, rows=P):
                link(TT(tmp[0:rows, 0:n], b_[:, o - 1:o - 1 + n], b_[:, o:o + n], ALU.subtract))
                return STT(out=b_[:, o:o + n], in0=tmp[0:rows, 0:n], scalar=mu, in1=b_[:, o:o + n],
                           op0=ALU.mult, op1=ALU.add)

            S0, S1 = PAD + SEQ, PAD + NTOK
            dve.wait_ge(win_out, 6)
            for b_, mu, rows in ((pwa, mu_wa, 64), (pgd, mu_gd, 96)):
                link(shift(b_, PAD + HALF, HALF, mu, rows))
                link(shift(b_, PAD, HALF, mu, rows))
                link(TT(tmp[0:rows, 0:DEC], b_[:, S1:S1 + DEC], b_[:, S0:S1], ALU.subtract))
                link(STT(out=b_[:, S0:S1], in0=tmp[0:rows, 0:DEC], scalar=mu, in1=b_[:, S0:S1], op0=ALU.mult,
                         op1=ALU.add))
            V.memset(rs, 0.0).then_inc(lora_shifted, 1)
            dve.wait_ge(lora_tanh, 2)
            done(TS(pgd[:, PAD:S1], pgd[:, PAD:S1], 0.5, 0.5, ALU.mult, ALU.add), lora_ready, 1)

            for j in range(NJ):
                def shift_tile(q, b_, mu):
                    parts = ((PAD, HALF, PAD - 1, tmp), (PAD + HALF, HALF, PAD + HALF - 1, Y), (S0, DEC, S1, diff_s))
                    for o, n, before_, d_ in parts:
                        lag(TT(d_, b_[:, before_:before_ + n], b_[:, o:o + n], ALU.subtract))
                    last_done()
                    for o, n, before_, d_ in parts:
                        dst = psm[:, q, j, :] if n == DEC else b_[:, o:o + n]
                        last = STT(out=dst, in0=d_, scalar=pcol(mu, j), in1=b_[:, o:o + n], op0=ALU.mult, op1=ALU.add)
                        if n == DEC:
                            return last
                        lag(last)

                def chunks(ap):
                    return ap.rearrange("p (c t) -> p c t", t=CHUNK)

                def ends(eP):
                    return chunks(eP)[:, :, CHUNK - 1:CHUNK].to_broadcast([P, HALF // CHUNK, CHUNK])

                dve.wait_ge(win_out, 6 + 15 * j + 3)
                done(shift_tile(0, pk, MU_K), HV["shifted"], j + 1)
                V.memset(S[:, 0, :], 0.0).then_inc(s_zero, 1)
                halves = [(2 * j + n + 1, slice(PAD + n * HALF, PAD + (n + 1) * HALF), *prep_bufs[n], *kept[n])
                          for n in range(2)]
                for n1, cols, sq, lam, cum, eN, aa, kk, AR0, AR1, bb, k2, Bh, Kh, eP, rkp in halves:
                    dve.wait_ge(HV["ta_ready"], n1)
                    lag(TS(lam, lam, -0.5 * DECAY, -0.5 * DECAY, ALU.mult, ALU.add))
                for n1, cols, sq, lam, cum, eN, aa, kk, AR0, AR1, bb, k2, Bh, Kh, eP, rkp in halves:
                    lag(V.tensor_tensor_scan(cum, reset, lam, 0.0, ALU.mult, ALU.add))
                for n1, cols, sq, lam, cum, eN, aa, kk, AR0, AR1, bb, k2, Bh, Kh, eP, rkp in halves:
                    lag(TS(aa, aa, 0.5, 0.5, ALU.mult, ALU.add))
                for n1, cols, sq, lam, cum, eN, aa, kk, AR0, AR1, bb, k2, Bh, Kh, eP, rkp in halves:
                    TT(lam, cum, lam, ALU.subtract).then_inc(HV["cum_ready"], 1)
                for n1, cols, sq, lam, cum, eN, aa, kk, AR0, AR1, bb, k2, Bh, Kh, eP, rkp in halves:
                    dve.wait_ge(HV["nrm_ready"], n1)
                    lag(TS(kk, kk, 1e-12, None, ALU.max))
                for n1, cols, sq, lam, cum, eN, aa, kk, AR0, AR1, bb, k2, Bh, Kh, eP, rkp in halves:
                    lag(V.reciprocal(kk, kk))
                for n1, cols, sq, lam, cum, eN, aa, kk, AR0, AR1, bb, k2, Bh, Kh, eP, rkp in halves:
                    lag(TS(sq, aa, pcol(K_A, j), dcol(D_OKA, j), ALU.mult, ALU.add))
                for n1, cols, sq, lam, cum, eN, aa, kk, AR0, AR1, bb, k2, Bh, Kh, eP, rkp in halves:
                    lag(STT(out=kk, in0=pk[:, cols], scalar=pcol(K_K, j), in1=kk, op0=ALU.mult, op1=ALU.mult))
                for n1, cols, sq, lam, cum, eN, aa, kk, AR0, AR1, bb, k2, Bh, Kh, eP, rkp in halves:
                    lag(TT(k2, pk[:, cols], sq, ALU.mult))
                for n1, cols, sq, lam, cum, eN, aa, kk, AR0, AR1, bb, k2, Bh, Kh, eP, rkp in halves:
                    lag(TT(bb, kk, aa, ALU.mult))
                for n1, cols, sq, lam, cum, eN, aa, kk, AR0, AR1, bb, k2, Bh, Kh, eP, rkp in halves:
                    dve.wait_ge(HV["exp_ready"], n1)
                    lag(STT(out=AR0, in0=kk, scalar=-1.0, in1=lam, op0=ALU.mult, op1=ALU.mult))
                for n1, cols, sq, lam, cum, eN, aa, kk, AR0, AR1, bb, k2, Bh, Kh, eP, rkp in halves:
                    lag(TT(bb, bb, eN, ALU.mult))
                for n1, cols, sq, lam, cum, eN, aa, kk, AR0, AR1, bb, k2, Bh, Kh, eP, rkp in halves:
                    lag(TT(chunks(Bh), chunks(bb), ends(eP), ALU.mult))
                dve.wait_ge(win_out, 6 + 15 * j + 6)
                link(shift_tile(1, pr, MU_R))
                for n1, cols, sq, lam, cum, eN, aa, kk, AR0, AR1, bb, k2, Bh, Kh, eP, rkp in halves:
                    STT(out=rkp, in0=pr[:, cols], scalar=pcol(R_K, j), in1=k2, op0=ALU.mult,
                        op1=ALU.mult).then_inc(HV["rkp_ready"], 1)
                for n1, cols, sq, lam, cum, eN, aa, kk, AR0, AR1, bb, k2, Bh, Kh, eP, rkp in halves:
                    lag(TT(AR1, pr[:, cols], eP, ALU.mult))
                for n1, cols, sq, lam, cum, eN, aa, kk, AR0, AR1, bb, k2, Bh, Kh, eP, rkp in halves:
                    lag(TT(k2, k2, eN, ALU.mult))
                for n1, cols, sq, lam, cum, eN, aa, kk, AR0, AR1, bb, k2, Bh, Kh, eP, rkp in halves:
                    lag(TT(chunks(Kh), chunks(k2), ends(eP), ALU.mult))
                dve.wait_ge(win_out, 6 + 15 * j + 9)
                if j == 0:
                    dve.wait_ge(mod_mm, 24)
                for n in range(2):
                    o = PAD + n * HALF
                    lag(TS(lru_bufs[n][0], prec[:, o - 3:o - 3 + HALF], pcol(CW0, j), pcol(C_BIAS, j), ALU.mult, ALU.add))
                for m in (1, 2):
                    for n in range(2):
                        o = PAD + n * HALF
                        xc = lru_bufs[n][0]
                        lag(STT(out=xc, in0=prec[:, o - 3 + m:o - 3 + m + HALF], scalar=pcol(CW0 + m, j), in1=xc,
                                op0=ALU.mult, op1=ALU.add))
                lag(V.tensor_copy(pxs[:, j, :], prec[:, S0:S1]))
                for n in range(2):
                    o = PAD + n * HALF
                    xc = lru_bufs[n][0]
                    STT(out=xc, in0=prec[:, o:o + HALF], scalar=pcol(CW3, j), in1=xc, op0=ALU.mult,
                        op1=ALU.add).then_inc(HV["conv_ready"], 1)
                dve.wait_ge(win_out, 6 + 15 * j + 12)
                link(shift_tile(2, pv, MU_V))
                for n, (xc, tr, ti, t2, hs) in enumerate(lru_bufs):
                    dve.wait_ge(HV["lru_exp"], 2 * j + n + 1)
                    lag(TS(hs, t2, 1.0, None, ALU.add))
                for xc, tr, ti, t2, hs in lru_bufs:
                    lag(TS(ti, ti, 0.5, 0.5, ALU.mult, ALU.add))
                for xc, tr, ti, t2, hs in lru_bufs:
                    lag(V.reciprocal(hs, hs))
                for xc, tr, ti, t2, hs in lru_bufs:
                    lag(TT(ti, ti, xc, ALU.mult))
                for xc, tr, ti, t2, hs in lru_bufs:
                    STT(out=t2, in0=t2, scalar=2.0, in1=hs, op0=ALU.mult, op1=ALU.mult).then_inc(HV["q_ready"], 1)
                for n in range(2):
                    o = PAD + n * HALF
                    dve.wait_ge(HV["bonus_mm"], 2 * j + n + 1)
                    TT(kept[n][7], ps[:, 3 + 2 * n, :], pv[:, o:o + HALF], ALU.mult).then_inc(HV["bonus_out"], 1)
                for n, (xc, tr, ti, t2, hs) in enumerate(lru_bufs):
                    dve.wait_ge(HV["lru_mult"], 2 * j + n + 1)
                    lag(TT(ti, ti, t2, ALU.mult))
                last_done()
                for n, (xc, tr, ti, t2, hs) in enumerate(lru_bufs):
                    start = lru_bufs[0][4][:, HALF - 1:HALF] if n else 0.0
                    link(V.tensor_tensor_scan(hs, tr, ti, start, ALU.mult, ALU.add))
                V.tensor_copy(lru_last[:, j, 0:1], lru_bufs[1][4][:, HALF - 1:HALF])
                dve.wait_ge(win_out, 6 + 15 * j + 15)
                for n, (xc, tr, ti, t2, hs) in enumerate(lru_bufs):
                    y_ = yT[:, NJ + j, HALF * n:HALF * n + HALF]
                    last = TT(y_, hs, y_, ALU.mult)
                done(last, HV["prep_done"], j + 1)
                for hf in range(2):
                    it = 2 * j + hf
                    n1 = it + 1
                    AR0, AR1, bb, k2, Bh, Kh, eP, rkp = kept[hf]

                    def banks2(g, b_, w):
                        return ps[:, 4 * g + b_:4 * g + b_ + 2, 0:w]

                    def four(m):
                        return m.unsqueeze(1).to_broadcast([P, 4, P])

                    def v4(ap):
                        return ap.rearrange("p h a t -> p (h a) t")

                    def strict_b(gi):
                        q = grp[gi % 2]
                        dve.wait_ge(HV["gram_b"], gi + 1)
                        TT(q.dtg.rearrange("p h a w t -> p (h a) (w t)"),
                           banks2(gi % 2, 0, 512).rearrange("p b (a x) -> p (b a) x", a=2),
                           mask_dt.rearrange("p w t -> p (w t)").unsqueeze(1).to_broadcast([P, 4, 256]),
                           ALU.mult).then_inc(HV["dt_out"], 1)

                    def strict_k(gi):
                        q = grp[gi % 2]
                        dve.wait_ge(HV["gram_k"], gi + 1)
                        TT(q.ak.rearrange("p h a w t -> p (h a) (w t)"),
                           banks2(gi % 2, 2, 512).rearrange("p b (a x) -> p (b a) x", a=2),
                           mask_ak.rearrange("p w t -> p (w t)").unsqueeze(1).to_broadcast([P, 4, 256]),
                           ALU.mult).then_inc(HV["ak_out"], 1)
                        dve.wait_ge(HV["dt_out"], gi + 1)
                        TT(v4(q.p), q.dtg[:, :, :, 0, :].rearrange("p h a t -> p (h a) t"), four(ident),
                           ALU.add).then_inc(HV["p1_out"], 1)

                    if hf == 0:
                        strict_b(2 * it)
                        strict_b(2 * it + 1)
                        strict_k(2 * it)
                    else:
                        strict_b(2 * it + 1)
                    strict_k(2 * it + 1)
                    for g in range(2):
                        q = grp[g]
                        gi = 2 * it + g + 1
                        dve.wait_ge(HV["gram_l"], gi)
                        src = banks2(g, 0, 256).rearrange("p b (a t) -> p b a t", a=2)
                        m4 = [m.unsqueeze(1).unsqueeze(1).to_broadcast([P, 2, 2, P]) for m in (mask_d, mask_e)]
                        TT(q.d, src, m4[0], ALU.mult)
                        TT(q.e, src, m4[1], ALU.mult).then_inc(HV["de_out"], 1)
                    for mm_, out_, b_ in (("p2_mm", "p2_out", 2), ("p3_mm", "p3_out", 2), ("p4_mm", "nt_out", 2)):
                        for g in range(2):
                            gi = 2 * it + g + 1
                            dve.wait_ge(HV[mm_], gi)
                            TT(grp[g].p_flat, grp[g].p_flat, grp[g].bank(b_), ALU.add).then_inc(HV[out_], 1)
                    for g in range(2):
                        gi = 2 * it + g + 1
                        dve.wait_ge(HV["f_mm"], gi)
                        V.tensor_copy(grp[g].z_flat, grp[g].bank(2)).then_inc(HV["z0_out"], 1)
                    for mm_, out_, b_ in (("z1_mm", "z1_out", 2), ("z2_mm", "z2_out", 1)):
                        for g in range(2):
                            gi = 2 * it + g + 1
                            dve.wait_ge(HV[mm_], gi)
                            TT(grp[g].z_flat, grp[g].z_flat, grp[g].bank(b_), ALU.add).then_inc(HV[out_], 1)
                    def transitions(g):
                        q = grp[g]
                        gi = 2 * it + g + 1
                        dve.wait_ge(HV["rt_mm"], gi)
                        TT(q.rh, AR1[:, q.c0:q.c0 + GRP], q.bank(0)[:, 0:GRP], ALU.add).then_inc(HV["rh_out"], 1)
                        link(TT(q.tt, banks2(g, 2, 256).rearrange("p c (a t) -> p c a t", a=2),
                                blk_ones.unsqueeze(1).unsqueeze(1).to_broadcast([P, 2, 2, P]), ALU.mult))
                        for n in range(4):
                            t_ = q.tt[:, n % 2, n // 2, :]
                            end = q.c0 + CHUNK * n + CHUNK - 1
                            last = STT(out=t_, in0=ident, scalar=eP[:, end:end + 1], in1=t_, op0=ALU.mult, op1=ALU.add)
                        last.then_inc(HV["tt_out"], 1)

                    def next_state(g, n):
                        dve.wait_ge(state_mm, 4 * (2 * it + g) + n + 1)
                        TT(S[:, (n + 1) % 2, :], grp[g].bank(2 + n % 2)[:, 256:384], blk_ones,
                           ALU.mult).then_inc(state_out, 1)

                    transitions(0)
                    next_state(0, 0)
                    transitions(1)
                    for n in range(1, 4):
                        next_state(0, n)
                    next_state(1, 0)
                    if hf == 0:
                        strict_b(2 * it + 2)
                    next_state(1, 1)
                    next_state(1, 2)
                    if hf == 0:
                        strict_k(2 * it + 2)
                    next_state(1, 3)
                    dve.wait_ge(HV["mean_mm"], n1)
                    TT(Y, Y, ps[:, 4, :], ALU.subtract).then_inc(HV["centred"], 1)
                    if hf:
                        dve.wait_ge(state_out, 8 * (it + 1))
                        lag(V.tensor_copy(sfin[:, j, :], S[:, 0, :]))
                    dve.wait_ge(HV["gsd_ready"], n1)
                    parts = [slice(GRP * g, GRP * g + GRP) for g in range(2)]
                    for c_ in parts:
                        lag(V.reciprocal(eP[:, c_], eP[:, c_]))
                    for c_ in parts:
                        lag(TT(Y[:, c_], Y[:, c_], eP[:, c_], ALU.mult))
                    for c_ in parts:
                        lag(TS(Y[:, c_], Y[:, c_], pcol(LNX_G, j), pcol(LNX_B, j), ALU.mult, ALU.add))
                    for c_ in parts:
                        lag(TT(Y[:, c_], Y[:, c_], rkp[:, c_], ALU.add))
                    last_done()
                    done(TT(yT[:, j, HALF * hf:HALF * hf + HALF], Y, ps[:, 6, :], ALU.mult), HV["half_done"], n1)

            def pb(q):
                return par[:, q, :].unsqueeze(2).to_broadcast([P, NJ, DEC])

            dve.wait_ge(row_mm, 1)
            V.tensor_copy(mod_rows_sb, ps[0:9 * KC, 0, :]).then_inc(row_out, 1)
            dve.wait_ge(ld_samp, 16 * 6)
            link(TT(s_xc, s_conv[:, :, 0, :], pb(CW0), ALU.mult))
            for m in (1, 2, 3):
                link(TT(s_kk, s_conv[:, :, m, :] if m < 3 else pxs, pb(CW0 + m), ALU.mult))
                link(TT(s_xc, s_xc, s_kk, ALU.add))
            done(TT(s_xc, s_xc, pb(C_BIAS), ALU.add), *SAMP["s_conv"])
            k_, r_, v_ = psm[:, 0], psm[:, 1], psm[:, 2]
            link(TT(s_kk, k_, pb(K_K), ALU.mult))
            done(TT(s_t, s_kk, s_kk, ALU.mult), *SAMP["s_sq"])
            dve.wait_ge(*SAMP["s_wa"])
            link(TS(s_lam, s_lam, -0.5 * DECAY, -0.5 * DECAY, ALU.mult, ALU.add))
            done(TS(s_a, s_a, 0.5, 0.5, ALU.mult, ALU.add), *SAMP["s_lam"])
            dve.wait_ge(*SAMP["s_nrm"])
            link(TS(s_t, s_t, 1e-12, None, ALU.max))
            link(V.reciprocal(s_t, s_t))
            link(TT(s_kk, s_kk, s_t, ALU.mult))
            link(TT(s_t, s_a, pb(K_A), ALU.mult))
            link(TT(s_t, s_t, der[:, D_OKA, :].unsqueeze(2).to_broadcast([P, NJ, DEC]), ALU.add))
            link(TT(s_vecs[:, 2], k_, s_t, ALU.mult))
            link(TT(s_t1, r_, pb(R_K), ALU.mult))
            done(TT(s_t1, s_t1, s_vecs[:, 2], ALU.mult), *SAMP["s_bon"])
            V.tensor_copy(s_vecs[:, 0], r_)
            V.tensor_copy(s_vecs[:, 3], v_)
            TS(s_vecs[:, 4], s_kk, -1.0, None, ALU.mult)
            dve.wait_ge(*SAMP["s_w"])
            TT(s_vecs[:, 5], s_kk, s_a, ALU.mult).then_inc(SAMP["s_vec"][0], 1)
            dve.wait_ge(*SAMP["s_lexp"])
            link(TS(s_ti, s_ti, 0.5, 0.5, ALU.mult, ALU.add))
            link(TT(s_ti, s_ti, s_xc, ALU.mult))
            link(TS(s_gl, s_t2, 1.0, None, ALU.add))
            link(V.reciprocal(s_gl, s_gl))
            done(STT(out=s_t2, in0=s_t2, scalar=2.0, in1=s_gl, op0=ALU.mult, op1=ALU.mult), *SAMP["s_q"])
            dve.wait_ge(*SAMP["s_mult"])
            link(TT(s_ti, s_ti, s_t2, ALU.mult))
            link(TT(s_hs, s_tr, s_lru0, ALU.mult))
            link(TT(s_hs, s_hs, s_ti, ALU.add))
            link(V.tensor_copy(lru_last[:, :, 1:9], s_hs))
            dve.wait_ge(*SAMP["s_gelu"])
            link(TT(yT[:, NJ:2 * NJ, SEQ:NTOK], s_hs, s_mu, ALU.mult))
            dve.wait_ge(*SAMP["s_turn"])
            link(TT(s_bon, ps[:, 5, 0:SN].rearrange("p (j b) -> p j b", j=NJ), v_, ALU.mult))
            link(V.tensor_copy(s_qt[:, 0:512], ps[0:32, 6, :]))
            done(V.tensor_copy(s_qt[:, 512:768], ps[0:32, 7, 0:256]), *SAMP["s_vrow"])

            def krow(n):
                return s_row[:, n, :].unsqueeze(1).to_broadcast([P, 32, HEAD])

            def vrow(x_):
                return x_.unsqueeze(2).to_broadcast([P, 32, HEAD])

            def sample_states():
                dve.wait_ge(HV["s_rows"], 16 * 7)
                link(TT(s_T, s_S, krow(3), ALU.mult))
                link(V.tensor_reduce(s_sa, s_T, AX_X, ALU.add))
                link(TT(s_S, s_S, krow(1), ALU.mult))
                link(TT(s_T, vrow(s_sa), krow(4), ALU.mult))
                link(TT(s_S, s_S, s_T, ALU.add))
                link(TT(s_T, vrow(s_vr), krow(2), ALU.mult))
                link(TT(s_S, s_S, s_T, ALU.add))
                link(TT(s_T, s_S, krow(0), ALU.mult))
                done(V.tensor_reduce(s_yr, s_T, AX_X, ALU.add), *SAMP["s_y"])

            def sample_rows():
                dve.wait_ge(*SAMP["s_yturn"])
                done(V.tensor_copy(s_y.rearrange("p j b -> p (j b)"), ps[:, 7, 0:SN]), *SAMP["s_yc"])

            def sample_centred():
                dve.wait_ge(*SAMP["s_mean"])
                done(TT(s_y, s_y, ps[:, 7, 0:SN].rearrange("p (j b) -> p j b", j=NJ), ALU.subtract), *SAMP["s_cent"])

            def sample_out():
                dve.wait_ge(*SAMP["s_gsd"])
                link(V.reciprocal(s_t1, s_t1))
                link(TT(s_y, s_y, s_t1, ALU.mult))
                link(TT(s_y, s_y, pb(LNX_G), ALU.mult))
                link(TT(s_y, s_y, pb(LNX_B), ALU.add))
                link(TT(s_y, s_y, s_bon, ALU.add))
                done(TT(yT[:, 0:NJ, SEQ:NTOK], s_y, s_g, ALU.mult), *SAMP["s_done"])

            dve.wait_ge(outs, 16 * 7)

            def norm(dst, src, rt, s_sd, n):
                dve.wait_ge(s_sd, n)
                link(V.reciprocal(rs[0:rt], sd[0:rt]))
                return TS(dst, src, mv[0:rt, 0:1], rs[0:rt], ALU.subtract, ALU.mult)

            dve.wait_ge(ld_late, 16 * 10)
            for i, (r0, rt) in enumerate(TILES):
                for at_, part in ((2, sample_states), (4, sample_rows), (5, sample_centred), (7, sample_out)):
                    if i == at_:
                        part()
                if i == 8:
                    dve.wait_ge(ld_late, 16 * 11)
                gb = (rowb if i < 8 else rows_s)[:, 0, :]
                dve.wait_ge(wo_mm, 2 * i + 2)
                z_ = x_ = x1[0:rt, i, :]
                done(TT(z_, ps[0:rt, 2 * (i % 2):2 * (i % 2) + 2, :].rearrange("p b x -> p (b x)"), gb[0:rt], ALU.mult),
                     wo_out, i + 1)
                dve.wait_ge(ld_x2[i % 2], 16 * (i // 2 + 1))
                link(STT(out=z_, in0=xr2[0:rt, i % 2, :], scalar=ALPHA, in1=z_, op0=ALU.mult, op1=ALU.add))
                moments(z_, rt, var_ready, 9 + 2 * i + 1)
                link(STT(out=x_, in0=z_, scalar=mv[0:rt, 0:1], in1=lnr[0:rt, 0, :], op0=ALU.subtract, op1=ALU.mult))
                dve.wait_ge(sd_ready, 9 + 2 * i + 1)
                link(V.reciprocal(rs[0:rt], sd[0:rt]))
                link(STT(out=x_, in0=x_, scalar=rs[0:rt], in1=lnr[0:rt, 1, :], op0=ALU.mult, op1=ALU.add))
                moments(x_, rt, var_ready, 9 + 2 * i + 2)
                if i >= 2:
                    dve.wait_ge(h2_turned, i - 1)
                    dve.wait_ge(h2_stored[i % 2], 16 * (i // 2))
                done(norm(n2[0:rt, i % 2, :], x_, rt, sd_ready, 9 + 2 * i + 2), n2_ready, i + 1)

            link(V.memset(lgt, 0.0))
            dve.wait_ge(router_mm, 9)
            lg_ps = ps[:, 6, 0:180].rearrange("p (i x) -> p i x", i=9)
            link(TT(lgt[:, 0:8, :], lg_ps[:, 0:8, :], brt.unsqueeze(1).to_broadcast([P, 8, 20]), ALU.add))
            link(TT(lgt[0:DEC, 8, :], lg_ps[0:DEC, 8, :], brt[0:DEC], ALU.add))

            def b4(x_):
                return x_.unsqueeze(2).to_broadcast([P, 9, 4])

            def first_of_max(o_, eq, left):
                link(TT(eq, eq, falling.unsqueeze(1).to_broadcast([P, 9, 4]), ALU.mult))
                link(V.tensor_reduce(left, eq, AX_X, ALU.max))
                link(TT(o_, eq, b4(left), ALU.is_equal))

            def by_group(x_):
                return x_.rearrange("p i (m e) -> p i m e", m=4)

            gl = lgt[:, :, 0:4]
            e_, oh, el, f1, f2, t4, c4, eq = rt_a
            gmax, gsum, em, ee, left, w1, w2, pg = rt_s
            link(V.tensor_reduce(gmax, gl, AX_X, ALU.max))
            done(TT(e_, gl, b4(gmax), ALU.subtract), lg_ready, 1)
            link(TT(eq, gl, b4(gmax), ALU.is_equal))
            first_of_max(oh, eq, left)
            picked = pick.rearrange("p (i m e) -> p i m e", i=9, m=4)
            link(TT(picked, by_group(lgt[:, :, 4:20]), oh.unsqueeze(3).to_broadcast([P, 9, 4, 4]), ALU.mult))
            link(V.tensor_reduce(el, picked.rearrange("p i m e -> p i e m"), AX_X, ALU.add))
            link(V.tensor_reduce(em, el, AX_X, ALU.max))
            link(TT(eq, el, b4(em), ALU.is_equal))
            first_of_max(f1, eq, left)
            link(TS(t4, f1, -1e30, None, ALU.mult))
            link(TT(el, el, t4, ALU.add))
            link(V.tensor_reduce(w1, el, AX_X, ALU.max))
            link(TT(eq, el, b4(w1), ALU.is_equal))
            first_of_max(f2, eq, left)
            done(TT(ee, w1, em, ALU.subtract), lg2_ready, 1)
            link(TT(f1, f1, b4(valid), ALU.mult))
            link(TT(f2, f2, b4(valid), ALU.mult))
            for e_a, f_a in ((e1, f1), (e2, f2)):
                link(TT(by_group(e_a), f_a.unsqueeze(2).to_broadcast([P, 9, 4, 4]),
                        oh.unsqueeze(3).to_broadcast([P, 9, 4, 4]), ALU.mult))
            done(TT(asg, e1, e2, ALU.add), assigned, 1)
            dve.wait_ge(ex_ready, 1)
            link(V.tensor_reduce(gsum, e_, AX_X, ALU.add))
            link(V.reciprocal(pg, gsum))
            dve.wait_ge(ex2_ready, 1)
            link(TS(w1, ee, 1.0, None, ALU.add))
            link(V.reciprocal(w1, w1))
            link(TT(w1, w1, pg, ALU.mult))
            link(TT(w2, w1, ee, ALU.mult))
            dve.wait_ge(rank_mm, 1)
            V.memset(carry[:, 0, :], 0.0)
            link(V.tensor_copy(carry[:, 1:10, :], ps[:, 1, NEXP:10 * NEXP].rearrange("p (i e) -> p i e", e=NEXP)))
            link(TT(rank, carry[:, 0:9, :], ps[:, 0, 0:9 * NEXP].rearrange("p (i e) -> p i e", i=9), ALU.add))
            full = asg.rearrange("p i e -> p (i e)").rearrange("p (e m) -> p e m", e=NEXP)
            link(TT(full, carry[:, 9, :].unsqueeze(2).to_broadcast([P, NEXP, 9]),
                    iota_t[:, 0:9].unsqueeze(1).to_broadcast([P, NEXP, 9]), ALU.is_gt))
            link(V.tensor_reduce(ntile, full, AX_X, ALU.add))
            link(V.tensor_tensor_scan(tend, ones[:, 0:NEXP], ntile, 0.0, ALU.mult, ALU.add))
            link(TT(tbase, tend, ntile, ALU.subtract))
            link(TS(tbase, tbase, float(P), None, ALU.mult))
            link(TT(rank, rank, tbase.unsqueeze(1).to_broadcast([P, 9, NEXP]), ALU.add))
            both = ((0, e1, pos1, pp1, ge, psn), (1, e2, pos2, pp2, ge2, psn2))
            for a, e_a, pos, pp, ge_, n_ in both:
                lag(TT(e_a, e_a, rank, ALU.mult))
            for a, e_a, pos, pp, ge_, n_ in both:
                lag(V.tensor_reduce(pos, e_a, AX_X, ALU.add))
            for a, e_a, pos, pp, ge_, n_ in both:
                lag(TT(ge_, pos.unsqueeze(2).to_broadcast([P, 9, STEPS + 1]),
                       iota_t.unsqueeze(1).to_broadcast([P, 9, STEPS + 1]), ALU.is_ge))
            for a, e_a, pos, pp, ge_, n_ in both:
                lag(V.tensor_reduce(n_, ge_, AX_X, ALU.add))
            for a, e_a, pos, pp, ge_, n_ in both:
                lag(TT(wt[:, a], ge_[:, :, 0:STEPS], ge_[:, :, 1:STEPS + 1], ALU.subtract))
            for a, e_a, pos, pp, ge_, n_ in both:
                lag(TS(n_, n_, float(-P), float(P), ALU.mult, ALU.add))
            for a, e_a, pos, pp, ge_, n_ in both:
                lag(TT(wt[:, a], wt[:, a], tok_id.unsqueeze(2).to_broadcast([P, 9, STEPS]), ALU.mult))
            for a, e_a, pos, pp, ge_, n_ in both:
                lag(TT(pp, pos, n_, ALU.add))
            for a, e_a, pos, pp, ge_, n_ in both:
                lag(V.tensor_copy(posu[:, a, :], pos))
            for b in range(2):
                dve.wait_ge(h2_stored[b], 16 * (5 - b))
            link(TT(tcmp, iota_s.unsqueeze(2).to_broadcast([P, STEPS, NEXP]),
                    tend.unsqueeze(1).to_broadcast([P, STEPS, NEXP]), ALU.is_ge))
            link(V.tensor_reduce(texp_f, tcmp, AX_X, ALU.add))
            link(TS(texp_f, texp_f, float(NEXP - 1), None, ALU.min))
            link(V.tensor_copy(texp, texp_f))
            for n in range(18):
                if n >= 9:
                    dve.wait_ge(hot_used, n - 8)
                pp = (pp1, pp2)[n // 9]
                TS(uu[:, n % 9, :], iota_p, pp[:, n % 9:n % 9 + 1], None, ALU.is_equal).then_inc(hot_ready, 1)
            dve.wait_ge(hot_used, 18)
            done(V.tensor_copy(perm, ps[:, 2, 0:STEPS]), route_ready, 1)

            def dve_hid(s, b):
                dve.wait_ge(silu_out, s + 1)
                V.tensor_tensor(hid[:, b, :], sil, ps[:, 2 + b, DEXP:2 * DEXP], ALU.mult).then_inc(hid_out, 1)

            def dve_ys(s, i, b, first):
                dve.wait_ge(dn_mm, s + 1)
                if not first:
                    dve.wait_ge(slot_stored[b], 16 * i)
                V.tensor_copy(ys[:, b, :], ps[:, 6:8, :].rearrange("p b x -> p (b x)")).then_inc(ys_out, 1)

            dve_hid(0, 0)
            dve_hid(1, 1)
            dve_ys(0, 0, 0, True)
            dve_hid(2, 0)
            dve_ys(1, 0, 1, True)
            with dve.Fori(1, STEPS // 2 - 1) as i:
                dve_hid(2 * i + 1, 1)
                dve_ys(2 * i, i, 0, False)
                dve_hid(2 * i + 2, 0)
                dve_ys(2 * i + 1, i, 1, False)
            i = STEPS // 2 - 1
            dve_hid(2 * i + 1, 1)
            dve_ys(2 * i, i, 0, False)
            dve_ys(2 * i + 1, i, 1, False)

            def scales(i):
                rt = TILES[i][1]
                dve.wait_ge(sd_ready, 27 + i + 1)
                if i >= 2:
                    dve.wait_ge(y_normed, i - 1)
                V.reciprocal(y_rs[0:rt, i % 2:i % 2 + 1], sd[0:rt]).then_inc(y_scale, 1)

            for i, (r0, rt) in enumerate(TILES):
                gb = (rowb if i < 8 else rows_s)[0:rt, 3, :]
                z_ = fz[i][0:rt]
                parts = (slice(0, 512), slice(512, 1024))
                dve.wait_ge(yg_used, i + 1)
                for n, c_ in enumerate(parts):
                    lag(TT(z_[:, c_], ps[0:rt, 2 * (i % 4) + n, :], gb[:, c_], ALU.mult))
                for c_ in parts:
                    lag(STT(out=z_[:, c_], in0=x1[0:rt, i, c_], scalar=ALPHA, in1=z_[:, c_], op0=ALU.mult, op1=ALU.add))
                if i:
                    scales(i - 1)
                V.bn_stats(st[0:rt, 0, :], z_[:, parts[0]])
                last_done()
                link(V.bn_stats(st[0:rt, 1, :], z_[:, parts[1]]))
                done(V.bn_aggr(mv[0:rt], st[0:rt]), var_ready, 27 + i + 1)
                chain_v.on(STT(out=z_, in0=z_, scalar=mv[0:rt, 0:1], in1=lnr[0:rt, 2, :], op0=ALU.subtract, op1=ALU.mult))
            scales(8)


def kernel(x_prompt, x_sample, c_prompt, c_sample, state_wkv, state_shift, state_conv, state_lru,
           w_ada, b_ada, w_in, mu_shift, w0, w_decay_up, a0, w_a_up, w_g_up, k_k, k_a, r_k,
           lnx_gain, lnx_bias, conv_w, conv_b, w_rgate, b_rgate, w_igate, b_igate, lru_lambda,
           w_out, ln1_gain, ln1_bias, w_router_group, b_router_group, w_router_expert,
           b_router_expert, w_exp_gate, w_exp_up, w_exp_down, ln2_gain, ln2_bias):
    import concourse.bacc as _bacc
    from concourse.bass_utils import run_bass_kernel_spmd as _run

    def tiles(v):
        return np.asarray(v).reshape(-1, P).T

    def rows(w):
        w = np.asarray(w)
        return w.reshape(KC, P, -1).transpose(1, 0, 2)

    x = np.concatenate([np.asarray(x_prompt)[0], np.asarray(x_sample)[:, 0]], 0)
    c = np.concatenate([np.asarray(c_prompt), np.asarray(c_sample)], 0)
    wi = np.asarray(w_in)[0]
    ca = 512
    sh = 3 * ca + 160
    at = {"k": ca, "r": 0, "v": 2 * ca, "rec": sh + ca, "gate": sh}
    mu = np.asarray(mu_shift)[0]
    st = np.asarray(state_wkv)[0].reshape(DEC, NJ, 2, HEAD, HEAD)
    d = {
        "x_all": x,
        "c_t": c.reshape(9, KC, P).transpose(2, 1, 0),
        "shift_t": np.asarray(state_shift)[0].reshape(DEC, KC, P).transpose(2, 1, 0),
        "wkv0": st.transpose(1, 0, 2, 3, 4).reshape(P, 2048),
        "conv0": np.asarray(state_conv)[0].reshape(DEC, 3, NJ, P).transpose(3, 2, 1, 0),
        "lru0": np.asarray(state_lru)[0].reshape(DEC, NJ, P).transpose(2, 1, 0),
        "state_conv": np.asarray(state_conv)[0],
        "w_ada": np.asarray(w_ada)[0].reshape(KC, P, 24, 256).transpose(2, 1, 0, 3).reshape(24, P, 2048),
        "b_ada": tiles(b_ada[0]),
        "w_in": np.stack([rows(wi[:, at[q] + P * j:at[q] + P * j + P]).reshape(P, KC * P)
                          for j in range(NJ) for q in ("k", "r", "rec", "v", "gate")]),
        "w_lo": rows(wi[:, 3 * ca:sh]).reshape(P, KC * 160),
        "prm": np.stack([tiles(v) for v in (
            mu[0:ca], mu[ca:2 * ca], mu[2 * ca:3 * ca], w0[0], a0[0], k_k[0], k_a[0], np.asarray(r_k)[0].reshape(-1),
            lnx_gain[0], lnx_bias[0], conv_w[0][0], conv_w[0][1], conv_w[0][2], conv_w[0][3], conv_b[0],
            b_rgate[0], b_igate[0], lru_lambda[0])], 1),
        "mu_lo": mu[3 * ca:].reshape(160, 1),
        "w_wa_up": np.concatenate([np.asarray(w_decay_up)[0], np.asarray(w_a_up)[0]], 0),
        "w_g_up": np.asarray(w_g_up)[0],
        "w_rg": np.asarray(w_rgate)[0].reshape(NJ, P, HEAD),
        "w_ig": np.asarray(w_igate)[0].reshape(NJ, P, HEAD),
        "w_out": np.asarray(w_out)[0].reshape(KC, P, D_MODEL),
        "ln_rows": np.stack([np.asarray(v)[0] for v in (ln1_gain, ln1_bias, ln2_gain, ln2_bias)]),
        "w_rt": rows(np.concatenate([np.asarray(w_router_group)[0], np.asarray(w_router_expert)[0]], 1)),
        "b_rt": np.concatenate([np.asarray(b_router_group)[0], np.asarray(b_router_expert)[0]]).reshape(1, 20),
        "w_gu": np.stack([np.asarray(w_exp_gate)[0], np.asarray(w_exp_up)[0]], 1)
                  .reshape(NEXP, 2, KC, P, DEXP).transpose(0, 3, 2, 1, 4).reshape(NEXP, P, 4096),
        "w_dn": np.asarray(w_exp_down)[0].reshape(NEXP, 2, P, D_MODEL).transpose(0, 2, 1, 3).reshape(NEXP, P, 2048),
    }
    outs = {"y_all": (NTOK, D_MODEL), "wkvp_o": (NJ, P, P), "wkvs_o": (P, 2048), "shift_o": (P, KC, 9),
            "conv_o": (NJ, P, 11), "convs_o": (DEC, 2, 512), "lru_o": (P, NJ, 9)}
    nc = _bacc.Bacc("TRN2", target_bir_lowering=False, num_devices=1)
    arrays, args = {}, {}
    for name, a in d.items():
        a = np.ascontiguousarray(a)
        arrays[f"in_{name}"] = a
        args[name] = nc.dram_tensor(f"in_{name}", a.shape, mybir.dt.from_np(a.dtype), kind="ExternalInput").ap()
    for name, shape in outs.items():
        args[name] = nc.dram_tensor(f"out_{name}", shape, F32, kind="ExternalOutput").ap()
    build(nc, **args)
    r = _run(nc, [arrays], core_ids=[0]).results[0]
    o = {name: r[f"out_{name}"] for name in outs}
    y = o["y_all"]
    sb_ = o["wkvp_o"].reshape(NJ, 2, HEAD, 2, HEAD)
    wkv_p = np.stack([sb_[:, q, :, q, :] for q in range(2)], 1).transpose(0, 1, 3, 2).reshape(1, 1, 8, HEAD, HEAD)
    wkv_s = o["wkvs_o"].reshape(NJ, DEC, 2, HEAD, HEAD).transpose(1, 0, 2, 3, 4).reshape(1, DEC, 8, HEAD, HEAD)
    shf = o["shift_o"].transpose(2, 1, 0).reshape(9, D_MODEL)
    cv = o["conv_o"].transpose(2, 0, 1).reshape(11, 512)
    conv_s = np.concatenate([o["convs_o"], cv[3:, None, :]], 1)
    lr = o["lru_o"].transpose(2, 1, 0).reshape(9, 512)
    cc = np.ascontiguousarray
    return (cc(y[None, :SEQ]), cc(y[SEQ:, None]), cc(wkv_p), cc(shf[None, 0:1]), cc(cv[None, None, 0:3]),
            cc(lr[None, 0:1]), cc(wkv_s), cc(shf[None, 1:]), cc(conv_s[None]), cc(lr[None, 1:]))
```
